# Optimizing a Trainium2 kernel written in Bass

```python
import math
import jax, jax.numpy as jnp
from jax import lax
import numpy as np

D_MODEL = 1024
BATCH = 1
SEQ = 512
DEPTH = 2

N_MEM = 256
D_FF = 2816
EPS = 1e-6
ROPE_THETA = 10000.0
GLA_HEADS = 4
GLA_DK = 64
GLA_DV = 128
GLA_RANK = 16
GLA_TAU = 16.0
GLA_CHUNK = 64
GLA_WIDTH = GLA_HEADS * GLA_DV
S5_GROUP = 16
S5_WIDTH = D_MODEL - GLA_WIDTH
S5_GROUPS = S5_WIDTH // S5_GROUP
S5_STATE = 64
S5_DT_MIN = 0.001
S5_DT_MAX = 0.1
ATT_HEADS = 8
ATT_KV_HEADS = 2
ATT_HEAD_DIM = D_MODEL // ATT_HEADS
IDX_HEADS = 8
IDX_DIM = 64
TOPK_MAX = 256
Q_BLOCK = 128
XA_HEADS = 4
XA_HEAD_DIM = D_MODEL // XA_HEADS

N_EVEN = (DEPTH + 1) // 2
N_ODD = DEPTH // 2
EV_SIZES = (GLA_HEADS * GLA_DK, GLA_HEADS * GLA_DK, GLA_WIDTH, GLA_WIDTH, GLA_RANK, S5_WIDTH)
OD_SIZES = (ATT_HEADS * ATT_HEAD_DIM, ATT_KV_HEADS * ATT_HEAD_DIM, ATT_KV_HEADS * ATT_HEAD_DIM,
            IDX_HEADS * IDX_DIM, IDX_DIM, IDX_HEADS)
EV_IN = sum(EV_SIZES)
OD_IN = sum(OD_SIZES)

kernel_name = "hybrid_gla_s5_dsa_macaron_memxattn"

def _splits(sizes):
    out, acc = [], 0
    for s in sizes[:-1]:
        acc += s
        out.append(acc)
    return out

def rmsnorm(x, g):
    xf = x.astype(jnp.float32)
    y = xf * lax.rsqrt(jnp.mean(xf * xf, axis=-1, keepdims=True) + EPS)
    return (y * g.astype(jnp.float32)).astype(x.dtype)

def rope_tables(positions, dim):
    inv = ROPE_THETA ** (-jnp.arange(0, dim, 2, dtype=jnp.float32) / dim)
    ang = positions.astype(jnp.float32)[..., None] * inv
    cos = jnp.cos(ang)
    sin = jnp.sin(ang)
    return jnp.concatenate([cos, cos], -1), jnp.concatenate([sin, sin], -1)

def apply_rope(x, cos, sin):
    xf = x.astype(jnp.float32)
    half = xf.shape[-1] // 2
    rot = jnp.concatenate([-xf[..., half:], xf[..., :half]], -1)
    return (xf * cos[:, :, None, :] + rot * sin[:, :, None, :]).astype(x.dtype)

def swiglu(h, w_gate, w_up, w_down):
    return (jax.nn.silu(h @ w_gate) * (h @ w_up)) @ w_down

def gla_mixer(q, k, v, r, a_low, w_a2, b_a, g_norm):
    f32 = jnp.float32
    Bsz, L, _ = q.shape
    C = GLA_CHUNK
    N = L // C
    log_a = jax.nn.log_sigmoid((a_low @ w_a2 + b_a).astype(f32)) / GLA_TAU

    def chunks(t, d):
        return t.reshape(Bsz, N, C, GLA_HEADS, d)

    qc = chunks(q.astype(f32), GLA_DK) * GLA_DK ** -0.5
    kc = chunks(k.astype(f32), GLA_DK)
    vc = chunks(v.astype(f32), GLA_DV)
    bc = jnp.cumsum(chunks(log_a, GLA_DK), axis=2)
    b_last = bc[:, :, -1]
    q_dec = qc * jnp.exp(bc)
    k_inv = kc * jnp.exp(-bc)
    k_end = kc * jnp.exp(b_last[:, :, None] - bc)
    causal = jnp.tril(jnp.ones((C, C), dtype=bool))
    scores = jnp.where(causal, jnp.einsum('bnihd,bnjhd->bnhij', q_dec, k_inv), 0.0)
    o_intra = jnp.einsum('bnhij,bnjhe->bnihe', scores, vc)
    dS = jnp.einsum('bnjhd,bnjhe->nbhde', k_end, vc)
    decay = jnp.exp(b_last).transpose(1, 0, 2, 3)

    def step(S, inp):
        dec, ds = inp
        return dec[..., None] * S + ds, S

    S0 = jnp.zeros((Bsz, GLA_HEADS, GLA_DK, GLA_DV), f32)
    _, S_prev = lax.scan(step, S0, (decay, dS))
    o_inter = jnp.einsum('bnihd,nbhde->bnihe', q_dec, S_prev)
    o = (o_intra + o_inter).reshape(Bsz, L, GLA_HEADS, GLA_DV)
    o = o * lax.rsqrt(jnp.mean(o * o, axis=-1, keepdims=True) + EPS) * g_norm.astype(f32)
    o = o.reshape(Bsz, L, GLA_WIDTH) * jax.nn.silu(r.astype(f32))
    return o.astype(q.dtype)

def s5_mixer(u, lam_re, lam_im, log_dt, B_re, B_im, C_re, C_im, D, w_glu, b_glu):
    f32 = jnp.float32
    Bsz, L, _ = u.shape
    uf = u.astype(f32).reshape(Bsz, L, S5_GROUPS, S5_GROUP)
    lr = jnp.minimum(lam_re.astype(f32), -1e-4)
    li = lam_im.astype(f32)
    dt = jnp.exp(log_dt.astype(f32))[:, None]
    mag = jnp.exp(lr * dt)
    ab_re = mag * jnp.cos(li * dt)
    ab_im = mag * jnp.sin(li * dt)
    den = lr * lr + li * li
    nr = ab_re - 1.0
    f_re = (nr * lr + ab_im * li) / den
    f_im = (ab_im * lr - nr * li) / den
    Br = B_re.astype(f32)
    Bi = B_im.astype(f32)
    bb_re = f_re[..., None] * Br - f_im[..., None] * Bi
    bb_im = f_re[..., None] * Bi + f_im[..., None] * Br
    bu_re = jnp.einsum('gpc,blgc->blgp', bb_re, uf)
    bu_im = jnp.einsum('gpc,blgc->blgp', bb_im, uf)
    a_re = jnp.broadcast_to(ab_re, bu_re.shape)
    a_im = jnp.broadcast_to(ab_im, bu_im.shape)

    def combine(e1, e2):
        a1r, a1i, b1r, b1i = e1
        a2r, a2i, b2r, b2i = e2
        return (a1r * a2r - a1i * a2i,
                a1r * a2i + a1i * a2r,
                a2r * b1r - a2i * b1i + b2r,
                a2r * b1i + a2i * b1r + b2i)

    _, _, xr, xi = lax.associative_scan(combine, (a_re, a_im, bu_re, bu_im), axis=1)
    y = (jnp.einsum('gcp,blgp->blgc', C_re.astype(f32), xr)
         - jnp.einsum('gcp,blgp->blgc', C_im.astype(f32), xi)
         + D.astype(f32) * uf)
    y = jax.nn.gelu(y.reshape(Bsz, L, S5_WIDTH))
    y = y * jax.nn.sigmoid(y @ w_glu.astype(f32) + b_glu.astype(f32))
    return y.astype(u.dtype)

def dsa_mixer(hn, w_in, w_out, cos_a, sin_a, cos_i, sin_i):
    f32 = jnp.float32
    Bsz, L, _ = hn.shape
    q, k, v, qi, ki, wi = jnp.split(hn @ w_in, _splits(OD_SIZES), axis=-1)
    q = apply_rope(q.reshape(Bsz, L, ATT_HEADS, ATT_HEAD_DIM), cos_a, sin_a) * ATT_HEAD_DIM ** -0.5
    k = apply_rope(k.reshape(Bsz, L, ATT_KV_HEADS, ATT_HEAD_DIM), cos_a, sin_a)
    v = v.reshape(Bsz, L, ATT_KV_HEADS, ATT_HEAD_DIM)
    qi = apply_rope(qi.reshape(Bsz, L, IDX_HEADS, IDX_DIM), cos_i, sin_i)
    ki = apply_rope(ki.reshape(Bsz, L, 1, IDX_DIM), cos_i, sin_i)[:, :, 0]
    wi = wi * (IDX_HEADS ** -0.5 * IDX_DIM ** -0.5)
    topk = min(TOPK_MAX, L // 4)
    nb = L // Q_BLOCK
    group = ATT_HEADS // ATT_KV_HEADS

    def to_blocks(t):
        return t.reshape(Bsz, nb, Q_BLOCK, *t.shape[2:]).swapaxes(0, 1)

    qpos = jnp.arange(L, dtype=jnp.int32).reshape(nb, Q_BLOCK)
    kpos = jnp.arange(L, dtype=jnp.int32)
    bidx = jnp.arange(Bsz)[:, None, None]

    def block(args):
        qb, qib, wib, tq = args
        logits = jnp.einsum('bqhd,bsd->bqhs', qib, ki)
        score = jnp.einsum('bqhs,bqh->bqs', jax.nn.relu(logits).astype(f32), wib.astype(f32))
        score = jnp.where(kpos[None, None, :] <= tq[None, :, None], score, -jnp.inf)
        _, idx = lax.top_k(score, topk)
        valid = idx <= tq[None, :, None]
        k_sel = k[bidx, idx]
        v_sel = v[bidx, idx]
        qg = qb.reshape(Bsz, Q_BLOCK, ATT_KV_HEADS, group, ATT_HEAD_DIM)
        s = jnp.einsum('bqkgd,bqnkd->bqkgn', qg, k_sel).astype(f32)
        s = jnp.where(valid[:, :, None, None, :], s, -jnp.inf)
        p = jax.nn.softmax(s, axis=-1).astype(v.dtype)
        o = jnp.einsum('bqkgn,bqnkd->bqkgd', p, v_sel)
        return o.reshape(Bsz, Q_BLOCK, ATT_HEADS * ATT_HEAD_DIM)

    out = lax.map(block, (to_blocks(q), to_blocks(qi), to_blocks(wi), qpos))
    out = out.swapaxes(0, 1).reshape(Bsz, L, ATT_HEADS * ATT_HEAD_DIM)
    return out @ w_out

def cross_attn(hn, mem_n, wq, wk, wv, wo):
    Bsz, L, _ = hn.shape
    M = mem_n.shape[1]
    q = (hn @ wq).reshape(Bsz, L, XA_HEADS, XA_HEAD_DIM) * XA_HEAD_DIM ** -0.5
    k = (mem_n @ wk).reshape(Bsz, M, XA_HEADS, XA_HEAD_DIM)
    v = (mem_n @ wv).reshape(Bsz, M, XA_HEADS, XA_HEAD_DIM)
    s = jnp.einsum('bqhd,bmhd->bhqm', q, k).astype(jnp.float32)
    p = jax.nn.softmax(s, axis=-1).astype(hn.dtype)
    o = jnp.einsum('bhqm,bmhd->bqhd', p, v).reshape(Bsz, L, XA_HEADS * XA_HEAD_DIM)
    return o @ wo

def setup_inputs(seed: int = 0) -> dict:
    key = jax.random.key(seed)
    ks = iter(jax.random.split(key, 48))
    f32 = jnp.float32

    def w(shape, fan_in):
        return jax.random.normal(next(ks), shape, f32) * fan_in ** -0.5

    def gain(shape):
        return 1.0 + 0.02 * jax.random.normal(next(ks), shape, f32)

    def small(shape, s=0.01):
        return s * jax.random.normal(next(ks), shape, f32)

    x = jax.random.normal(next(ks), (BATCH, SEQ, D_MODEL), f32)
    mem = jax.random.normal(next(ks), (BATCH, N_MEM, D_MODEL), f32)
    offset = jax.random.randint(next(ks), (BATCH, 1), 0, 1024, dtype=jnp.int32)
    positions = offset + jnp.arange(SEQ, dtype=jnp.int32)[None, :]
    n_idx = jnp.arange(S5_STATE, dtype=f32)
    lam_re = -0.5 + small((N_EVEN, S5_GROUPS, S5_STATE))
    lam_im = math.pi * n_idx + small((N_EVEN, S5_GROUPS, S5_STATE))
    log_dt = jax.random.uniform(next(ks), (N_EVEN, S5_GROUPS), f32,
                                math.log(S5_DT_MIN), math.log(S5_DT_MAX))
    return {
        "x": x,
        "mem": mem,
        "positions": positions,
        "ffn1_norm": gain((DEPTH, D_MODEL)),
        "ffn1_w_gate": w((DEPTH, D_MODEL, D_FF), D_MODEL),
        "ffn1_w_up": w((DEPTH, D_MODEL, D_FF), D_MODEL),
        "ffn1_w_down": w((DEPTH, D_FF, D_MODEL), D_FF),
        "mix_norm": gain((DEPTH, D_MODEL)),
        "ev_w_in": w((N_EVEN, D_MODEL, EV_IN), D_MODEL),
        "ev_w_out": w((N_EVEN, GLA_WIDTH + S5_WIDTH, D_MODEL), GLA_WIDTH + S5_WIDTH),
        "gla_w_alpha": w((N_EVEN, GLA_RANK, GLA_HEADS * GLA_DK), GLA_RANK),
        "gla_b_alpha": small((N_EVEN, GLA_HEADS * GLA_DK), 0.1),
        "gla_norm": gain((N_EVEN, GLA_DV)),
        "s5_lambda_re": lam_re,
        "s5_lambda_im": lam_im,
        "s5_log_dt": log_dt,
        "s5_B_re": w((N_EVEN, S5_GROUPS, S5_STATE, S5_GROUP), 2 * S5_GROUP),
        "s5_B_im": w((N_EVEN, S5_GROUPS, S5_STATE, S5_GROUP), 2 * S5_GROUP),
        "s5_C_re": 0.5 * jax.random.normal(next(ks), (N_EVEN, S5_GROUPS, S5_GROUP, S5_STATE), f32),
        "s5_C_im": 0.5 * jax.random.normal(next(ks), (N_EVEN, S5_GROUPS, S5_GROUP, S5_STATE), f32),
        "s5_D": jax.random.normal(next(ks), (N_EVEN, S5_GROUPS, S5_GROUP), f32),
        "s5_w_glu": w((N_EVEN, S5_WIDTH, S5_WIDTH), S5_WIDTH),
        "s5_b_glu": small((N_EVEN, S5_WIDTH)),
        "od_w_in": w((N_ODD, D_MODEL, OD_IN), D_MODEL),
        "od_w_out": w((N_ODD, ATT_HEADS * ATT_HEAD_DIM, D_MODEL), ATT_HEADS * ATT_HEAD_DIM),
        "xa_norm": gain((DEPTH, D_MODEL)),
        "mem_norm": gain((D_MODEL,)),
        "xa_wq": w((DEPTH, D_MODEL, D_MODEL), D_MODEL),
        "xa_wk": w((DEPTH, D_MODEL, D_MODEL), D_MODEL),
        "xa_wv": w((DEPTH, D_MODEL, D_MODEL), D_MODEL),
        "xa_wo": w((DEPTH, D_MODEL, D_MODEL), D_MODEL),
        "ffn2_norm": gain((DEPTH, D_MODEL)),
        "ffn2_w_gate": w((DEPTH, D_MODEL, D_FF), D_MODEL),
        "ffn2_w_up": w((DEPTH, D_MODEL, D_FF), D_MODEL),
        "ffn2_w_down": w((DEPTH, D_FF, D_MODEL), D_FF),
        "final_norm": gain((D_MODEL,)),
    }

def reference(x, mem, positions, ffn1_norm, ffn1_w_gate, ffn1_w_up, ffn1_w_down, mix_norm,
              ev_w_in, ev_w_out, gla_w_alpha, gla_b_alpha, gla_norm, s5_lambda_re, s5_lambda_im,
              s5_log_dt, s5_B_re, s5_B_im, s5_C_re, s5_C_im, s5_D, s5_w_glu, s5_b_glu,
              od_w_in, od_w_out, xa_norm, mem_norm, xa_wq, xa_wk, xa_wv, xa_wo,
              ffn2_norm, ffn2_w_gate, ffn2_w_up, ffn2_w_down, final_norm):
    cos_a, sin_a = rope_tables(positions, ATT_HEAD_DIM)
    cos_i, sin_i = rope_tables(positions, IDX_DIM)
    mem_n = rmsnorm(mem, mem_norm)
    h = x
    for layer in range(DEPTH):
        h = h + 0.5 * swiglu(rmsnorm(h, ffn1_norm[layer]),
                             ffn1_w_gate[layer], ffn1_w_up[layer], ffn1_w_down[layer])
        hn = rmsnorm(h, mix_norm[layer])
        if layer % 2 == 0:
            e = layer // 2
            q, k, v, r, a_low, u = jnp.split(hn @ ev_w_in[e], _splits(EV_SIZES), axis=-1)
            o_gla = gla_mixer(q, k, v, r, a_low, gla_w_alpha[e], gla_b_alpha[e], gla_norm[e])
            o_s5 = s5_mixer(u, s5_lambda_re[e], s5_lambda_im[e], s5_log_dt[e], s5_B_re[e],
                            s5_B_im[e], s5_C_re[e], s5_C_im[e], s5_D[e], s5_w_glu[e], s5_b_glu[e])
            mix = jnp.concatenate([o_gla, o_s5], axis=-1) @ ev_w_out[e]
        else:
            o = layer // 2
            mix = dsa_mixer(hn, od_w_in[o], od_w_out[o], cos_a, sin_a, cos_i, sin_i)
        h = h + mix
        h = h + cross_attn(rmsnorm(h, xa_norm[layer]), mem_n,
                           xa_wq[layer], xa_wk[layer], xa_wv[layer], xa_wo[layer])
        h = h + 0.5 * swiglu(rmsnorm(h, ffn2_norm[layer]),
                             ffn2_w_gate[layer], ffn2_w_up[layer], ffn2_w_down[layer])
    return rmsnorm(h, final_norm)


_drawn_inputs = setup_inputs


def setup_inputs(seed=0):
    import zlib

    import numpy as np

    out = dict(_drawn_inputs(seed))
    spreads = {}
    factors = {'ffn1_norm': 3.173,
     'gla_norm': 4.651,
     's5_lambda_re': 8.0,
     's5_b_glu': 8.0,
     'xa_norm': 8.0,
     'mem_norm': 7.716,
     'ffn2_norm': 4.174,
     'final_norm': 2.946}
    for name, (base, spread) in spreads.items():
        noise = np.random.default_rng([zlib.crc32(name.encode()), seed]).standard_normal(out[name].shape)
        drawn = base * np.exp(spread * noise) if base else spread * noise
        out[name] = __import__('jax').numpy.asarray(drawn.astype(out[name].dtype))
    for name, factor in factors.items():
        out[name] = (out[name] * factor).astype(out[name].dtype)
    return out
```

```python
from contextlib import ExitStack

import numpy as np

import concourse.bass as bass
from concourse import mybir

F32 = mybir.dt.float32
F32R = mybir.dt.float32r
I32 = mybir.dt.int32
ALU = mybir.AluOpType
ACT = mybir.ActivationFunctionType
AX = mybir.AxisListType

P = 128
T = 512
D = 1024
KC = D // P
MEM = 256
FF = 2816
FC = FF // P
EPS = 1e-6
BLK = 1024
MAGIC = 12582912.0
TWO_PI_BELOW = 6.2831845
PI_BELOW = 3.1415925
TWO_PI_1, TWO_PI_2, TWO_PI_3 = 6.28125, 0.0019350051879882812, 3.0199159819e-07

GLA_HEADS, GLA_DK, GLA_DV, GLA_CHUNK, GLA_TAU = 4, 64, 128, 64, 16.0
NCH = T // GLA_CHUNK
S5_TILES = 16
QB = T // P
TOPK = 128
IDX_HEADS, IDX_DIM = 8, 64
ATT_HEADS, ATT_DIM = 8, 128
XA_HEADS, XA_DIM = 4, 256
MASKED = -1.0e30
TAKEN = -3.0e38

FFN_BLOCKS = 3 * FC
FFN_AT = [0, 125, 191, 315]
EV_AT, EV_TILES = 66, 13
EV_V_AT = 79
KV_AT = [83, 275]
GLU_AT = 99
OUT_AT = [101, 117, 291, 307]
XQ_AT = [109, 299]
OD_AT, OD_TILES = 257, 16
OD_V_AT = 273
N_BLOCKS = 381

BANKS = [2, 4, 3, 5]
DOWN_BANKS = [0, 2, 4, 3, 5, 6, 7, 1]
SSQ_BANK = 0

NORM_TO = [0, 1, 1, 1, 0, 1, 1, 1]
FFN_NORM = [0, 3, 4, 7]

OUT_NORM = [2, 3, 6, 7]
XQ_BASE, OD_BASE = [13, 37], 21

_SPLITS = [("n0", 8), ("h0", FC), ("n1", 8), ("gla", 4), ("y", 4), ("glu", 4), ("n2", 8), ("xa0", 8),
           ("n3", 8), ("h1", FC), ("n4", 8), ("h2", FC), ("n5", 8), ("att", 8), ("n6", 8), ("xa1", 8),
           ("n7", 8), ("h3", FC)]
BEFORE = {name: sum(n for _, n in _SPLITS[:i]) for i, (name, _) in enumerate(_SPLITS)}
X_LO_NORM = [BEFORE[f"n{i}"] for i in range(8)]
X_LO_HID = [BEFORE[f"h{i}"] for i in range(4)]
X_LO_GLA, X_LO_Y, X_LO_GLU, X_LO_ATT = (BEFORE[i] for i in ("gla", "y", "glu", "att"))
X_LO_XA = [BEFORE["xa0"], BEFORE["xa1"]]

ROPE_TILES = range(15)
UNITS = [(g, qb) for g in range(2) for qb in range(QB)]
UNIT_TR = [sum(qb + 1 for _, qb in UNITS[:i + 1]) for i in range(len(UNITS))]

V_GAIN = 0
V_MEMG = 72
V_GLAN = 80
V_BALPHA = 81
V_D = 83
V_BGLU = 87
V_LRE, V_LIM, V_LDT = 91, 107, 123
V_INVA, V_INVI = 139, 140
NV = 141
C_MAG, C_PH, C_PL, C_FR, C_FI = [16 * i for i in range(5)]

A_V = EV_TILES * T
A_BC = A_V + 4 * T
A_KINV = A_BC + 2 * T
A_KENDT = A_KINV + 2 * T
A_S = A_KENDT + 2 * T
A_O = A_S + 4 * T
ARENA = A_O + 4 * T
A_MEM = A_O
A_S5B = 5 * T
A_S5C = 7 * T
A_S5T = A_V
A_YG = ARENA - 4 * T
A_TIME = A_S5T + 14 * T
A_ODV = OD_TILES * T
A_TAB = A_ODV + 2 * T
A_SC = A_TAB + 4 * T
A_P = A_SC + 4 * T
A_P1 = A_TAB
A_PT = 10 * T
A_MEM1 = A_P
A_XP = 8 * T
A_XPT = A_XP + 4 * T


def build_trunk(nc, xT, memT, pos, vecs, w_alpha, s5b, s5c, mats, mask, rows, stream, out):
    with ExitStack() as ctx:
        def sb(name, shape, dt=F32):
            return ctx.enter_context(nc.sbuf_tensor(name, shape, dt))

        sems = {}

        def S(name):
            if name not in sems:
                sems[name] = ctx.enter_context(nc.semaphore(name))
            return sems[name]

        ps = ctx.enter_context(nc.psum_tensor("ps", [P, 8, T], F32))
        h = sb("h", [P, KC, T])
        X = [sb(f"x{i}", [P, KC, 2, T], F32R) for i in range(2)]
        W = sb("w_split", [P, 2, 2, BLK], F32R)
        raw = sb("w_raw", [P, 2, BLK])
        kv = sb("kv", [P, 8 * T])
        ar = sb("arena", [P, ARENA])
        tg = sb("tg", [P, 2, T])
        tu = sb("tu", [P, 2, T])
        sg = sb("sg", [P, 2, T])
        sq = sb("sq", [P, 2, T])
        rstd = sb("rstd", [P, T])
        std = sb("std", [P, T])
        vec = sb("vec", [P, NV])
        mat = sb("mat", [P, 4, P])
        msk = sb("msk", [P, P], I32)
        ones = sb("ones", [P, P])
        sc5 = sb("sc5", [P, 80])
        tiny = sb("tiny", [P, 12, 16])
        col = sb("col", [P, 64])
        epsc = sb("epsc", [P, 2])

        ident = mat[:, 0, :]
        cmask = mat[:, 3, :]
        gate = sb("gate", [P, 2])
        tiny_i = sb("tiny_i", [P, 16], I32)
        Pt = [ar[:, i * T:(i + 1) * T] for i in range(16)]
        KT = kv[:, 0:4 * T].rearrange("p (n m) -> p n m", m=MEM)
        VM = kv[:, 4 * T:8 * T].rearrange("p (t d) -> p t d", t=2)
        hid = ar[:, 0:FC * T].rearrange("p (k t) -> p k t", t=T)
        memX = X[0][:, 4:8, :, :].rearrange("p a b t -> p (a b t)").rearrange(
            "p (k s m) -> p k s m", k=KC, s=2)

        def area(at, n=T):
            return ar[:, at:at + n]

        val = area(A_V, 4 * T).rearrange("p (t d) -> p t d", t=4)
        kend_t = area(A_KENDT, 2 * T).rearrange("p (t q f) -> p t q f", t=4, q=2)
        state = area(A_S, 4 * T).rearrange("p (q c e) -> p q c e", q=2, c=NCH)
        chunk_mask = area(A_S)
        wal = area(A_S + T, 2 * P)[0:16, :]
        s5bt = area(A_S5B, 2 * T).rearrange("p (c q s) -> p c q s", c=2, q=4)
        s5ct = area(A_S5C, 2 * T).rearrange("p (c j o) -> p c j o", c=2, j=16)
        od_val = area(A_ODV, 2 * T).rearrange("p (t d) -> p t d", t=4)

        def gain(n, k):
            return vec[:, V_GAIN + 8 * n + k:V_GAIN + 8 * n + k + 1]

        block = ctx.enter_context(nc.Block())

        @block.sync
        def _(sp):
            sp.dma_start(raw[:, 0, :], stream[0]).then_inc(S("raw0_full"), 16)
            sp.dma_start(h[:, 0:2, :], xT[:, 0:2, :]).then_inc(S("x_in0"), 16)
            sp.dma_start(vec[:], vecs).then_inc(S("vec_in"), 16)
            sp.dma_start(raw[:, 1, :], stream[1]).then_inc(S("raw1_full"), 16)
            sp.dma_start(h[:, 2:8, :], xT[:, 2:8, :]).then_inc(S("x_in1"), 16)
            sp.dma_start(mat[:], mats).then_inc(S("mat_in"), 16)
            sp.dma_start(msk[:], mask).then_inc(S("msk_in"), 16)
            with sp.Fori(1, N_BLOCKS // 2) as i:
                for s in range(2):
                    sp.wait_ge(S("raw_used"), i * 2 + (s - 1))
                    sp.dma_start(raw[:, s, :], stream[bass.ds(i * 2 + s, 1)].rearrange("a p n -> p (a n)")
                                 ).then_inc(S(f"raw{s}_full"), 16)
            sp.wait_ge(S("raw_used"), N_BLOCKS - 2)
            sp.dma_start(raw[:, 0, :], stream[N_BLOCKS - 1]).then_inc(S("raw0_full"), 16)

        @block.gpsimd
        def _(pool):
            def split(s, b, full, first):
                pool.wait_ge(S(f"raw{s}_full"), full)
                if not first:
                    pool.wait_ge(S("block_done"), b - 1)
                    pool.tensor_tensor(gate[:, 0:1], gate[:, 1:2], gate[:, 1:2], ALU.add)
                pool.tensor_scalar(W[:, s, 0, :], raw[:, s, :], 1.0, 0.0, ALU.mult, ALU.add
                                   ).then_inc(S("w_hi"), 1)
                pool.wait_ge(S("w_hi"), b + 1)
                pool.tensor_tensor(W[:, s, 1, :], raw[:, s, :], W[:, s, 0, :].bitcast(F32), ALU.subtract
                                   ).then_inc(S("raw_used"), 1)

            pool.memset(gate[:], 0.0).then_inc(S("gate_set"), 1)
            pool.wait_ge(S("gate_set"), 1)
            split(0, 0, 16, True)
            split(1, 1, 16, True)
            with pool.Fori(1, N_BLOCKS // 2) as i:
                for s in range(2):
                    split(s, i * 2 + s, i * 16 + 16, False)
            split(0, N_BLOCKS - 1, 16 * (N_BLOCKS // 2 + 1), False)

        split_ready = S("raw_used")

        @block.tensor
        def _(pe):
            def mm3(dst, wh, wl, xh, xl, start, stop):
                pe.matmul(dst, wh, xh, start=start, stop=False)
                pe.matmul(dst, wh, xl, start=False, stop=False)
                return pe.matmul(dst, wl, xh, start=False, stop=stop)

            def tile_k(bank, slot, x, k, start, stop):
                c = slice(k * P, (k + 1) * P)
                return mm3(ps[:, bank, :], W[:, slot, 0, c], W[:, slot, 1, c],
                           X[x][:, k, 0, :], X[x][:, k, 1, :], start, stop)

            def ssq(n, k, cols=T):
                pe.wait_ge(S("sq_ready"), 8 * n + k + 1)
                if k == 0:
                    pe.wait_ge(*((S("ones_set"), 1) if n == 0 else (S("std_ready"), n)))
                pe.matmul(ps[:, SSQ_BANK, :], ones[:], sq[:, k % 2, :], start=(k == 0), stop=(k == 7)
                          ).then_inc(S("ssq_done"), 1)

            def tile(b, t, x, free=None):
                slot, bank = t
                pe.wait_ge(split_ready, b + 1)
                if free is not None:
                    pe.wait_ge(*free)
                for k in range(KC):
                    m = tile_k(bank, slot, x, k, k == 0, k == KC - 1)
                m.then_inc(S("block_done"), 1)

            def project(n, at, nt, x, free_sem, free_base, per, waits0, waits1):
                pe.wait_ge(split_ready, at + 2)
                for s, v in waits0:
                    pe.wait_ge(s, v)
                for k in range(KC):
                    pe.wait_ge(S("x_lo"), X_LO_NORM[n] + k + 1)
                    for t in range(min(2, nt)):
                        m = tile_k(BANKS[t], (at + t) % 2, x, k, k == 0, k == KC - 1)
                        if k == KC - 1:
                            m.then_inc(S("block_done"), 1)
                    if n in OUT_NORM and k < 2:
                        ssq(n, 6 + k)
                    elif n not in OUT_NORM and k >= 1:
                        ssq(n, k - 1)
                if n not in OUT_NORM:
                    ssq(n, KC - 1)
                for s, v in waits1:
                    pe.wait_ge(s, v)
                for t in (2, 3):
                    tile(at + t, ((at + t) % 2, BANKS[t]), x)
                full = (nt - 4) // 4
                if full >= 1:
                    with pe.Fori(1, 1 + full) as i:
                        for t in range(4):
                            need = (i * 2 + (t // 2 - 1) if per == 2 else i * 4 + (t - 3)) + free_base
                            tile(i * 4 + (at + t), ((at + t) % 2, BANKS[t]), x, (free_sem, need))
                for t in range(4 + 4 * full, nt):
                    tile(at + t, ((at + t) % 2, BANKS[t % 4]), x, (free_sem, free_base + t - 3))

            def ffn(f):
                n, at = FFN_NORM[f], FFN_AT[f]
                x, xo = NORM_TO[n], 1 - NORM_TO[n]
                w0 = [(S("h_ready"), 8 * (n - 1) + (3 if f == 2 else 6))] if n else []
                w1 = [(S("h_ready"), 8 * n)] if n else []
                project(n, at, 2 * FC, x, S("hid_done"), FC * f, 2, w0, w1)
                dn = at + 2 * FC

                def down_k(slot, d4, b, nn, start, stop):
                    c = slice(nn * P, (nn + 1) * P)
                    ch = [6, 7, 4, 5][d4]
                    return mm3(ps[:, DOWN_BANKS[nn], :], W[:, slot, 0, c], W[:, slot, 1, c],
                               X[xo][:, ch, 0, :], X[xo][:, ch, 1, :], start, stop)

                def down(b, slot, d4, lo, first):
                    pe.wait_ge(split_ready, b + 1)
                    pe.wait_ge(S("x_lo"), lo)
                    order = [5, 6, 7, 0, 1, 2, 3, 4]
                    for nn in order:
                        if first and nn == 0:
                            pe.wait_ge(S("std_ready"), n + 1)
                        if first and nn == 1:
                            pe.wait_ge(S("hid_done"), FC * (f + 1))
                        m = down_k(slot, d4, b, nn, first, False)
                    m.then_inc(S("block_done"), 1)

                lo0 = X_LO_HID[f]
                for d in range(4):
                    down(dn + d, (dn + d) % 2, d, lo0 + d + 1, d == 0)
                with pe.Fori(1, 5) as i:
                    for s in range(4):
                        down(i * 4 + (dn + s), (dn + s) % 2, s, i * 4 + (lo0 + s + 1), False)
                pe.wait_ge(split_ready, dn + FC)
                pe.wait_ge(S("x_lo"), lo0 + FC)
                for nn in range(8):
                    m = down_k((dn + 20) % 2, 0, 0, nn, False, False)
                    if nn == 7:
                        m.then_inc(S("block_done"), 1)
                    m = down_k((dn + 21) % 2, 1, 0, nn, False, True)
                    m.then_inc(S("down_out") if nn < 7 else S("block_done"), 1)

            def out_proj(o, lo, n_prev_free):
                at, n = OUT_AT[o], OUT_NORM[o]
                for s, v in n_prev_free:
                    pe.wait_ge(s, v)
                for t in range(8):
                    pe.wait_ge(split_ready, at + t + 1)
                    if t >= 4:
                        pe.wait_ge(S("h_ready"), 8 * (n - 1) + t - 3)
                    for k in range(KC):
                        if t == 0:
                            pe.wait_ge(S("x_lo"), lo[k])
                        m = tile_k(BANKS[t % 4], (at + t) % 2, 0, k, k == 0, k == KC - 1)
                    m.then_inc(S("block_done"), 1)
                    if t >= 2:
                        ssq(n, t - 2)

            def memory_norm(l):
                pe.wait_ge(*((S("rcol_ready"), 1) if l == 0 else (S("wi_ready"), 1)))
                for k in range(KC):
                    pe.wait_ge(S("msq_ready"), 8 * l + k + 1)
                    pe.matmul(ps[:, 1, 0:MEM], ones[:], sq[:, k % 2, 0:MEM], start=(k == 0), stop=(k == 7)
                              ).then_inc(S("mssq_done"), 1)

            def keys_values(l):
                at = KV_AT[l]
                pe.wait_ge(S("mem_lo"), 8 * l + 8)
                for t in range(8):
                    b = at + t
                    pe.wait_ge(split_ready, b + 1)
                    if t >= 2:
                        pe.wait_ge(S("kv_out"), 12 * l + t - 1)
                    for k in range(KC):
                        c = slice(k * P, (k + 1) * P)
                        m = mm3(ps[:, 6 + t % 2, 0:MEM], W[:, b % 2, 0, c], W[:, b % 2, 1, c],
                                memX[:, k, 0, :], memX[:, k, 1, :], k == 0, k == 7)
                    m.then_inc(S("block_done"), 1)
                for half in range(2):
                    pe.wait_ge(S("kv_out"), 12 * l + 8 + 2 * half)
                    for q in range(4):
                        b = at + 8 + 4 * half + q
                        pe.wait_ge(split_ready, b + 1)
                        for kk in range(2):
                            k = 2 * q + kk
                            for mt in range(2):
                                mc = slice(mt * P, (mt + 1) * P)
                                wc = slice(kk * T, (kk + 1) * T)
                                m = mm3(ps[:, 6 + mt, :], memX[:, k, 0, mc], memX[:, k, 1, mc],
                                        W[:, b % 2, 0, wc], W[:, b % 2, 1, wc], k == 0, k == 7)
                        m.then_inc(S("block_done"), 1)

            def values(at, nblk, width, free):
                for s, v in free:
                    pe.wait_ge(s, v)
                per = BLK // width
                for q in range(nblk):
                    b = at + q
                    pe.wait_ge(split_ready, b + 1)
                    for kk in range(per):
                        k = q * per + kk
                        for tt in range(4):
                            tc = slice(tt * P, (tt + 1) * P)
                            wc = slice(kk * width, (kk + 1) * width)
                            m = mm3(ps[:, BANKS[tt], 0:width], X[1][:, k, 0, tc], X[1][:, k, 1, tc],
                                    W[:, b % 2, 0, wc], W[:, b % 2, 1, wc], k == 0, k == 7)
                    m.then_inc(S("block_done"), 1)

            def rstd_columns(l):
                pe.wait_ge(S("rstd_ready"), [2, 6][l])
                if l == 0:
                    pe.wait_ge(S("mat_in"), 16)
                for tt in range(4):
                    m = pe.transpose(ps[:, 1, tt * P:(tt + 1) * P], rstd[:, tt * P:(tt + 1) * P], ident)
                m.then_inc(S("rcol_mm"), 1)

            def gla():
                pe.wait_ge(S("proj_out"), 5)
                pe.wait_ge(S("wal_in"), 16)
                pe.wait_ge(S("kv_out"), 12)
                for p in range(2):
                    m = pe.matmul(ps[:, 6 + p, :], wal[:, p * P:(p + 1) * P], Pt[4][0:16, :],
                                  start=True, stop=True)
                m.then_inc(S("alpha_mm"), 1)
                pe.wait_ge(S("kend"), 2)
                pe.wait_ge(S("zb_ready"), 2)
                for p in range(2):
                    for tt in range(4):
                        m = pe.transpose(ps[:, 6 + p, tt * P:(tt + 1) * P],
                                         Pt[7 + p][:, tt * P:(tt + 1) * P], ident)
                m.then_inc(S("kend_tr"), 1)
                pe.wait_ge(S("kend_t"), 2)
                pe.wait_ge(S("gla_v"), 4)
                for c in range(NCH - 1):
                    if c >= 4:
                        pe.wait_ge(S("state"), 4 * (c - 3))
                    r = slice(64 * (c % 2), 64 * (c % 2) + 64)
                    for p in range(2):
                        m = pe.matmul(ps[:, BANKS[c % 4], p * 256:(p + 1) * 256],
                                      kend_t[r, c // 2, p, :], val[r, c // 2, p * 256:(p + 1) * 256],
                                      start=True, stop=True)
                    m.then_inc(S("state_mm"), 1)
                pe.wait_ge(S("qdec"), 2)
                pe.wait_ge(S("kinv"), 2)

                def scores(hd):
                    p, r = hd // 2, slice(64 * (hd % 2), 64 * (hd % 2) + 64)
                    if hd >= 2:
                        pe.wait_ge(S("gscore"), hd - 1)
                    for tt in range(4):
                        tc = slice(tt * P, (tt + 1) * P)
                        m = pe.matmul(ps[:, 6 + hd % 2, tc], area(A_KINV + p * T)[r, tc], Pt[5 + p][r, tc],
                                      start=True, stop=True)
                    m.then_inc(S("gscore_mm"), 1)

                scores(0)
                pe.wait_ge(S("state"), 4 * (NCH - 1))
                for hd in range(4):
                    if hd < 3:
                        scores(hd + 1)
                    p, r = hd // 2, slice(64 * (hd % 2), 64 * (hd % 2) + 64)
                    pe.wait_ge(S("gscore"), hd + 1)
                    for tt in range(4):
                        dst = ps[:, BANKS[hd], tt * P:(tt + 1) * P]
                        pe.matmul(dst, val[:, tt, hd * P:(hd + 1) * P], tg[:, hd % 2, tt * P:(tt + 1) * P],
                                  start=True, stop=False)
                        for c in (2 * tt, 2 * tt + 1):
                            if c == 0:
                                continue
                            cc = slice(c * 64, (c + 1) * 64)
                            m = pe.matmul(ps[:, BANKS[hd], cc], state[r, p, c, :], Pt[5 + p][r, cc],
                                          start=False, stop=(c % 2 == 1))
                    m.then_inc(S("go_mm"), 1)
                    pe.wait_ge(S("gsq"), hd + 1)
                    if hd >= 2:
                        pe.wait_ge(S("gstd"), hd - 1)
                    pe.matmul(ps[:, hd % 2, :], ones[:], sq[:, hd % 2, :], start=True, stop=True
                              ).then_inc(S("gms_mm"), 1)

            def s5():
                def inputs(j):
                    q, r = j // 4, slice(32 * (j % 4), 32 * (j % 4) + 32)
                    if j == 0:
                        pe.wait_ge(S("s5b_in"), 16)
                        pe.wait_ge(S("gstd"), 4)
                        pe.wait_ge(S("gscore"), 4)
                    if j >= 2:
                        pe.wait_ge(S("s5_wi"), j - 1)
                    for c in range(2):
                        m = pe.matmul(ps[:, [0, 6][j % 2] + c, :], s5bt[r, c, q, :], Pt[q][r, :],
                                      start=True, stop=True)
                    m.then_inc(S("s5_in_mm"), 1)

                def outputs(j):
                    q, r = j // 4, slice(32 * (j % 4), 32 * (j % 4) + 32)
                    if j == 0:
                        pe.wait_ge(S("s5_c"), 2)
                        pe.wait_ge(S("gla_o"), 4)
                    pe.wait_ge(S("s5_xi"), j + 1)
                    t = A_S5T + (j % 2) * 7 * T
                    pe.matmul(ps[r, BANKS[q], :], s5ct[:, 0, j, :], area(t + 4 * T), start=True, stop=False)
                    pe.matmul(ps[r, BANKS[q], :], s5ct[:, 1, j, :], area(t + 6 * T), start=False, stop=True
                              ).then_inc(S("s5_out_mm"), 1)

                inputs(0)
                for j in range(S5_TILES):
                    if j + 1 < S5_TILES:
                        inputs(j + 1)
                    outputs(j)

            def glu():
                for n in range(4):
                    if n == 0:
                        pe.wait_ge(S("s5_wi"), 16)
                    pe.wait_ge(split_ready, GLU_AT + n // 2 + 1)
                    for k in range(4):
                        if n == 0:
                            pe.wait_ge(S("x_lo"), X_LO_Y + k + 1)
                        b = GLU_AT + n // 2
                        c = slice(((n % 2) * 4 + k) * P, ((n % 2) * 4 + k + 1) * P)
                        m = mm3(ps[:, [0, 1, 6, 7][n], :], W[:, b % 2, 0, c], W[:, b % 2, 1, c],
                                X[1][:, k, 0, :], X[1][:, k, 1, :], k == 0, k == 3)
                    m.then_inc(S("glu_mm") if n % 2 == 0 else S("block_done"), 1)

            def rope():
                pe.wait_ge(S("od_v"), 4)
                for i, t in enumerate(ROPE_TILES):
                    if i >= 4:
                        pe.wait_ge(S("rope_s"), i - 3)
                    pe.matmul(ps[:, BANKS[i % 4], :], mat[:, 1 if t < 10 else 2, :], Pt[t], start=True, stop=True
                              ).then_inc(S("rope_mm"), 1)
                pe.wait_ge(S("rcol_ready"), 2)
                for tt in range(4):
                    m = pe.transpose(ps[:, 1, tt * P:(tt + 1) * P], Pt[15][:, tt * P:(tt + 1) * P], ident)
                m.then_inc(S("wi_mm"), 1)

            def indexer():
                pe.wait_ge(S("rope_done"), len(ROPE_TILES))
                i = 0
                for qb in range(1, QB):
                    nk = (qb + 1) * P
                    for hd in range(IDX_HEADS):
                        r = slice(64 * (hd % 2), 64 * (hd % 2) + 64)
                        if i >= 4:
                            pe.wait_ge(S("relu"), i - 3)
                        pe.matmul(ps[:, BANKS[i % 4], 0:nk], Pt[10 + hd // 2][r, qb * P:(qb + 1) * P],
                                  Pt[14][r, 0:nk], start=True, stop=True).then_inc(S("logit_mm"), 1)
                        i += 1

            def attention():
                def scores(i):
                    g, qb = UNITS[i]
                    nk = (qb + 1) * P
                    if i == 0:
                        pe.wait_ge(S("relu"), 24)
                    if i >= 1:
                        pe.wait_ge(S("att_s"), i)
                    for j in range(4):
                        m = pe.matmul(ps[:, 2 + j, 0:nk], Pt[4 * g + j][:, qb * P:(qb + 1) * P],
                                      Pt[8 + g][:, 0:nk], start=True, stop=True)
                    m.then_inc(S("att_mm"), 1)

                nt = 0
                scores(0)
                for i, (g, qb) in enumerate(UNITS):
                    pe.wait_ge(S("att_p"), i + 1)
                    if i == 0:
                        pe.wait_ge(S("kv_out"), 24)
                    pb = A_P if i % 2 == 0 else A_P1
                    for kc in range(qb + 1):
                        if nt >= 2:
                            pe.wait_ge(S("att_t"), nt - 1)
                        for j in range(4):
                            m = pe.transpose(ps[:, 6 + nt % 2, j * P:(j + 1) * P],
                                             area(pb + j * T)[:, kc * P:(kc + 1) * P], ident)
                        m.then_inc(S("att_tr"), 1)
                        nt += 1
                    if i + 1 < len(UNITS):
                        scores(i + 1)
                    if i >= 2:
                        pe.wait_ge(S("x_lo"), X_LO_ATT + i - 1)
                    pe.wait_ge(S("att_t"), nt)
                    for kc in range(qb + 1):
                        m = pe.matmul(ps[:, i % 2, :], od_val[:, kc, g * P:(g + 1) * P],
                                      area(A_PT + kc * T), start=(kc == 0), stop=(kc == qb))
                    m.then_inc(S("att_o"), 1)

            def cross(l):
                base = XQ_BASE[l]

                pe.wait_ge(S("kv_out"), 12 * (l + 1))

                def scores(hd):
                    if hd >= 1:
                        pe.wait_ge(S("xa_p"), 4 * l + hd)
                    for qb in range(QB):
                        for c in range(2):
                            m = pe.matmul(ps[:, 2 + qb // 2, (qb % 2) * MEM:(qb % 2 + 1) * MEM],
                                          Pt[2 * hd + c][:, qb * P:(qb + 1) * P], KT[:, 2 * hd + c, :],
                                          start=(c == 0), stop=(c == 1))
                    m.then_inc(S("xa_mm"), 1)

                pe.wait_ge(S("proj_out"), base + 8)
                scores(0)
                for hd in range(XA_HEADS):
                    pe.wait_ge(S("xa_pn"), 4 * l + hd + 1)
                    if hd >= 1:
                        pe.wait_ge(S("xa_t"), 8 * l + 2 * hd)
                    pb = A_XP + (hd % 2) * 2 * T
                    for mc in range(2):
                        for qb in range(QB):
                            m = pe.transpose(ps[:, 6 + mc, qb * P:(qb + 1) * P],
                                             area(pb + qb * MEM)[:, mc * P:(mc + 1) * P], ident)
                        m.then_inc(S("xa_tr"), 1)
                    if hd < 3:
                        scores(hd + 1)
                    pe.wait_ge(S("xa_t"), 8 * l + 2 * hd + 2)
                    for dc in range(2):
                        if hd >= 1:
                            pe.wait_ge(S("x_lo"), X_LO_XA[l] + 2 * (hd - 1) + dc + 1)
                        ch = 2 * hd + dc
                        for mc in range(2):
                            m = pe.matmul(ps[:, 4 + dc, :], VM[:, mc, ch * P:(ch + 1) * P],
                                          area(A_XPT + (hd % 2) * 2 * T + mc * T), start=(mc == 0), stop=(mc == 1))
                        m.then_inc(S("xa_o"), 1)

            ffn(0)
            project(1, EV_AT, EV_TILES, 1, S("proj_out"), 0, 1,
                    [(S("h_ready"), 3)], [(S("h_ready"), 8)])
            rstd_columns(0)
            values(EV_V_AT, 4, T, [(S("proj_out"), 13)])
            memory_norm(0)
            keys_values(0)
            gla()
            s5()
            glu()
            out_proj(0, [X_LO_GLA + k + 1 for k in range(4)] + [X_LO_GLU + k + 1 for k in range(4)],
                     [(S("s5_y"), 4)])
            project(2, XQ_AT[0], 8, 1, S("proj_out"), XQ_BASE[0], 1,
                    [(S("h_ready"), 14), (S("glu_sig"), 4)], [(S("h_ready"), 16)])
            cross(0)
            out_proj(1, [X_LO_XA[0] + k + 1 for k in range(8)], [])
            ffn(1)
            ffn(2)
            project(5, OD_AT, OD_TILES, 1, S("proj_out"), OD_BASE, 1,
                    [(S("h_ready"), 35)], [(S("h_ready"), 40)])
            rstd_columns(1)
            values(OD_V_AT, 2, 2 * P, [(S("proj_out"), OD_BASE + 16)])
            rope()
            indexer()
            memory_norm(1)
            keys_values(1)
            attention()
            out_proj(2, [X_LO_ATT + 8] * 8, [(S("att_s"), 8)])
            project(6, XQ_AT[1], 8, 1, S("proj_out"), XQ_BASE[1], 1,
                    [(S("h_ready"), 46), (S("x_lo"), X_LO_ATT + 8)], [(S("h_ready"), 48)])
            cross(1)
            out_proj(3, [X_LO_XA[1] + k + 1 for k in range(8)], [])
            ffn(3)
            for k in range(KC):
                if k == 0:
                    pe.wait_ge(S("h_ready"), 8 * 7 + 1)
                ssq(8, k)

        @block.scalar
        def _(act):
            def hi(dst, src, count, **kw):
                act.activation(dst, src, ACT.Copy, **kw).then_inc(S("x_hi"), 1)

            def norm(n):
                to = NORM_TO[n] if n < 8 else None
                for k in range(KC):
                    if n == 0:
                        if k == 0:
                            act.wait_ge(S("vec_in"), 16)
                            act.wait_ge(S("x_in0"), 16)
                        if k == 2:
                            act.wait_ge(S("x_in1"), 16)
                    else:
                        act.wait_ge(S("h_ready"), 8 * (n - 1) + k + 1)
                    if to is not None:
                        if n in (1, 4, 5) and k >= 4:
                            f = {1: 0, 4: 1, 5: 2}[n]
                            act.wait_ge(S("block_done"), FFN_AT[f] + FFN_BLOCKS - (2 if k < 6 else 0))
                        hi(X[to][:, k, 0, :], h[:, k, :], 0, scale=gain(n, k))
                    if 8 * n + k >= 2:
                        act.wait_ge(S("ssq_done"), 8 * n + k - 1)
                    act.activation(sq[:, k % 2, :], h[:, k, :], ACT.Square).then_inc(S("sq_ready"), 1)
                if n == 0:
                    act.wait_ge(S("eps_set"), 2)
                act.wait_ge(S("ssq_done"), 8 * n + 8)
                if n >= 1:
                    act.wait_ge(S("rstd_ready"), n)
                act.activation(std[:], ps[:, SSQ_BANK, :], ACT.Sqrt, bias=epsc[:, 0:1]
                               ).then_inc(S("std_ready"), 1)

            def ffn(f):
                at, xo = FFN_AT[f], 1 - NORM_TO[FFN_NORM[f]]

                def silu(s, need):
                    act.wait_ge(S("gate_ready"), need)
                    act.activation(sg[:, s, :], tg[:, s, :], ACT.Silu).then_inc(S("silu"), 1)

                with act.Fori(0, FC // 2) as i:
                    for s in range(2):
                        silu(s, i * 2 + (FC * f + s + 1))
                dn = at + 2 * FC

                def part(d, d4, used):
                    if used is not None:
                        act.wait_ge(S("block_done"), used)
                    ch = [6, 7, 4, 5][d4]
                    act.activation(X[xo][:, ch:ch + 1, 0, :], hid[:, d, :], ACT.Copy).then_inc(S("x_hi"), 1)

                for d in range(4):
                    act.wait_ge(S("hid_done"), FC * f + d + 1)
                    part(slice(d, d + 1), d, None)
                act.wait_ge(S("hid_done"), FC * (f + 1))
                with act.Fori(1, 5) as i:
                    for s in range(4):
                        part(bass.ds(i * 4 + s, 1), s, i * 4 + (dn + s - 3))
                for d in (20, 21):
                    part(slice(d, d + 1), d % 4, dn + d - 3)

            def memory(l):
                at = A_MEM if l == 0 else A_MEM1
                m = area(at, 4 * T).rearrange("p (k m) -> p k m", m=MEM)
                if l == 0:
                    act.wait_ge(S("hid_done"), FC)
                    act.wait_ge(S("x_hi"), 8 + FC)
                else:
                    act.wait_ge(S("hid_done"), 3 * FC)
                act.dma_start(m, memT).then_inc(S("mem_in"), 16)
                if l == 0:
                    act.dma_start(chunk_mask, rows[1:2, :].to_broadcast([P, T])).then_inc(S("cmask_in"), 16)
                    act.dma_start(wal, w_alpha).then_inc(S("wal_in"), 16)
                act.wait_ge(S("mem_in"), 16 * (l + 1))
                for k in range(KC):
                    if k >= 2:
                        act.wait_ge(S("mssq_done"), 8 * l + k - 1)
                    act.activation(sq[:, k % 2, 0:MEM], m[:, k, :], ACT.Square).then_inc(S("msq_ready"), 1)
                act.wait_ge(S("mssq_done"), 8 * l + 8)
                act.wait_ge(S("rcol_ready"), l + 1)
                act.activation(std[:, 0:MEM], ps[:, 1, 0:MEM], ACT.Sqrt, bias=epsc[:, 0:1]
                               ).then_inc(S("mstd"), 1)
                for k in range(KC):
                    act.wait_ge(S("mem_n"), 8 * l + k + 1)
                    act.activation(memX[:, k, 0, :], m[:, k, :], ACT.Copy).then_inc(S("mem_hi"), 1)

            def keys_values(l):
                for t in range(8):
                    act.wait_ge(S("block_done"), KV_AT[l] + t + 1)
                    act.activation(KT[:, t, :], ps[:, 6 + t % 2, 0:MEM], ACT.Copy).then_inc(S("kv_out"), 1)
                for half in range(2):
                    act.wait_ge(S("block_done"), KV_AT[l] + 12 + 4 * half)
                    for mt in range(2):
                        act.activation(VM[:, mt, half * T:(half + 1) * T], ps[:, 6 + mt, :], ACT.Copy
                                       ).then_inc(S("kv_out"), 1)

            def gla():
                for p in range(2):
                    act.wait_ge(S("zb_ready"), p + 1)
                    act.activation(sg[:, p, :], tu[:, p, :], ACT.Abs).then_inc(S("g_abs"), 1)
                act.wait_ge(S("g_abs"), 2)
                act.activation(sg[:, :, :], sg[:, :, :], ACT.Exp, scale=-1.0).then_inc(S("g_exp"), 1)
                act.wait_ge(S("g_exp"), 1)
                act.activation(sg[:, :, :], sg[:, :, :], ACT.Ln, bias=1.0).then_inc(S("g_ln"), 1)
                for p in range(2):
                    bc = area(A_BC + p * T)
                    act.wait_ge(S("g_cum"), p + 1)
                    if p == 0:
                        act.wait_ge(S("g_cum"), 2)
                    act.activation(tg[:, p, :], bc, ACT.Exp, scale=1.0 / GLA_TAU).then_inc(S("g_eb"), 1)
                    act.activation(area(A_KINV + p * T), bc, ACT.Exp, scale=-1.0 / GLA_TAU).then_inc(S("g_einv"), 1)
                    act.activation(col[:, p * 8:p * 8 + 8], bc.rearrange("p (c i) -> p c i", i=64)[:, :, 63],
                                   ACT.Exp, scale=1.0 / GLA_TAU).then_inc(S("g_decay"), 1)
                for p in range(2):
                    act.wait_ge(S("g_rel"), p + 1)
                    act.activation(tu[:, p, :], tu[:, p, :], ACT.Exp, scale=-1.0 / GLA_TAU).then_inc(S("g_eend"), 1)
                act.wait_ge(S("proj_out"), 13)
                act.activation(ar[:, 9 * T:13 * T], ar[:, 9 * T:13 * T], ACT.Silu).then_inc(S("g_silu"), 1)
                act.wait_ge(S("kend_tr"), 1)
                for p in range(2):
                    act.activation(kend_t[:, :, p, :], ps[:, 6 + p, :].rearrange("p (t f) -> p t f", t=4), ACT.Copy
                                   ).then_inc(S("kend_t"), 1)
                for hd in range(4):
                    act.wait_ge(S("go_mm"), hd + 1)
                    if hd >= 2:
                        act.wait_ge(S("gms_mm"), hd - 1)
                    act.activation(sq[:, hd % 2, :], ps[:, BANKS[hd], :], ACT.Square).then_inc(S("gsq"), 1)
                    act.wait_ge(S("gms_mm"), hd + 1)
                    if hd == 0:
                        act.wait_ge(S("mrstd"), 1)
                    if hd >= 1:
                        act.wait_ge(S("grstd"), hd)
                    act.activation(std[:], ps[:, hd % 2, :], ACT.Sqrt, bias=epsc[:, 0:1], scale=float(KC)
                                   ).then_inc(S("gstd"), 1)
                    act.wait_ge(S("gla_o"), hd + 1)
                    hi(X[0][:, hd, 0, :], area(A_O + hd * T), 0)

            def s5_constants():
                act.wait_ge(S("th_ready"), 1)
                act.activation(tiny[:, 6, :], tiny[:, 5, :], ACT.Abs).then_inc(S("th_abs"), 1)
                act.activation(tiny[:, 8, :], tiny[:, 5, :], ACT.Sin).then_inc(S("th_trig"), 1)
                act.wait_ge(S("th_abs"), 1)
                act.activation(tiny[:, 7, :], tiny[:, 6, :], ACT.Sin, scale=-1.0, bias=epsc[:, 1:2]
                               ).then_inc(S("th_trig"), 1)

            def s5():
                act.dma_start(s5bt[:], s5b).then_inc(S("s5b_in"), 16)
                act.dma_start(s5ct[:], s5c).then_inc(S("s5c_in"), 16)
                act.wait_ge(S("x_lo"), X_LO_GLA + 4)
                act.dma_start(area(A_TIME), rows[0:1, :].to_broadcast([P, T])).then_inc(S("time_in"), 16)
                for j in range(S5_TILES):
                    t = A_S5T + (j % 2) * 7 * T
                    act.wait_ge(S("s5_turn"), j + 1)
                    act.activation(area(t + T), area(t + 2 * T), ACT.Sin, scale=TWO_PI_BELOW).then_inc(S("s5_sin"), 1)
                    act.activation(area(t + 2 * T), area(t + 2 * T), ACT.Abs).then_inc(S("s5_abs"), 1)
                    act.wait_ge(S("s5_abs"), j + 1)
                    act.activation(area(t), area(t + 2 * T), ACT.Sin, scale=-TWO_PI_BELOW, bias=epsc[:, 1:2]
                                   ).then_inc(S("s5_cos"), 1)
                for q in range(4):
                    act.wait_ge(S("s5_y"), q + 1)
                    act.activation(area(A_YG + q * T), area(A_YG + q * T), ACT.Gelu_apprx_tanh).then_inc(S("gelu"), 1)
                    act.wait_ge(S("gelu"), q + 1)
                    hi(X[1][:, q, 0, :], area(A_YG + q * T), 0)

            def glu():
                for n in range(4):
                    if n % 2 == 0:
                        act.wait_ge(S("glu_mm"), n // 2 + 1)
                    else:
                        act.wait_ge(S("block_done"), GLU_AT + n // 2 + 1)
                    if n >= 2:
                        act.wait_ge(S("glu_o"), n - 1)
                    act.activation(sg[:, n % 2, :], ps[:, [0, 1, 6, 7][n], :], ACT.Sigmoid,
                                   bias=vec[:, V_BGLU + n:V_BGLU + n + 1]).then_inc(S("glu_sig"), 1)
                    act.wait_ge(S("glu_o"), n + 1)
                    hi(X[0][:, 4 + n, 0, :], area(A_YG + n * T), 0)

            def tables():
                act.dma_start(area(A_SC + T).bitcast(I32), pos.to_broadcast([P, T])).then_inc(S("pos_in"), 16)
                for i in range(2):
                    act.wait_ge(S("ang"), i + 1)
                    s, c = area(A_TAB + (2 * i + 1) * T), area(A_TAB + 2 * i * T)
                    act.activation(c, s, ACT.Abs).then_inc(S("ang_abs"), 1)
                    act.wait_ge(S("ang_abs"), i + 1)
                    act.activation(s, s, ACT.Sin).then_inc(S("tab"), 1)
                    act.activation(c, c, ACT.Sin, scale=-1.0, bias=epsc[:, 1:2]).then_inc(S("tab"), 1)

            def indexer():
                for i in range(24):
                    nk = (i // 8 + 2) * P
                    act.wait_ge(S("logit_mm"), i + 1)
                    if i >= 2:
                        act.wait_ge(S("idx_acc"), i - 1)
                    act.activation(tg[:, i % 2, 0:nk], ps[:, BANKS[i % 4], 0:nk], ACT.Relu).then_inc(S("relu"), 1)

            def attention():
                nt = 0
                for i, (g, qb) in enumerate(UNITS):
                    nk = (qb + 1) * P
                    pb = A_P if i % 2 == 0 else A_P1
                    act.wait_ge(S("att_nm"), i + 1)
                    for j in range(4):
                        act.activation(area(pb + j * T)[:, 0:nk], area(pb + j * T)[:, 0:nk], ACT.Exp,
                                       bias=col[:, 4 + j:5 + j], accum_out=col[:, 8 + j:9 + j]
                                       ).then_inc(S("att_e"), 1)
                    for kc in range(qb + 1):
                        act.wait_ge(S("att_tr"), nt + 1)
                        if i >= 1 and kc == 0:
                            act.wait_ge(S("att_o"), i)
                        act.activation(area(A_PT + kc * T), ps[:, 6 + nt % 2, :], ACT.Copy).then_inc(S("att_t"), 1)
                        nt += 1
                    act.wait_ge(S("att_o"), i + 1)
                    hi(X[0][:, 4 * g:4 * g + 4, 0, qb * P:(qb + 1) * P],
                       ps[:, i % 2, :].rearrange("p (j q) -> p j q", j=4), 0)

            def cross(l):
                for hd in range(XA_HEADS):
                    pb = A_XP + (hd % 2) * 2 * T
                    act.wait_ge(S("xa_nm"), 4 * l + hd + 1)
                    for qb in range(QB):
                        e = act.activation(area(pb + qb * MEM, MEM),
                                           ps[:, 2 + qb // 2, (qb % 2) * MEM:(qb % 2 + 1) * MEM], ACT.Exp,
                                           scale=XA_DIM ** -0.5, bias=col[:, 4 + qb:5 + qb],
                                           accum_out=col[:, 8 + qb:9 + qb])
                    e.then_inc(S("xa_p"), 1)
                    for mc in range(2):
                        act.wait_ge(S("xa_tr"), 8 * l + 2 * hd + mc + 1)
                        if hd >= 2:
                            act.wait_ge(S("xa_o"), 8 * l + 2 * hd - 2)
                        act.activation(area(A_XPT + (hd % 2) * 2 * T + mc * T), ps[:, 6 + mc, :], ACT.Copy
                                       ).then_inc(S("xa_t"), 1)
                    for dc in range(2):
                        act.wait_ge(S("xa_o"), 8 * l + 2 * hd + dc + 1)
                        hi(X[0][:, 2 * hd + dc, 0, :], ps[:, 4 + dc, :], 0)

            norm(0)
            ffn(0)
            norm(1)
            memory(0)
            s5_constants()
            keys_values(0)
            gla()
            s5()
            glu()
            norm(2)
            cross(0)
            norm(3)
            ffn(1)
            norm(4)
            ffn(2)
            norm(5)
            tables()
            indexer()
            memory(1)
            keys_values(1)
            attention()
            norm(6)
            cross(1)
            norm(7)
            ffn(3)
            norm(8)
            for k in range(KC):
                act.wait_ge(S("y_ready"), k + 1)
                act.dma_start(out[:, k, :], h[:, k, :]).then_inc(S("out_done"), 16)
            act.wait_ge(S("out_done"), 16 * KC)

        @block.vector
        def _(dve):
            step = [0]

            def chain(ins):
                step[0] += 1
                ins.then_inc(S("dve_step"), 1)
                dve.wait_ge(S("dve_step"), step[0])

            def lo_of(dst, src, hi_ap, count):
                dve.wait_ge(S("x_hi"), count)
                dve.tensor_tensor(dst, src, hi_ap.bitcast(F32), ALU.subtract).then_inc(S("x_lo"), 1)

            def norm(n, factor, mm_sem, mm_base, banks):
                to = NORM_TO[n] if n < 8 else None

                def lower(k):
                    if to is None:
                        return
                    dve.wait_ge(S("x_hi"), X_LO_NORM[n] + k + 1)
                    dve.scalar_tensor_tensor(X[to][:, k, 1, :], h[:, k, :], gain(n, k),
                                             X[to][:, k, 0, :].bitcast(F32), ALU.mult, ALU.subtract
                                             ).then_inc(S("x_lo"), 1)

                if n == 0:
                    for k in range(KC):
                        lower(k)
                else:
                    for k in range(KC):
                        if mm_sem is not None and k < 7:
                            dve.wait_ge(mm_sem, mm_base[0] + k + 1)
                        elif mm_sem is not None:
                            dve.wait_ge(S("block_done"), mm_base[1])
                        else:
                            dve.wait_ge(S("block_done"), mm_base[0] + k + 1)
                        dve.scalar_tensor_tensor(h[:, k, :], ps[:, banks[k], :], factor, h[:, k, :],
                                                 ALU.mult, ALU.add).then_inc(S("h_ready"), 1)
                        if k >= 1:
                            lower(k - 1)
                    lower(KC - 1)
                dve.wait_ge(S("std_ready"), n + 1)
                dve.reciprocal(rstd[:], std[:]).then_inc(S("rstd_ready"), 1)
                dve.wait_ge(S("rstd_ready"), n + 1)

            def norm_after_ffn(n, f):
                norm(n, 0.5, S("down_out"), (7 * f, FFN_AT[f] + FFN_BLOCKS), DOWN_BANKS)

            def norm_after_out(n, o):
                norm(n, 1.0, None, (OUT_AT[o],), [BANKS[t % 4] for t in range(8)])

            def ffn(f):
                at, xo = FFN_AT[f], 1 - NORM_TO[FFN_NORM[f]]
                with dve.Fori(0, FC // 2) as i:
                    for s in range(2):
                        j = i * 2 + s
                        dve.wait_ge(S("block_done"), i * 4 + (at + 2 * s + 1))
                        dve.tensor_tensor(tg[:, s, :], ps[:, BANKS[2 * s], :], rstd[:], ALU.mult
                                          ).then_inc(S("gate_ready"), 1)
                        dve.wait_ge(S("block_done"), i * 4 + (at + 2 * s + 2))
                        dve.tensor_tensor(tu[:, s, :], ps[:, BANKS[2 * s + 1], :], rstd[:], ALU.mult
                                          ).then_inc(S("up_ready"), 1)
                        dve.wait_ge(S("up_ready"), i * 2 + (FC * f + s + 1))
                        dve.wait_ge(S("silu"), i * 2 + (FC * f + s + 1))
                        dve.tensor_tensor(hid[:, bass.ds(j, 1), :], sg[:, s:s + 1, :], tu[:, s:s + 1, :], ALU.mult
                                          ).then_inc(S("hid_done"), 1)

                def part(d, d4, count):
                    ch = [6, 7, 4, 5][d4]
                    dve.wait_ge(S("x_hi"), count)
                    dve.tensor_tensor(X[xo][:, ch:ch + 1, 1, :], hid[:, d, :],
                                      X[xo][:, ch:ch + 1, 0, :].bitcast(F32), ALU.subtract
                                      ).then_inc(S("x_lo"), 1)

                base = X_LO_HID[f]
                dve.wait_ge(S("hid_done"), FC * (f + 1))
                for d in range(4):
                    part(slice(d, d + 1), d, base + d + 1)
                with dve.Fori(1, 5) as i:
                    for s in range(4):
                        part(bass.ds(i * 4 + s, 1), s, i * 4 + (base + s + 1))
                for d in (20, 21):
                    part(slice(d, d + 1), d % 4, base + d + 1)

            def projected(at, nt, base):
                PA = ar[:, 0:16 * T].rearrange("p (t n) -> p t n", n=T)

                def one(t, b, bank):
                    dve.wait_ge(S("block_done"), b + 1)
                    dve.tensor_tensor(PA[:, t, :], ps[:, bank:bank + 1, :], rstd[:].unsqueeze(1), ALU.mult
                                      ).then_inc(S("proj_out"), 1)

                with dve.Fori(0, nt // 4) as i:
                    for s in range(4):
                        one(bass.ds(i * 4 + s, 1), i * 4 + (at + s), BANKS[s])
                for t in range(nt - nt % 4, nt):
                    one(slice(t, t + 1), at + t, BANKS[t % 4])

            def rstd_columns(l):
                dve.wait_ge(S("rcol_mm"), l + 1)
                dve.tensor_copy(col[:, 16:20], ps[:, 1, :].rearrange("p (t n) -> p t n", n=P)[:, :, 0]
                                ).then_inc(S("rcol_ready"), 1)
                dve.wait_ge(S("rcol_ready"), l + 1)

            def memory(l):
                at = A_MEM if l == 0 else A_MEM1
                m = area(at, 4 * T).rearrange("p (k m) -> p k m", m=MEM)
                dve.wait_ge(S("mstd"), l + 1)
                dve.reciprocal(rstd[:, 0:MEM], std[:, 0:MEM]).then_inc(S("mrstd"), 1)
                dve.wait_ge(S("mrstd"), l + 1)
                for k in range(KC):
                    g = vec[:, V_MEMG + k:V_MEMG + k + 1]
                    dve.scalar_tensor_tensor(m[:, k, :], m[:, k, :], g, rstd[:, 0:MEM], ALU.mult, ALU.mult
                                             ).then_inc(S("mem_n"), 1)
                for k in range(KC):
                    dve.wait_ge(S("mem_hi"), 8 * l + k + 1)
                    dve.tensor_tensor(memX[:, k, 1, :], m[:, k, :], memX[:, k, 0, :].bitcast(F32), ALU.subtract
                                      ).then_inc(S("mem_lo"), 1)

            def tn(i):
                return tiny[:, i, :]

            def exact_exp(dst, src):
                k, r, p = tn(9), tn(10), tn(11)
                chain(dve.tensor_scalar(k, src, 1.4426950408889634, MAGIC, ALU.mult, ALU.add))
                chain(dve.tensor_scalar(k, k, MAGIC, None, ALU.subtract))
                chain(dve.tensor_scalar(k, k, -126.0, 127.0, ALU.max, ALU.min))
                chain(dve.scalar_tensor_tensor(r, k, -0.693359375, src, ALU.mult, ALU.add))
                chain(dve.scalar_tensor_tensor(r, k, 2.12194440e-4, r, ALU.mult, ALU.add))
                chain(dve.tensor_scalar(p, r, 1.0 / 5040, 1.0 / 720, ALU.mult, ALU.add))
                for c in (1.0 / 120, 1.0 / 24, 1.0 / 6, 0.5, 1.0, 1.0):
                    chain(dve.tensor_tensor(p, p, r, ALU.mult))
                    chain(dve.tensor_scalar(p, p, c, None, ALU.add))
                chain(dve.tensor_scalar(k, k, 127.0, None, ALU.add))
                chain(dve.tensor_copy(tiny_i[:], k))
                chain(dve.tensor_scalar(tiny_i[:], tiny_i[:], 23, None, ALU.logical_shift_left))
                chain(dve.tensor_tensor(dst, p, tiny_i[:].bitcast(F32), ALU.mult))

            def s5_constants():
                lr, dt, th, ab_r, ab_i = tn(0), tn(1), tn(2), tn(3), tn(4)
                mag, ph, pl = sc5[:, C_MAG:C_MAG + 16], sc5[:, C_PH:C_PH + 16], sc5[:, C_PL:C_PL + 16]
                fr, fi = sc5[:, C_FR:C_FR + 16], sc5[:, C_FI:C_FI + 16]
                li = vec[:, V_LIM:V_LIM + 16]
                dve.wait_ge(S("vec_in"), 16)
                chain(dve.tensor_scalar(lr, vec[:, V_LRE:V_LRE + 16], -1e-4, None, ALU.min))
                exact_exp(dt, vec[:, V_LDT:V_LDT + 16])
                chain(dve.tensor_tensor(th, lr, dt, ALU.mult))
                exact_exp(mag, th)
                chain(dve.tensor_tensor(th, li, dt, ALU.mult))
                reduce_angle(th, tn(5))
                dve.tensor_scalar(tn(5), th, PI_BELOW, -PI_BELOW, ALU.min, ALU.max).then_inc(S("th_ready"), 1)
                chain(dve.tensor_scalar(th, th, 0.15915494309189535, None, ALU.mult))
                chain(dve.tensor_scalar(ph, th, 4096.0, MAGIC, ALU.mult, ALU.add))
                chain(dve.tensor_scalar(ph, ph, MAGIC, 1.0 / 4096, ALU.subtract, ALU.mult))
                chain(dve.tensor_tensor(pl, th, ph, ALU.subtract))
                dve.wait_ge(S("th_trig"), 2)
                chain(dve.tensor_tensor(ab_r, tn(7), mag, ALU.mult))
                chain(dve.tensor_tensor(ab_i, tn(8), mag, ALU.mult))
                chain(dve.tensor_scalar(ab_r, ab_r, 1.0, None, ALU.subtract))
                den, t1 = tn(5), tn(6)
                chain(dve.tensor_tensor(den, lr, lr, ALU.mult))
                chain(dve.tensor_tensor(t1, li, li, ALU.mult))
                chain(dve.tensor_tensor(den, den, t1, ALU.add))
                chain(dve.reciprocal(den, den))
                chain(dve.tensor_tensor(fr, ab_r, lr, ALU.mult))
                chain(dve.tensor_tensor(t1, ab_i, li, ALU.mult))
                chain(dve.tensor_tensor(fr, fr, t1, ALU.add))
                chain(dve.tensor_tensor(fr, fr, den, ALU.mult))
                chain(dve.tensor_tensor(fi, ab_i, lr, ALU.mult))
                chain(dve.tensor_tensor(t1, ab_r, li, ALU.mult))
                chain(dve.tensor_tensor(fi, fi, t1, ALU.subtract))
                chain(dve.tensor_tensor(fi, fi, den, ALU.mult))

            def reduce_angle(x, k):
                chain(dve.tensor_scalar(k, x, 0.15915494309189535, MAGIC, ALU.mult, ALU.add))
                chain(dve.tensor_scalar(k, k, MAGIC, None, ALU.subtract))
                for c in (TWO_PI_1, TWO_PI_2, TWO_PI_3):
                    chain(dve.scalar_tensor_tensor(x, k, -c, x, ALU.mult, ALU.add))

            def gla():
                dve.wait_ge(S("alpha_mm"), 1)
                for p in range(2):
                    dve.tensor_scalar(tu[:, p, :], ps[:, 6 + p, :], vec[:, V_BALPHA + p:V_BALPHA + p + 1], None,
                                      ALU.add).then_inc(S("zb_ready"), 1)
                dve.wait_ge(S("g_ln"), 1)
                dve.wait_ge(S("cmask_in"), 16)
                for p in range(2):
                    chain(dve.scalar_tensor_tensor(tu[:, p, :], tu[:, p, :], 0.0, sg[:, p, :], ALU.min, ALU.subtract))
                    dve.tensor_tensor_scan(area(A_BC + p * T), chunk_mask, tu[:, p, :], 0.0, ALU.mult, ALU.add
                                           ).then_inc(S("g_cum"), 1)
                dve.wait_ge(S("g_cum"), 2)
                for p in range(2):
                    bc = area(A_BC + p * T).rearrange("p (c i) -> p c i", i=64)
                    dve.tensor_tensor(tu[:, p, :].rearrange("p (c i) -> p c i", i=64), bc,
                                      bc[:, :, 63:64].to_broadcast([P, NCH, 64]), ALU.subtract).then_inc(S("g_rel"), 1)
                for p in range(2):
                    dve.wait_ge(S("g_eb"), p + 1)
                    dve.scalar_tensor_tensor(Pt[5 + p], Pt[5 + p], GLA_DK ** -0.5, tg[:, p, :], ALU.mult, ALU.mult
                                             ).then_inc(S("qdec"), 1)
                    dve.wait_ge(S("g_einv"), p + 1)
                    dve.tensor_tensor(area(A_KINV + p * T), area(A_KINV + p * T), Pt[7 + p], ALU.mult
                                      ).then_inc(S("kinv"), 1)
                    dve.wait_ge(S("g_eend"), p + 1)
                    dve.tensor_tensor(Pt[7 + p], Pt[7 + p], tu[:, p, :], ALU.mult).then_inc(S("kend"), 1)
                dve.wait_ge(S("qdec"), 2)
                for p in range(2):
                    chain(dve.memset(tg[:, p, :], 0.0))
                dve.wait_ge(S("g_decay"), 2)
                for c in range(NCH - 1):
                    dve.wait_ge(S("state_mm"), c + 1)
                    for p in range(2):
                        for e in range(2):
                            r = slice(64 * e, 64 * e + 64)
                            src = ps[r, BANKS[c % 4], p * 256 + e * P:p * 256 + (e + 1) * P]
                            if c == 0:
                                dve.tensor_copy(state[r, p, 1, :], src).then_inc(S("state"), 1)
                            else:
                                dve.scalar_tensor_tensor(state[r, p, c + 1, :], state[r, p, c, :],
                                                         col[r, p * 8 + c:p * 8 + c + 1], src, ALU.mult, ALU.add
                                                         ).then_inc(S("state"), 1)
                    dve.wait_ge(S("state"), 4 * (c + 1))

                def score(hd):
                    dve.wait_ge(S("gscore_mm"), hd + 1)
                    if hd >= 2:
                        dve.wait_ge(S("go_mm"), hd - 1)
                    dve.copy_predicated(tg[:, hd % 2, :].rearrange("p (t i) -> p t i", t=4),
                                        msk[:].unsqueeze(1).to_broadcast([P, 4, P]),
                                        ps[:, 6 + hd % 2, :].rearrange("p (t i) -> p t i", t=4)
                                        ).then_inc(S("gscore"), 1)

                dve.wait_ge(S("msk_in"), 16)
                score(0)
                for hd in range(4):
                    if hd < 3:
                        score(hd + 1)
                    dve.wait_ge(S("gstd"), hd + 1)
                    dve.reciprocal(rstd[:], std[:]).then_inc(S("grstd"), 1)
                    dve.wait_ge(S("grstd"), hd + 1)
                    o = area(A_O + hd * T)
                    chain(dve.scalar_tensor_tensor(o, ps[:, BANKS[hd], :], vec[:, V_GLAN:V_GLAN + 1], rstd[:],
                                                   ALU.mult, ALU.mult))
                    if hd == 0:
                        dve.wait_ge(S("g_silu"), 1)
                    dve.tensor_tensor(o, o, Pt[9 + hd], ALU.mult).then_inc(S("gla_o"), 1)
                    dve.wait_ge(S("x_hi"), X_LO_GLA + hd + 1)
                    dve.wait_ge(S("gla_o"), hd + 1)
                    dve.tensor_tensor(X[0][:, hd, 1, :], o, X[0][:, hd, 0, :].bitcast(F32), ALU.subtract
                                      ).then_inc(S("x_lo"), 1)

            def s5():
                dve.wait_ge(S("s5c_in"), 16)
                cr, ci = s5ct[:, 0, :, :], s5ct[:, 1, :, :]
                fr = sc5[:, C_FR:C_FR + 16].unsqueeze(2).to_broadcast([P, 16, 32])
                fi = sc5[:, C_FI:C_FI + 16].unsqueeze(2).to_broadcast([P, 16, 32])
                tA = tu[:, 0, :].rearrange("p (j c) -> p j c", j=16)
                tB = tu[:, 1, :].rearrange("p (j c) -> p j c", j=16)
                chain(dve.tensor_tensor(tA, cr, fi, ALU.mult))
                chain(dve.tensor_tensor(tB, ci, fi, ALU.mult))
                chain(dve.tensor_tensor(cr, cr, fr, ALU.mult))
                dve.tensor_tensor(cr, cr, tB, ALU.subtract).then_inc(S("s5_c"), 1)
                chain(dve.tensor_tensor(ci, ci, fr, ALU.mult))
                chain(dve.tensor_tensor(ci, ci, tA, ALU.add))
                dve.tensor_scalar(ci, ci, -1.0, None, ALU.mult).then_inc(S("s5_c"), 1)
                time = area(A_TIME)
                dve.wait_ge(S("time_in"), 16)

                def turns(j):
                    t = A_S5T + (j % 2) * 7 * T
                    a, b = area(t + 2 * T), area(t + 3 * T)
                    ph, pl = sc5[:, C_PH + j:C_PH + j + 1], sc5[:, C_PL + j:C_PL + j + 1]
                    chain(dve.tensor_scalar(a, time, ph, None, ALU.mult))
                    chain(dve.tensor_scalar(b, a, MAGIC, MAGIC, ALU.add, ALU.subtract))
                    chain(dve.tensor_tensor(a, a, b, ALU.subtract))
                    chain(dve.scalar_tensor_tensor(a, time, pl, a, ALU.mult, ALU.add))
                    chain(dve.tensor_scalar(b, a, MAGIC, MAGIC, ALU.add, ALU.subtract))
                    dve.tensor_tensor(a, a, b, ALU.subtract).then_inc(S("s5_turn"), 1)

                def scan_tile(j):
                    t = A_S5T + (j % 2) * 7 * T
                    c, s, zr, zi, t1, t2, t3 = [area(t + i * T) for i in range(7)]
                    b0 = [0, 6][j % 2]
                    vr, vi = ps[:, b0, :], ps[:, b0 + 1, :]
                    mag = sc5[:, C_MAG + j:C_MAG + j + 1].to_broadcast([P, T])
                    dve.wait_ge(S("s5_cos"), j + 1)
                    dve.wait_ge(S("s5_in_mm"), j + 1)
                    if j >= 2:
                        dve.wait_ge(S("s5_out_mm"), j - 1)
                    chain(dve.tensor_tensor(t1, vr, c, ALU.mult))
                    chain(dve.tensor_tensor(t2, vi, s, ALU.mult))
                    chain(dve.tensor_tensor(t1, t1, t2, ALU.add))
                    chain(dve.tensor_tensor(t3, vi, c, ALU.mult))
                    dve.tensor_tensor(t2, vr, s, ALU.mult).then_inc(S("s5_wi"), 1)
                    dve.wait_ge(S("s5_wi"), j + 1)
                    chain(dve.tensor_tensor(t3, t3, t2, ALU.subtract))
                    chain(dve.tensor_tensor_scan(zr, mag, t1, 0.0, ALU.mult, ALU.add))
                    chain(dve.tensor_tensor_scan(zi, mag, t3, 0.0, ALU.mult, ALU.add))
                    chain(dve.tensor_tensor(t1, zr, c, ALU.mult))
                    chain(dve.tensor_tensor(t2, zi, s, ALU.mult))
                    chain(dve.tensor_tensor(t1, t1, t2, ALU.subtract))
                    chain(dve.tensor_tensor(t3, zr, s, ALU.mult))
                    chain(dve.tensor_tensor(t2, zi, c, ALU.mult))
                    dve.tensor_tensor(t3, t3, t2, ALU.add).then_inc(S("s5_xi"), 1)
                    dve.wait_ge(S("s5_xi"), j + 1)

                turns(0)
                for j in range(S5_TILES):
                    if j + 1 < S5_TILES:
                        turns(j + 1)
                    scan_tile(j)
                dve.wait_ge(S("s5_out_mm"), 16)
                for q in range(4):
                    dve.scalar_tensor_tensor(area(A_YG + q * T), Pt[q], vec[:, V_D + q:V_D + q + 1],
                                             ps[:, BANKS[q], :], ALU.mult, ALU.add).then_inc(S("s5_y"), 1)
                for q in range(4):
                    lo_of(X[1][:, q, 1, :], area(A_YG + q * T), X[1][:, q, 0, :], X_LO_Y + q + 1)

            def glu():
                for n in range(4):
                    dve.wait_ge(S("glu_sig"), n + 1)
                    dve.tensor_tensor(area(A_YG + n * T), area(A_YG + n * T), sg[:, n % 2, :], ALU.mult
                                      ).then_inc(S("glu_o"), 1)
                    dve.wait_ge(S("glu_o"), n + 1)
                    lo_of(X[0][:, 4 + n, 1, :], area(A_YG + n * T), X[0][:, 4 + n, 0, :], X_LO_GLU + n + 1)

            def tables():
                dve.wait_ge(S("pos_in"), 16)
                chain(dve.tensor_copy(area(A_SC), area(A_SC + T).bitcast(I32)))
                for i in range(2):
                    x = area(A_TAB + (2 * i + 1) * T)
                    chain(dve.tensor_scalar(x, area(A_SC), vec[:, V_INVA + i:V_INVA + i + 1], None, ALU.mult))
                    reduce_angle(x, area(A_TAB + 2 * i * T))
                    dve.tensor_scalar(x, x, PI_BELOW, -PI_BELOW, ALU.min, ALU.max).then_inc(S("ang"), 1)

            def rope():
                for i, t in enumerate(ROPE_TILES):
                    c = area(A_TAB + (0 if t < 10 else 2) * T)
                    s = area(A_TAB + (1 if t < 10 else 3) * T)
                    dve.wait_ge(S("tab"), 4)
                    dve.wait_ge(S("rope_mm"), i + 1)
                    dve.tensor_tensor(tg[:, i % 2, :], ps[:, BANKS[i % 4], :], s, ALU.mult).then_inc(S("rope_s"), 1)
                    chain(dve.tensor_tensor(Pt[t], Pt[t], c, ALU.mult))
                    dve.wait_ge(S("rope_s"), i + 1)
                    dve.tensor_tensor(Pt[t], Pt[t], tg[:, i % 2, :], ALU.add).then_inc(S("rope_done"), 1)
                dve.wait_ge(S("wi_mm"), 1)
                dve.tensor_scalar(col[:, 32:64].rearrange("p (t i) -> p t i", i=8),
                                  ps[:, 1, :].rearrange("p (t n) -> p t n", n=P)[:, :, 0:8],
                                  (IDX_HEADS * IDX_DIM) ** -0.5, None, ALU.mult).then_inc(S("wi_ready"), 1)
                dve.wait_ge(S("wi_ready"), 1)

            def indexer():
                dve.wait_ge(S("rope_done"), len(ROPE_TILES))
                i = 0
                for qb in range(1, QB):
                    nk = (qb + 1) * P
                    sc = area(A_SC + qb * T)[:, 0:nk]
                    for hd in range(IDX_HEADS):
                        w = col[:, 32 + 8 * qb + hd:33 + 8 * qb + hd]
                        dve.wait_ge(S("relu"), i + 1)
                        if hd == 0:
                            ins = dve.tensor_scalar(sc, tg[:, i % 2, 0:nk], w, None, ALU.mult)
                        else:
                            ins = dve.scalar_tensor_tensor(sc, tg[:, i % 2, 0:nk], w, sc, ALU.mult, ALU.add)
                        ins.then_inc(S("idx_acc"), 1)
                        i += 1
                        dve.wait_ge(S("idx_acc"), i)
                    chain(dve.tensor_tensor(sc[:, qb * P:nk], sc[:, qb * P:nk], cmask, ALU.add))
                chain(dve.tensor_copy(area(A_SC)[:, 0:P], cmask))

            def topk():
                for qb in range(1, QB):
                    nk = (qb + 1) * P
                    sc = area(A_SC + qb * T)[:, 0:nk]
                    for _ in range(TOPK // 8):
                        chain(dve.max(col[:, 20:28], sc))
                        chain(dve.match_replace(sc, col[:, 20:28], sc, TAKEN))
                    chain(dve.tensor_scalar(sc, sc, TAKEN / 2, MASKED, ALU.is_gt, ALU.mult))

            def attention():
                for i, (g, qb) in enumerate(UNITS):
                    nk = (qb + 1) * P
                    pb = A_P if i % 2 == 0 else A_P1
                    pr = area(pb, 4 * T).rearrange("p (j n) -> p j n", j=4)[:, :, 0:nk]
                    bias = area(A_SC + qb * T)[:, 0:nk].unsqueeze(1).to_broadcast([P, 4, nk])
                    dve.wait_ge(S("att_mm"), i + 1)
                    if i >= 2:
                        dve.wait_ge(S("att_tr"), UNIT_TR[i - 2])
                    dve.scalar_tensor_tensor(pr, ps[:, 2:6, 0:nk], ATT_DIM ** -0.5, bias, ALU.mult, ALU.add
                                             ).then_inc(S("att_s"), 1)
                    dve.wait_ge(S("att_s"), i + 1)
                    chain(dve.tensor_reduce(col[:, 0:4], pr, AX.X, ALU.max))
                    dve.tensor_scalar(col[:, 4:8], col[:, 0:4], -1.0, None, ALU.mult).then_inc(S("att_nm"), 1)
                    dve.wait_ge(S("att_e"), 4 * i + 4)
                    chain(dve.reciprocal(col[:, 12:16], col[:, 8:12]))
                    dve.tensor_tensor(pr, pr, col[:, 12:16].unsqueeze(2).to_broadcast([P, 4, nk]), ALU.mult
                                      ).then_inc(S("att_p"), 1)
                    dve.wait_ge(S("x_hi"), X_LO_ATT + i + 1)
                    qc = slice(qb * P, (qb + 1) * P)
                    dve.tensor_tensor(X[0][:, 4 * g:4 * g + 4, 1, qc],
                                      ps[:, i % 2, :].rearrange("p (j q) -> p j q", j=4),
                                      X[0][:, 4 * g:4 * g + 4, 0, qc].bitcast(F32), ALU.subtract
                                      ).then_inc(S("x_lo"), 1)

            def cross(l):
                for hd in range(XA_HEADS):
                    pb = A_XP + (hd % 2) * 2 * T
                    pr = area(pb, 2 * T).rearrange("p (j n) -> p j n", j=4)
                    dve.wait_ge(S("xa_mm"), 4 * l + hd + 1)
                    chain(dve.tensor_reduce(col[:, 0:4], ps[:, 2:4, :].rearrange("p a (b n) -> p (a b) n", b=2),
                                            AX.X, ALU.max))
                    dve.tensor_scalar(col[:, 4:8], col[:, 0:4], -XA_DIM ** -0.5, None, ALU.mult
                                      ).then_inc(S("xa_nm"), 1)
                    dve.wait_ge(S("xa_p"), 4 * l + hd + 1)
                    chain(dve.reciprocal(col[:, 12:16], col[:, 8:12]))
                    dve.tensor_tensor(pr, pr, col[:, 12:16].unsqueeze(2).to_broadcast([P, 4, MEM]), ALU.mult
                                      ).then_inc(S("xa_pn"), 1)
                    for dc in range(2):
                        lo_of(X[0][:, 2 * hd + dc, 1, :], ps[:, 4 + dc, :], X[0][:, 2 * hd + dc, 0, :],
                              X_LO_XA[l] + 2 * hd + dc + 1)

            dve.memset(ones[:], 1.0 / D).then_inc(S("ones_set"), 1)
            dve.memset(epsc[:, 0:1], EPS).then_inc(S("eps_set"), 1)
            dve.memset(epsc[:, 1:2], float(np.pi / 2)).then_inc(S("eps_set"), 1)
            norm(0, 1.0, None, (0,), None)
            ffn(0)
            norm_after_ffn(1, 0)
            projected(EV_AT, EV_TILES, 0)
            rstd_columns(0)
            dve.wait_ge(S("block_done"), EV_V_AT + 4)
            for tt in range(4):
                dve.tensor_scalar(val[:, tt, :], ps[:, BANKS[tt], :], col[:, 16 + tt:17 + tt], None, ALU.mult
                                  ).then_inc(S("gla_v"), 1)
            memory(0)
            s5_constants()
            gla()
            s5()
            glu()
            norm_after_out(2, 0)
            projected(XQ_AT[0], 8, 0)
            cross(0)
            norm_after_out(3, 1)
            ffn(1)
            norm_after_ffn(4, 1)
            ffn(2)
            norm_after_ffn(5, 2)
            projected(OD_AT, OD_TILES, 0)
            rstd_columns(1)
            dve.wait_ge(S("block_done"), OD_V_AT + 2)
            for tt in range(4):
                dve.tensor_scalar(od_val[:, tt, :], ps[:, BANKS[tt], 0:2 * P], col[:, 16 + tt:17 + tt], None,
                                  ALU.mult).then_inc(S("od_v"), 1)
            tables()
            rope()
            indexer()
            memory(1)
            topk()
            attention()
            norm_after_out(6, 2)
            projected(XQ_AT[1], 8, 0)
            cross(1)
            norm_after_out(7, 3)
            ffn(3)
            norm_after_ffn(8, 3)
            for k in range(KC):
                dve.scalar_tensor_tensor(h[:, k, :], h[:, k, :], gain(8, k), rstd[:], ALU.mult, ALU.mult
                                         ).then_inc(S("y_ready"), 1)


def wide(w):
    k, n = w.shape
    return w.reshape(k // P, P, n // P, P).transpose(2, 1, 0, 3)


def rows_of(w, per):
    k, n = w.shape
    return w.reshape(k // P // per, per, P, n).transpose(0, 2, 1, 3)


def lay_out(inp):
    f = np.float32
    a = {k: np.asarray(v) for k, v in inp.items()}

    def chunks(m):
        return np.ascontiguousarray(m.T.reshape(KC, P, -1).transpose(1, 0, 2))

    def cols(v):
        return v.reshape(-1, P).T

    def pad(w):
        return np.concatenate([w, np.zeros((w.shape[0], P - w.shape[1]), f)], axis=1)

    blocks = []

    def add(b):
        blocks.append(b.reshape(b.shape[0], P, BLK))

    def ffn(name, l):
        gate, up = wide(a[f"{name}_w_gate"][l]), wide(a[f"{name}_w_up"][l])
        add(np.stack([gate, up], axis=1).reshape(2 * FC, P, KC, P))
        add(rows_of(a[f"{name}_w_down"][l], 1))

    def memory(l):
        add(wide(a["xa_wk"][l]))
        wv = a["xa_wv"][l]
        for half in range(2):
            add(rows_of(wv[:, half * T:(half + 1) * T], 2))

    ev, od = a["ev_w_in"][0], a["od_w_in"][0]
    q, k, v, r, al, u = np.split(ev, np.cumsum([256, 256, 512, 512, 16]), axis=1)
    ffn("ffn1", 0)
    add(wide(np.concatenate([u, pad(al), q, k, r], axis=1)))
    add(rows_of(v, 2))
    memory(0)
    add(wide(a["s5_w_glu"][0]).reshape(2, 2, P, 4, P).transpose(0, 2, 1, 3, 4))
    add(wide(a["ev_w_out"][0]))
    add(wide(a["xa_wq"][0]))
    add(wide(a["xa_wo"][0]))
    ffn("ffn2", 0)
    ffn("ffn1", 1)
    q, k, v, qi, ki, wi = np.split(od, np.cumsum([1024, 256, 256, 512, 64]), axis=1)
    add(wide(np.concatenate([q, k, qi, ki, ki, pad(wi)], axis=1)))
    add(rows_of(v, 4))
    memory(1)
    add(wide(a["od_w_out"][0]))
    add(wide(a["xa_wq"][1]))
    add(wide(a["xa_wo"][1]))
    ffn("ffn2", 1)
    stream = np.concatenate(blocks, axis=0)
    assert stream.shape == (N_BLOCKS, P, BLK)

    norms = [a["ffn1_norm"][0], a["mix_norm"][0], a["xa_norm"][0], a["ffn2_norm"][0],
             a["ffn1_norm"][1], a["mix_norm"][1], a["xa_norm"][1], a["ffn2_norm"][1], a["final_norm"]]
    lane = np.arange(P)
    inv_a = (np.float32(10000.0) ** (-(2 * (lane % 64)).astype(f) / np.float32(128)))[:, None].astype(f)
    inv_i = (np.float32(10000.0) ** (-(2 * (lane % 32)).astype(f) / np.float32(64)))[:, None].astype(f)
    vecs = np.concatenate(
        [cols(n) for n in norms] + [cols(a["mem_norm"]), cols(a["gla_norm"][0]), cols(a["gla_b_alpha"][0]),
         cols(a["s5_D"][0].reshape(-1)), cols(a["s5_b_glu"][0]),
         cols(a["s5_lambda_re"][0].reshape(-1)), cols(a["s5_lambda_im"][0].reshape(-1)),
         cols(np.repeat(a["s5_log_dt"][0], 64)), inv_a, inv_i], axis=1)

    s5b = np.zeros((P, 2, 4, P), f)
    s5c = np.zeros((P, 2, S5_TILES, 32), f)
    for g in range(32):
        j, e = g // 2, g % 2
        p0 = 32 * (j % 4) + 16 * e
        for c, (b, cc) in enumerate((("s5_B_re", "s5_C_re"), ("s5_B_im", "s5_C_im"))):
            s5b[p0:p0 + 16, c, j // 4, 64 * e:64 * e + 64] = a[b][0, g].T
            s5c[64 * e:64 * e + 64, c, j, 16 * e:16 * e + 16] = a[cc][0, g].T

    mats = np.zeros((P, 4, P), f)
    mats[:, 0] = np.eye(P)
    for i, half in ((1, 64), (2, 32)):
        for m in range(P):
            low = m % (2 * half) < half
            mats[m + half if low else m - half, i, m] = -1.0 if low else 1.0
    mats[:, 3] = np.where(lane[None, :] <= lane[:, None], 0.0, MASKED)
    mask = ((lane[:, None] // 64 == lane[None, :] // 64) & (lane[:, None] <= lane[None, :])).astype(np.int32)
    rows = np.stack([np.arange(T), np.arange(T) % GLA_CHUNK != 0]).astype(f)
    return {
        "xT": chunks(a["x"][0]), "memT": chunks(a["mem"][0]), "pos": a["positions"],
        "vecs": vecs, "w_alpha": a["gla_w_alpha"][0], "s5b": s5b, "s5c": s5c, "mats": mats,
        "mask": mask, "rows": rows, "stream": stream,
    }


def kernel(**inputs):
    import concourse.bacc as bacc
    from concourse.bass_utils import run_bass_kernel_spmd as run

    nc = bacc.Bacc("TRN2", target_bir_lowering=False, num_devices=1)
    arrays, args = {}, []
    for name, a in lay_out(inputs).items():
        a = np.ascontiguousarray(a)
        arrays[f"in_{name}"] = a
        args.append(nc.dram_tensor(f"in_{name}", a.shape, mybir.dt.from_np(a.dtype), kind="ExternalInput").ap())
    args.append(nc.dram_tensor("out_0", (P, KC, T), F32, kind="ExternalOutput").ap())
    build_trunk(nc, *args)
    r = run(nc, [arrays], core_ids=[0])
    got = r.results[0]["out_0"]
    return np.ascontiguousarray(got.transpose(2, 1, 0).reshape(1, T, D))
```

```python
from contextlib import ExitStack

import numpy as np

import concourse.bass as bass
from concourse import mybir

F32 = mybir.dt.float32
F32R = mybir.dt.float32r
I32 = mybir.dt.int32
ALU = mybir.AluOpType
ACT = mybir.ActivationFunctionType
AX = mybir.AxisListType

P = 128
T = 512
D = 1024
KC = D // P
MEM = 256
FF = 2816
FC = FF // P
EPS = 1e-6
BLK = 1024
HALF = BLK // 2
MAGIC = 12582912.0
TWO_PI_BELOW = 6.2831845
PI_BELOW = 3.1415925
TWO_PI_1, TWO_PI_2, TWO_PI_3 = 6.28125, 0.0019350051879882812, 3.0199159819e-07

GLA_HEADS, GLA_DK, GLA_DV, GLA_CHUNK, GLA_TAU = 4, 64, 128, 64, 16.0
NCH = T // GLA_CHUNK
S5_TILES = 16
QB = T // P
TOPK = 128
IDX_HEADS, IDX_DIM = 8, 64
ATT_HEADS, ATT_DIM = 8, 128
XA_HEADS, XA_DIM = 4, 256
MASKED = -1.0e30
TAKEN = -3.0e38

XS_BANKS = [0, 6]
XO_BANKS = [(2, 4)] * 3 + [(6, 7)]

FFN_BLOCKS = 3 * FC
FFN_AT = [0, 125, 191, 315]
EV_AT, EV_TILES = 66, 13
EV_V_AT = 79
GLU_AT = 86


def kv_block(l, t):
    return 275 + t if l else 83 + t + (2 if t >= 3 else 0)


OUT_AT = [101, 117, 291, 307]
XQ_AT = [109, 299]
OD_AT, OD_TILES = 257, 16
OD_V_AT = 273
N_BLOCKS = 381

BANKS = [2, 4, 3, 5]
DOWN_BANKS = [0, 2, 4, 3, 5, 6, 7, 1]
SSQ_BANK = 0
GLU_BANKS = [0, 1, 2, 4]
KV_BANKS = [3, 5]

NORM_TO = [0, 1, 1, 1, 0, 1, 1, 1]
FFN_NORM = [0, 3, 4, 7]

OUT_NORM = [2, 3, 6, 7]
XQ_BASE, OD_BASE = [13, 37], 21

_SPLITS = [("n0", 8), ("h0", FC), ("n1", 8), ("y", 4), ("gla", 4), ("glu", 4), ("n2", 8), ("xa0", 8),
           ("n3", 8), ("h1", FC), ("n4", 8), ("h2", FC), ("n5", 8), ("att", 8), ("n6", 8), ("xa1", 8),
           ("n7", 8), ("h3", FC)]
BEFORE = {name: sum(n for _, n in _SPLITS[:i]) for i, (name, _) in enumerate(_SPLITS)}
X_LO_NORM = [BEFORE[f"n{i}"] for i in range(8)]
X_LO_HID = [BEFORE[f"h{i}"] for i in range(4)]
X_LO_GLA, X_LO_Y, X_LO_GLU, X_LO_ATT = (BEFORE[i] for i in ("gla", "y", "glu", "att"))
X_LO_XA = [BEFORE["xa0"], BEFORE["xa1"]]

ROPE_TILES = range(15)
UNITS = [(g, qb) for g in range(2) for qb in range(QB)]
UNIT_TR = [sum(qb + 1 for _, qb in UNITS[:i + 1]) for i in range(len(UNITS))]

V_GAIN = 0
V_MEMG = 72
V_GLAN = 80
V_BALPHA = 81
V_D = 83
V_BGLU = 87
V_LRE, V_LIM, V_LDT = 91, 107, 123
V_INVA, V_INVI = 139, 140
NV = 141
C_MAG, C_PH, C_PL, C_FR, C_FI = [16 * i for i in range(5)]

A_TIME = FC * T
A_MEM = 27 * T
ARENA = 31 * T
A_V = EV_TILES * T
A_S5B = A_V + 4 * T
A_S5C = A_S5B + 2 * T
A_S5T = A_S5C + 2 * T
A_S5X = A_S5T + 6 * T
A_BC = A_V + 4 * T
A_KINV = A_BC + 2 * T
A_KENDT = A_KINV + 2 * T
A_S = A_KENDT + 2 * T
A_O = A_S + 4 * T
A_ODV = OD_TILES * T
A_SC = A_ODV + 2 * T
A_TAB = FC * T
A_POS = A_TAB + 4 * T
A_P = A_TAB + 4 * T
A_P1 = A_TAB
A_PT = 10 * T
A_XP = 8 * T
A_XPT = A_XP + 4 * T


def build_trunk(nc, xT, memT, pos, vecs, w_alpha, s5b, s5c, mats, mask, rows, stream, out):
    with ExitStack() as ctx:
        def sb(name, shape, dt=F32):
            return ctx.enter_context(nc.sbuf_tensor(name, shape, dt))

        sems = {}

        def S(name):
            if name not in sems:
                sems[name] = ctx.enter_context(nc.semaphore(name))
            return sems[name]

        ps = ctx.enter_context(nc.psum_tensor("ps", [P, 8, T], F32))
        h = sb("h", [P, KC, T])
        X = [sb(f"x{i}", [P, KC, 2, T], F32R) for i in range(2)]
        W = sb("w_split", [P, 2, 2, BLK], F32R)
        raw = sb("w_raw", [P, 2, BLK])
        kv = sb("kv", [P, 8 * T])
        ar = sb("arena", [P, ARENA])
        tg = sb("tg", [P, 2, T])
        tu = sb("tu", [P, 2, T])
        sg = sb("sg", [P, 2, T])
        sq = sb("sq", [P, 2, T])
        rstd = sb("rstd", [P, T])
        std = sb("std", [P, T])
        vec = sb("vec", [P, NV])
        mat = sb("mat", [P, 4, P])
        msk = sb("msk", [P, P], I32)
        ones = sb("ones", [P, P])
        sc5 = sb("sc5", [P, 80])
        tiny = sb("tiny", [P, 12, 16])
        col = sb("col", [P, 64])
        epsc = sb("epsc", [P, 2])

        s5_tables = nc.dram_tensor("s5_tables", (S5_TILES, P, 2 * T), F32, kind="Internal").ap()
        ident = mat[:, 0, :]
        cmask = mat[:, 3, :]
        gate = sb("gate", [P, 2])
        tiny_i = sb("tiny_i", [P, 16], I32)
        Pt = [ar[:, i * T:(i + 1) * T] for i in range(16)]
        KT = kv[:, 0:4 * T].rearrange("p (n m) -> p n m", m=MEM)
        VM = kv[:, 4 * T:8 * T].rearrange("p (t d) -> p t d", t=2)
        hid = ar[:, 0:FC * T].rearrange("p (k t) -> p k t", t=T)
        memX = X[0][:, 4:8, :, :].rearrange("p a b t -> p (a b t)").rearrange(
            "p (k s m) -> p k s m", k=KC, s=2)

        def area(at, n=T):
            return ar[:, at:at + n]

        val = area(A_V, 4 * T).rearrange("p (t d) -> p t d", t=4)
        kend_t = area(A_KENDT, 2 * T).rearrange("p (t q f) -> p t q f", t=4, q=2)
        state = area(A_S, 4 * T).rearrange("p (q c e) -> p q c e", q=2, c=NCH)
        chunk_mask = area(A_S)
        wal = area(A_S + T, 2 * P)[0:16, :]
        s5bt = area(A_S5B, 2 * T).rearrange("p (c q s) -> p c q s", c=2, q=4)
        s5ct = area(A_S5C, 2 * T).rearrange("p (c j o) -> p c j o", c=2, j=16)
        od_val = area(A_ODV, 2 * T).rearrange("p (t d) -> p t d", t=4)

        def gain(n, k):
            return vec[:, V_GAIN + 8 * n + k:V_GAIN + 8 * n + k + 1]

        block = ctx.enter_context(nc.Block())

        @block.sync
        def _(sp):
            for s in range(2):
                sp.dma_start(raw[:, s, 0:HALF], stream[s][:, 0:HALF]).then_inc(S(f"raw{s}_half"), 16)
                if s == 0:
                    sp.dma_start(h[:, 0:2, :], xT[:, 0:2, :]).then_inc(S("x_in0"), 16)
                    sp.dma_start(vec[:], vecs).then_inc(S("vec_in"), 16)
            for s in range(2):
                sp.dma_start(raw[:, s, HALF:], stream[s][:, HALF:]).then_inc(S(f"raw{s}_full"), 16)
            sp.dma_start(h[:, 2:8, :], xT[:, 2:8, :]).then_inc(S("x_in1"), 16)
            sp.dma_start(mat[:], mats).then_inc(S("mat_in"), 16)
            sp.dma_start(msk[:], mask).then_inc(S("msk_in"), 16)
            sp.dma_start(area(A_MEM, 4 * T).rearrange("p (k m) -> p k m", m=MEM), memT).then_inc(S("mem_in0"), 16)
            sp.dma_start(area(A_TIME), rows[0:1, :].to_broadcast([P, T])).then_inc(S("time_in"), 16)
            with sp.Fori(1, N_BLOCKS // 2) as i:
                for s in range(2):
                    sp.wait_ge(S("raw_used"), i * 2 + (s - 1))
                    sp.dma_start(raw[:, s, :], stream[bass.ds(i * 2 + s, 1)].rearrange("a p n -> p (a n)")
                                 ).then_inc(S(f"raw{s}_full"), 16)
            sp.wait_ge(S("raw_used"), N_BLOCKS - 2)
            sp.dma_start(raw[:, 0, :], stream[N_BLOCKS - 1]).then_inc(S("raw0_full"), 16)

        @block.gpsimd
        def _(pool):
            def split(s, b, half, loaded, free):
                c = slice(half * HALF, (half + 1) * HALF)
                if loaded is not None:
                    pool.wait_ge(*loaded)
                if free is not None:
                    pool.wait_ge(free, b - 1)
                    pool.tensor_tensor(gate[:, 0:1], gate[:, 1:2], gate[:, 1:2], ALU.add)
                pool.tensor_scalar(W[:, s, 0, c], raw[:, s, c], 1.0, 0.0, ALU.mult, ALU.add
                                   ).then_inc(S("w_hi"), 1)
                pool.wait_ge(S("w_hi"), b * 2 + (half + 1))
                pool.tensor_tensor(W[:, s, 1, c], raw[:, s, c], W[:, s, 0, c].bitcast(F32), ALU.subtract
                                   ).then_inc(S("raw_used") if half else S("half_split"), 1)

            def split_block(s, b, full):
                split(s, b, 0, (S(f"raw{s}_full"), full), S("half_done"))
                split(s, b, 1, None, S("block_done"))

            pool.memset(gate[:], 0.0).then_inc(S("gate_set"), 1)
            pool.wait_ge(S("gate_set"), 1)
            for s in range(2):
                pool.wait_ge(S(f"raw{s}_half"), 16)
                pool.tensor_scalar(W[:, s, 0, 0:HALF], raw[:, s, 0:HALF], 1.0, 0.0, ALU.mult, ALU.add
                                   ).then_inc(S("w_hi"), 1)
                pool.wait_ge(S("w_hi"), s + 1)
                pool.tensor_tensor(W[:, s, 1, 0:HALF], raw[:, s, 0:HALF], W[:, s, 0, 0:HALF].bitcast(F32),
                                   ALU.subtract).then_inc(S("half_split"), 1)
            for s in range(2):
                pool.wait_ge(S(f"raw{s}_full"), 16)
                pool.tensor_scalar(W[:, s, 0, HALF:], raw[:, s, HALF:], 1.0, 0.0, ALU.mult, ALU.add
                                   ).then_inc(S("w_hi"), 1)
                pool.wait_ge(S("w_hi"), s + 3)
                pool.tensor_tensor(W[:, s, 1, HALF:], raw[:, s, HALF:], W[:, s, 0, HALF:].bitcast(F32),
                                   ALU.subtract).then_inc(S("raw_used"), 1)
            with pool.Fori(1, N_BLOCKS // 2) as i:
                for s in range(2):
                    split_block(s, i * 2 + s, i * 16 + 16)
            split_block(0, N_BLOCKS - 1, 16 * (N_BLOCKS // 2 + 1))

        split_ready = S("raw_used")

        @block.tensor
        def _(pe):
            def mm3(dst, wh, wl, xh, xl, start, stop):
                pe.matmul(dst, wh, xh, start=start, stop=False)
                pe.matmul(dst, wh, xl, start=False, stop=False)
                return pe.matmul(dst, wl, xh, start=False, stop=stop)

            def tile_k(bank, slot, x, k, start, stop):
                c = slice(k * P, (k + 1) * P)
                return mm3(ps[:, bank, :], W[:, slot, 0, c], W[:, slot, 1, c],
                           X[x][:, k, 0, :], X[x][:, k, 1, :], start, stop)

            def ssq(n, k, cols=T):
                pe.wait_ge(S("sq_ready"), 8 * n + k + 1)
                if k == 0:
                    pe.wait_ge(*((S("ones_set"), 1) if n == 0 else (S("std_ready"), n)))
                pe.matmul(ps[:, SSQ_BANK, :], ones[:], sq[:, k % 2, :], start=(k == 0), stop=(k == 7)
                          ).then_inc(S("ssq_done"), 1)

            def tile(b, t, x, free=None):
                slot, bank = t
                pe.wait_ge(S("half_split"), b + 1)
                if free is not None:
                    pe.wait_ge(*free)
                for k in range(KC):
                    if k == KC // 2:
                        m.then_inc(S("half_done"), 1)
                        pe.wait_ge(split_ready, b + 1)
                    m = tile_k(bank, slot, x, k, k == 0, k == KC - 1)
                m.then_inc(S("block_done"), 1)

            def project(n, at, nt, x, free_sem, free_base, per, waits0, waits1, between=None):
                pe.wait_ge(S("half_split"), at + 2)
                for s, v in waits0:
                    pe.wait_ge(s, v)
                for k in range(KC):
                    if k == KC // 2:
                        pe.wait_ge(split_ready, at + 2)
                    pe.wait_ge(S("x_lo"), X_LO_NORM[n] + k + 1)
                    for t in range(min(2, nt)):
                        m = tile_k(BANKS[t], (at + t) % 2, x, k, k == 0, k == KC - 1)
                        if k == KC // 2 - 1:
                            m.then_inc(S("half_done"), 1)
                        if k == KC - 1:
                            m.then_inc(S("block_done"), 1)
                    if n in OUT_NORM and k < 2:
                        ssq(n, 6 + k)
                    elif n not in OUT_NORM and k >= 1:
                        ssq(n, k - 1)
                if n not in OUT_NORM:
                    ssq(n, KC - 1)
                for s, v in waits1:
                    pe.wait_ge(s, v)
                for t in (2, 3):
                    tile(at + t, ((at + t) % 2, BANKS[t]), x)
                full, first = (nt - 4) // 4, 1
                if between is not None:
                    for t in range(4, 8):
                        tile(at + t, ((at + t) % 2, BANKS[t % 4]), x, (free_sem, free_base + t // 2 - 1))
                    between()
                    first = 2
                if full >= 1:
                    with pe.Fori(first, 1 + full) as i:
                        for t in range(4):
                            need = (i * 2 + (t // 2 - 1) if per == 2 else i * 4 + (t - 3)) + free_base
                            tile(i * 4 + (at + t), ((at + t) % 2, BANKS[t]), x, (free_sem, need))
                for t in range(4 + 4 * full, nt):
                    tile(at + t, ((at + t) % 2, BANKS[t % 4]), x, (free_sem, free_base + t - 3))

            def ffn(f):
                n, at = FFN_NORM[f], FFN_AT[f]
                x, xo = NORM_TO[n], 1 - NORM_TO[n]
                w0 = [(S("h_ready"), 8 * (n - 1) + (3 if f == 2 else 6))] if n else []
                w1 = [(S("h_ready"), 8 * n)] if n else []
                project(n, at, 2 * FC, x, S("hid_done"), FC * f, 2, w0, w1,
                        (lambda: memory_norm(f // 2)) if f % 2 == 0 else None)
                dn = at + 2 * FC

                def down_k(slot, d4, b, nn, start, stop):
                    c = slice(nn * P, (nn + 1) * P)
                    ch = [6, 7, 4, 5][d4]
                    return mm3(ps[:, DOWN_BANKS[nn], :], W[:, slot, 0, c], W[:, slot, 1, c],
                               X[xo][:, ch, 0, :], X[xo][:, ch, 1, :], start, stop)

                def down(b, slot, d4, lo, first):
                    pe.wait_ge(S("half_split"), b + 1)
                    pe.wait_ge(S("x_lo"), lo)
                    order = [5, 6, 7, 0, 1, 2, 3, 4] if first else list(range(8))
                    for nn in order:
                        if nn == (5 if first else 4):
                            pe.wait_ge(split_ready, b + 1)
                        if first and nn == 0:
                            pe.wait_ge(S("std_ready"), n + 1)
                        if first and nn == 1:
                            pe.wait_ge(S("hid_done"), FC * (f + 1))
                        m = down_k(slot, d4, b, nn, first, False)
                        if nn == 3:
                            m.then_inc(S("half_done"), 1)
                    m.then_inc(S("block_done"), 1)

                lo0 = X_LO_HID[f]
                for d in range(4):
                    down(dn + d, (dn + d) % 2, d, lo0 + d + 1, d == 0)
                with pe.Fori(1, 5) as i:
                    for s in range(4):
                        down(i * 4 + (dn + s), (dn + s) % 2, s, i * 4 + (lo0 + s + 1), False)
                pe.wait_ge(S("half_split"), dn + FC)
                pe.wait_ge(S("x_lo"), lo0 + FC)
                for nn in range(8):
                    if nn == 4:
                        pe.wait_ge(split_ready, dn + FC)
                    m = down_k((dn + 20) % 2, 0, 0, nn, False, False)
                    if nn in (3, 4):
                        m.then_inc(S("half_done"), 1)
                    if nn == 7:
                        m.then_inc(S("block_done"), 1)
                    m = down_k((dn + 21) % 2, 1, 0, nn, False, True)
                    m.then_inc(S("down_out") if nn < 7 else S("block_done"), 1)

            def out_proj(o, lo, n_prev_free):
                at, n = OUT_AT[o], OUT_NORM[o]
                for s, v in n_prev_free:
                    pe.wait_ge(s, v)
                for t in range(8):
                    pe.wait_ge(S("half_split"), at + t + 1)
                    if t >= 4:
                        pe.wait_ge(S("h_ready"), 8 * (n - 1) + t - 3)
                    for k in range(KC):
                        if k == KC // 2:
                            m.then_inc(S("half_done"), 1)
                            pe.wait_ge(split_ready, at + t + 1)
                        if t == 0:
                            pe.wait_ge(S("x_lo"), lo[k])
                        m = tile_k(BANKS[t % 4], (at + t) % 2, 0, k, k == 0, k == KC - 1)
                    m.then_inc(S("block_done"), 1)
                    if t >= 2:
                        ssq(n, t - 2)

            def memory_norm(l):
                for k in range(KC):
                    pe.wait_ge(S("msq_ready"), 8 * l + k + 1)
                    pe.matmul(ps[:, 1, 0:MEM], ones[:], sq[:, k % 2, 0:MEM], start=(k == 0), stop=(k == 7)
                              ).then_inc(S("mssq_done"), 1)

            def kv_tile(l, t, banks):
                b = kv_block(l, t)
                if t == 0:
                    pe.wait_ge(S("mem_lo"), 8 * l + 8)
                pe.wait_ge(S("half_split"), b + 1)
                if t < 8:
                    if t >= 2:
                        pe.wait_ge(S("kv_out"), 12 * l + t - 1)
                    for k in range(KC):
                        if k == KC // 2:
                            m.then_inc(S("half_done"), 1)
                            pe.wait_ge(split_ready, b + 1)
                        c = slice(k * P, (k + 1) * P)
                        m = mm3(ps[:, banks[t % 2], 0:MEM], W[:, b % 2, 0, c], W[:, b % 2, 1, c],
                                memX[:, k, 0, :], memX[:, k, 1, :], k == 0, k == 7)
                else:
                    half, q = (t - 8) // 4, t % 4
                    if q == 0:
                        pe.wait_ge(S("kv_out"), 12 * l + 8 + 2 * half)
                    for kk in range(2):
                        if kk == 1:
                            m.then_inc(S("half_done"), 1)
                            pe.wait_ge(split_ready, b + 1)
                        k = 2 * q + kk
                        for mt in range(2):
                            mc = slice(mt * P, (mt + 1) * P)
                            wc = slice(kk * T, (kk + 1) * T)
                            m = mm3(ps[:, banks[mt], :], memX[:, k, 0, mc], memX[:, k, 1, mc],
                                    W[:, b % 2, 0, wc], W[:, b % 2, 1, wc], k == 0, k == 7)
                m.then_inc(S("block_done"), 1)

            def values(at, q, width):
                per = BLK // width
                b = at + q
                pe.wait_ge(S("half_split"), b + 1)
                for kk in range(per):
                    if kk == per // 2:
                        m.then_inc(S("half_done"), 1)
                        pe.wait_ge(split_ready, b + 1)
                    k = q * per + kk
                    for tt in range(4):
                        tc = slice(tt * P, (tt + 1) * P)
                        wc = slice(kk * width, (kk + 1) * width)
                        m = mm3(ps[:, BANKS[tt], 0:width], X[1][:, k, 0, tc], X[1][:, k, 1, tc],
                                W[:, b % 2, 0, wc], W[:, b % 2, 1, wc], k == 0, k == 7)
                m.then_inc(S("block_done"), 1)

            def rstd_columns(l):
                pe.wait_ge(S("rstd_ready"), [2, 6][l])
                if l == 0:
                    pe.wait_ge(S("mat_in"), 16)
                for tt in range(4):
                    m = pe.transpose(ps[:, 1, tt * P:(tt + 1) * P], rstd[:, tt * P:(tt + 1) * P], ident)
                m.then_inc(S("rcol_mm"), 1)

            def gla_alpha():
                pe.wait_ge(S("proj_out"), 5)
                pe.wait_ge(S("wal_in"), 16)
                pe.wait_ge(S("s5_y"), 4)
                for p in range(2):
                    m = pe.matmul(ps[:, 6 + p, :], wal[:, p * P:(p + 1) * P], Pt[4][0:16, :],
                                  start=True, stop=True)
                m.then_inc(S("alpha_mm"), 1)

            def gla(fill):
                fill(3)
                pe.wait_ge(S("kend"), 2)
                pe.wait_ge(S("zb_ready"), 2)
                for p in range(2):
                    for tt in range(4):
                        m = pe.transpose(ps[:, 6 + p, tt * P:(tt + 1) * P],
                                         Pt[7 + p][:, tt * P:(tt + 1) * P], ident)
                m.then_inc(S("kend_tr"), 1)
                pe.wait_ge(S("glu_sig"), 4)
                pe.wait_ge(S("kend_t"), 2)
                pe.wait_ge(S("gla_v"), 4)
                for c in range(NCH - 1):
                    if c >= 2:
                        pe.wait_ge(S("state"), 4 * (c - 1))
                    r = slice(64 * (c % 2), 64 * (c % 2) + 64)
                    for p in range(2):
                        m = pe.matmul(ps[:, BANKS[c % 2], p * 256:(p + 1) * 256],
                                      kend_t[r, c // 2, p, :], val[r, c // 2, p * 256:(p + 1) * 256],
                                      start=True, stop=True)
                    m.then_inc(S("state_mm"), 1)
                    if c in (2, 5):
                        fill(1)
                pe.wait_ge(S("qdec"), 2)
                pe.wait_ge(S("kinv"), 2)

                def scores(hd):
                    p, r = hd // 2, slice(64 * (hd % 2), 64 * (hd % 2) + 64)
                    if hd >= 2:
                        pe.wait_ge(S("gscore"), hd - 1)
                    for tt in range(4):
                        tc = slice(tt * P, (tt + 1) * P)
                        m = pe.matmul(ps[:, 6 + hd % 2, tc], area(A_KINV + p * T)[r, tc], Pt[5 + p][r, tc],
                                      start=True, stop=True)
                    m.then_inc(S("gscore_mm"), 1)

                scores(0)
                fill(1)
                pe.wait_ge(S("state"), 4 * (NCH - 1))
                for hd in range(4):
                    if hd < 3:
                        scores(hd + 1)
                    if hd >= 2:
                        pe.wait_ge(S("gla_o"), hd - 1)
                    p, r = hd // 2, slice(64 * (hd % 2), 64 * (hd % 2) + 64)
                    pe.wait_ge(S("gscore"), hd + 1)
                    for tt in range(4):
                        dst = ps[:, BANKS[hd % 2], tt * P:(tt + 1) * P]
                        pe.matmul(dst, val[:, tt, hd * P:(hd + 1) * P], tg[:, hd % 2, tt * P:(tt + 1) * P],
                                  start=True, stop=False)
                        for c in (2 * tt, 2 * tt + 1):
                            if c == 0:
                                continue
                            cc = slice(c * 64, (c + 1) * 64)
                            m = pe.matmul(ps[:, BANKS[hd % 2], cc], state[r, p, c, :], Pt[5 + p][r, cc],
                                          start=False, stop=(c % 2 == 1))
                    m.then_inc(S("go_mm"), 1)
                    pe.wait_ge(S("gsq"), hd + 1)
                    if hd >= 2:
                        pe.wait_ge(S("gstd"), hd - 1)
                    pe.matmul(ps[:, hd % 2, :], ones[:], sq[:, hd % 2, :], start=True, stop=True
                              ).then_inc(S("gms_mm"), 1)
                    fill(2)

            def s5(fill):
                def inputs(j):
                    q, r = j // 4, slice(32 * (j % 4), 32 * (j % 4) + 32)
                    if j == 0:
                        pe.wait_ge(S("s5b_in"), 16)
                        pe.wait_ge(S("rcol_ready"), 1)
                    if j % 4 == 0:
                        pe.wait_ge(S("proj_out"), q + 1)
                    if j >= 1:
                        pe.wait_ge(S("s5_read"), j)
                    for c in range(2):
                        m = pe.matmul(ps[:, c, :], s5bt[r, c, q, :], Pt[q][r, :], start=True, stop=True)
                    m.then_inc(S("s5_in_mm"), 1)

                def outputs(j):
                    q, r = j // 4, slice(32 * (j % 4), 32 * (j % 4) + 32)
                    if j == 0:
                        pe.wait_ge(S("s5_c"), 2)
                    if j % 4 == 0 and q >= 2:
                        pe.wait_ge(S("s5_y"), q - 1)
                    pe.wait_ge(S("s5_xi"), j + 1)
                    x = A_S5X + (j % 2) * 2 * T
                    pe.matmul(ps[r, 6 + q % 2, :], s5ct[:, 0, j, :], area(x), start=True, stop=False)
                    pe.matmul(ps[r, 6 + q % 2, :], s5ct[:, 1, j, :], area(x + T), start=False, stop=True
                              ).then_inc(S("s5_out_mm"), 1)

                inputs(0)
                for j in range(S5_TILES):
                    fill(j)
                    if j + 1 < S5_TILES:
                        inputs(j + 1)
                    outputs(j)

            def glu():
                for n in range(4):
                    pe.wait_ge(S("half_split") if n % 2 == 0 else split_ready, GLU_AT + n // 2 + 1)
                    for k in range(4):
                        if n == 0:
                            pe.wait_ge(S("x_lo"), X_LO_Y + k + 1)
                        b = GLU_AT + n // 2
                        c = slice(((n % 2) * 4 + k) * P, ((n % 2) * 4 + k + 1) * P)
                        m = mm3(ps[:, GLU_BANKS[n], :], W[:, b % 2, 0, c], W[:, b % 2, 1, c],
                                X[1][:, k, 0, :], X[1][:, k, 1, :], k == 0, k == 3)
                    m.then_inc(S("half_done") if n % 2 == 0 else S("block_done"), 1)

            def rope(t):
                pe.wait_ge(S("proj_out"), OD_BASE + t + 1)
                if t == 0:
                    pe.wait_ge(S("kv_out"), 12)
                if t >= 2:
                    pe.wait_ge(S("rope_s"), t - 1)
                pe.matmul(ps[:, 6 + t % 2, :], mat[:, 1 if t < 10 else 2, :], Pt[t], start=True, stop=True
                          ).then_inc(S("rope_mm"), 1)

            def indexer_weights():
                pe.wait_ge(S("rcol_ready"), 2)
                pe.wait_ge(S("proj_out"), OD_BASE + 16)
                for tt in range(4):
                    m = pe.transpose(ps[:, 1, tt * P:(tt + 1) * P], Pt[15][:, tt * P:(tt + 1) * P], ident)
                m.then_inc(S("wi_mm"), 1)

            def indexer(fill):
                pe.wait_ge(S("rope_done"), len(ROPE_TILES))
                pe.wait_ge(S("od_v"), 4)
                i = 0
                for qb in range(1, QB):
                    nk = (qb + 1) * P
                    for hd in range(IDX_HEADS):
                        r = slice(64 * (hd % 2), 64 * (hd % 2) + 64)
                        if i >= 4:
                            pe.wait_ge(S("relu"), i - 3)
                        pe.matmul(ps[:, BANKS[i % 4], 0:nk], Pt[10 + hd // 2][r, qb * P:(qb + 1) * P],
                                  Pt[14][r, 0:nk], start=True, stop=True).then_inc(S("logit_mm"), 1)
                        i += 1
                        if hd == 3:
                            fill(1)

            def attention():
                def scores(i):
                    g, qb = UNITS[i]
                    nk = (qb + 1) * P
                    if i == 0:
                        pe.wait_ge(S("relu"), 24)
                    else:
                        pe.wait_ge(S("att_s"), i)
                    for j in range(4):
                        m = pe.matmul(ps[:, 2 + j, 0:nk], Pt[4 * g + j][:, qb * P:(qb + 1) * P],
                                      Pt[8 + g][:, 0:nk], start=True, stop=True)
                    m.then_inc(S("att_mm"), 1)

                nt = 0
                scores(0)
                scores(1)
                for i, (g, qb) in enumerate(UNITS):
                    pe.wait_ge(S("att_p"), i + 1)
                    if i == 0:
                        pe.wait_ge(S("kv_out"), 24)
                    pb = A_P if i % 2 == 0 else A_P1
                    for kc in range(qb + 1):
                        if nt >= 2:
                            pe.wait_ge(S("att_t"), nt - 1)
                        for j in range(4):
                            m = pe.transpose(ps[:, 6 + nt % 2, j * P:(j + 1) * P],
                                             area(pb + j * T)[:, kc * P:(kc + 1) * P], ident)
                        m.then_inc(S("att_tr"), 1)
                        nt += 1
                    if i + 2 < len(UNITS):
                        scores(i + 2)
                    if i >= 2:
                        pe.wait_ge(S("x_lo"), X_LO_ATT + i - 1)
                    pe.wait_ge(S("att_t"), nt)
                    for kc in range(qb + 1):
                        m = pe.matmul(ps[:, i % 2, :], od_val[:, kc, g * P:(g + 1) * P],
                                      area(A_PT + kc * T), start=(kc == 0), stop=(kc == qb))
                    m.then_inc(S("att_o"), 1)

            def cross(l, n, waits0, waits1):
                base, at = XQ_BASE[l], XQ_AT[l]

                def scores(hd):
                    pe.wait_ge(S("proj_out"), base + 2 * hd + 2)
                    if hd == 0:
                        pe.wait_ge(S("kv_out"), 12 * (l + 1))
                        pe.wait_ge(S("std_ready"), n + 1)
                    if hd >= 2:
                        pe.wait_ge(S("xa_p"), 4 * l + hd - 1)
                    for qb in range(QB):
                        for c in range(2):
                            m = pe.matmul(ps[:, XS_BANKS[hd % 2] + qb // 2, (qb % 2) * MEM:(qb % 2 + 1) * MEM],
                                          Pt[2 * hd + c][:, qb * P:(qb + 1) * P], KT[:, 2 * hd + c, :],
                                          start=(c == 0), stop=(c == 1))
                    m.then_inc(S("xa_mm"), 1)

                def turn(hd):
                    pe.wait_ge(S("xa_pn"), 4 * l + hd + 1)
                    if hd >= 1:
                        pe.wait_ge(S("xa_t"), 8 * l + 2 * hd)
                    pb = A_XP + (hd % 2) * 2 * T
                    for mc in range(2):
                        for qb in range(QB):
                            m = pe.transpose(ps[:, BANKS[2 + mc], qb * P:(qb + 1) * P],
                                             area(pb + qb * MEM)[:, mc * P:(mc + 1) * P], ident)
                        m.then_inc(S("xa_tr"), 1)

                def outputs(hd):
                    pe.wait_ge(S("xa_t"), 8 * l + 2 * hd + 2)
                    for dc in range(2):
                        if 1 <= hd <= 2:
                            pe.wait_ge(S("x_lo"), X_LO_XA[l] + 2 * (hd - 1) + dc + 1)
                        ch = 2 * hd + dc
                        for mc in range(2):
                            m = pe.matmul(ps[:, XO_BANKS[hd][dc], :], VM[:, mc, ch * P:(ch + 1) * P],
                                          area(A_XPT + (hd % 2) * 2 * T + mc * T), start=(mc == 0), stop=(mc == 1))
                        m.then_inc(S("xa_o"), 1)

                project(n, at, 4, 1, S("proj_out"), base, 1, waits0, waits1)
                for t in range(4, 8):
                    if t in (4, 6):
                        scores((t - 4) // 2)
                    tile(at + t, ((at + t) % 2, BANKS[t % 4]), 1, (S("proj_out"), base + t - 3))
                pe.wait_ge(S("proj_out"), base + 8)
                turn(0)
                scores(2)
                outputs(0)
                turn(1)
                scores(3)
                outputs(1)
                for hd in (2, 3):
                    turn(hd)
                    outputs(hd)

            def ev_fill(j):
                if j < 9:
                    t = 4 + j
                    tile(EV_AT + t, ((EV_AT + t) % 2, BANKS[t % 4]), 1, (S("proj_out"), t - 3))
                elif j < 13:
                    if j == 9:
                        pe.wait_ge(S("proj_out"), 13)
                    values(EV_V_AT, j - 9, T)
                else:
                    if j == 13:
                        pe.wait_ge(S("gla_v"), 4)
                    kv_tile(0, j - 13, KV_BANKS)

            kv_at = [3]

            def gla_fill(n):
                for _ in range(n):
                    if kv_at[0] < 16:
                        kv_tile(0, kv_at[0], KV_BANKS)
                        kv_at[0] += 1

            ffn(0)
            project(1, EV_AT, 4, 1, S("proj_out"), 0, 1,
                    [(S("h_ready"), 3)], [(S("h_ready"), 8)])
            rstd_columns(0)
            s5(ev_fill)
            gla_alpha()
            glu()
            gla(gla_fill)
            gla_fill(16)
            out_proj(0, [X_LO_GLA + k + 1 for k in range(4)] + [X_LO_GLU + k + 1 for k in range(4)], [])
            cross(0, 2, [(S("h_ready"), 14)], [(S("h_ready"), 16)])
            out_proj(1, [X_LO_XA[0] + max(k + 1, 6) for k in range(8)], [])
            ffn(1)
            ffn(2)
            project(5, OD_AT, 4, 1, S("proj_out"), OD_BASE, 1,
                    [(S("h_ready"), 35)], [(S("h_ready"), 40)])
            for t in range(4, OD_TILES):
                tile(OD_AT + t, ((OD_AT + t) % 2, BANKS[t % 4]), 1, (S("proj_out"), OD_BASE + t - 3))
                if t >= 7:
                    for r in ([2 * (t - 7), 2 * (t - 7) + 1] if t < 13 else [t - 1]):
                        rope(r)
            rstd_columns(1)
            pe.wait_ge(S("proj_out"), OD_BASE + 16)
            for q in range(2):
                values(OD_V_AT, q, 2 * P)
            indexer_weights()
            kv_at[0] = 0

            def od_fill(n):
                for _ in range(n):
                    if kv_at[0] < 16:
                        kv_tile(1, kv_at[0], [6, 7])
                        kv_at[0] += 1

            indexer(od_fill)
            od_fill(16)
            attention()
            out_proj(2, [X_LO_ATT + 8] * 8, [(S("att_s"), 8)])
            cross(1, 6, [(S("h_ready"), 46), (S("x_lo"), X_LO_ATT + 8)], [(S("h_ready"), 48)])
            out_proj(3, [X_LO_XA[1] + max(k + 1, 6) for k in range(8)], [])
            ffn(3)
            for k in range(KC):
                if k == 0:
                    pe.wait_ge(S("h_ready"), 8 * 7 + 1)
                ssq(8, k)

        @block.scalar
        def _(act):
            def hi(dst, src, count, **kw):
                act.activation(dst, src, ACT.Copy, **kw).then_inc(S("x_hi"), 1)

            def norm(n):
                to = NORM_TO[n] if n < 8 else None
                for k in range(KC):
                    if n == 0:
                        if k == 0:
                            act.wait_ge(S("vec_in"), 16)
                            act.wait_ge(S("x_in0"), 16)
                        if k == 2:
                            act.wait_ge(S("x_in1"), 16)
                    else:
                        act.wait_ge(S("h_ready"), 8 * (n - 1) + k + 1)
                    if to is not None:
                        if n in (1, 4, 5) and k >= 4:
                            f = {1: 0, 4: 1, 5: 2}[n]
                            act.wait_ge(S("block_done"), FFN_AT[f] + FFN_BLOCKS - (2 if k < 6 else 0))
                        hi(X[to][:, k, 0, :], h[:, k, :], 0, scale=gain(n, k))
                    if 8 * n + k >= 2:
                        act.wait_ge(S("ssq_done"), 8 * n + k - 1)
                    act.activation(sq[:, k % 2, :], h[:, k, :], ACT.Square).then_inc(S("sq_ready"), 1)
                if n == 0:
                    act.wait_ge(S("eps_set"), 2)
                act.wait_ge(S("ssq_done"), 8 * n + 8)
                if n >= 1:
                    act.wait_ge(S("rstd_ready"), n)
                act.activation(std[:], ps[:, SSQ_BANK, :], ACT.Sqrt, bias=epsc[:, 0:1]
                               ).then_inc(S("std_ready"), 1)

            def ffn(f, beside=None):
                at, xo = FFN_AT[f], 1 - NORM_TO[FFN_NORM[f]]

                def silu(i, s):
                    act.wait_ge(S("gate_ready"), i * 2 + (FC * f + s + 1))
                    act.activation(sg[:, s, :], tg[:, s, :], ACT.Silu).then_inc(S("silu"), 1)

                def table(i, s):
                    act.wait_ge(S("s5_turn"), i * 2 + (s - 5))
                    m, c, sn = kv[:, 4 * s * T:(4 * s + 1) * T], kv[:, (4 * s + 2) * T:(4 * s + 3) * T], \
                        kv[:, (4 * s + 3) * T:(4 * s + 4) * T]
                    if not (isinstance(i, int) and i == 3):
                        act.wait_ge(S(f"tab_out{s}"), i * 16 - 48)
                    act.activation(sn, m, ACT.Sin, scale=TWO_PI_BELOW).then_inc(S("s5_sin"), 1)
                    act.wait_ge(S("s5_sin"), i * 2 + (s - 5))
                    act.activation(m, m, ACT.Abs).then_inc(S("s5_abs"), 1)
                    act.wait_ge(S("s5_abs"), i * 2 + (s - 5))
                    act.activation(c, m, ACT.Sin, scale=-TWO_PI_BELOW, bias=epsc[:, 1:2]).then_inc(S("s5_cos"), 1)
                    act.wait_ge(S("s5_cos"), i * 2 + (s - 5))
                    j = i * 2 + (s - 6)
                    dst = s5_tables[j] if isinstance(i, int) else \
                        s5_tables[bass.ds(j, 1)].rearrange("a p n -> p (a n)")
                    act.dma_start(dst, kv[:, (4 * s + 2) * T:(4 * s + 4) * T]).then_inc(S(f"tab_out{s}"), 16)

                last = FC // 2 - 1
                if f == 0:
                    for i in range(4):
                        for s in range(2):
                            silu(i, s)
                        if i == 0:
                            memory(0)
                        if i == 1:
                            s5_constants()
                        if i == 3:
                            for s in range(2):
                                table(i, s)
                    with act.Fori(4, last) as i:
                        for s in range(2):
                            silu(i, s)
                        for s in range(2):
                            table(i, s)
                elif f == 2:
                    for s in range(2):
                        silu(0, s)
                    memory(1)
                    with act.Fori(1, last) as i:
                        for s in range(2):
                            silu(i, s)
                else:
                    with act.Fori(0, last) as i:
                        for s in range(2):
                            silu(i, s)
                dn = at + 2 * FC

                def part(d, d4, used):
                    if used is not None:
                        act.wait_ge(S("block_done"), used)
                    ch = [6, 7, 4, 5][d4]
                    act.activation(X[xo][:, ch:ch + 1, 0, :], hid[:, d, :], ACT.Copy).then_inc(S("x_hi"), 1)

                for d in range(4):
                    act.wait_ge(S("hid_done"), FC * f + d + 1)
                    part(slice(d, d + 1), d, None)
                for s in range(2):
                    silu(last, s)
                if f == 0:
                    for s in range(2):
                        table(last, s)
                act.wait_ge(S("hid_done"), FC * (f + 1))
                if beside is not None:
                    beside()
                with act.Fori(1, 5) as i:
                    for s in range(4):
                        part(bass.ds(i * 4 + s, 1), s, i * 4 + (dn + s - 3))
                for d in (20, 21):
                    part(slice(d, d + 1), d % 4, dn + d - 3)

            def memory(l):
                m = area(A_MEM, 4 * T).rearrange("p (k m) -> p k m", m=MEM)
                act.wait_ge(S(f"mem_in{l}"), 16)
                for k in range(KC):
                    if k >= 2:
                        act.wait_ge(S("mssq_done"), 8 * l + k - 1)
                    act.activation(sq[:, k % 2, 0:MEM], m[:, k, :], ACT.Square).then_inc(S("msq_ready"), 1)
                act.wait_ge(S("mssq_done"), 8 * l + 8)
                act.wait_ge(S("rstd_ready"), [1, 5][l])
                act.activation(std[:, 0:MEM], ps[:, 1, 0:MEM], ACT.Sqrt, bias=epsc[:, 0:1]
                               ).then_inc(S("mstd"), 1)

            def memory_split(l):
                m = area(A_MEM, 4 * T).rearrange("p (k m) -> p k m", m=MEM)
                act.wait_ge(S("mem_n"), 8 * l + 8)
                act.wait_ge(S("block_done"), FFN_AT[2 * l] + 2 * FC)
                for k in range(KC):
                    act.activation(memX[:, k, 0, :], m[:, k, :], ACT.Copy).then_inc(S("mem_hi"), 1)

            def kv_out(l, t, banks):
                act.wait_ge(S("block_done"), kv_block(l, t) + 1)
                if t < 8:
                    act.activation(KT[:, t, :], ps[:, banks[t % 2], 0:MEM], ACT.Copy).then_inc(S("kv_out"), 1)
                elif t % 4 == 3:
                    half = (t - 8) // 4
                    for mt in range(2):
                        act.activation(VM[:, mt, half * T:(half + 1) * T], ps[:, banks[mt], :], ACT.Copy
                                       ).then_inc(S("kv_out"), 1)

            def gla_decay():
                for p in range(2):
                    act.wait_ge(S("zb_ready"), p + 1)
                    act.activation(sg[:, p, :], tu[:, p, :], ACT.Abs).then_inc(S("g_abs"), 1)
                act.wait_ge(S("g_abs"), 2)
                act.activation(sg[:, :, :], sg[:, :, :], ACT.Exp, scale=-1.0).then_inc(S("g_exp"), 1)
                act.wait_ge(S("g_exp"), 1)
                act.activation(sg[:, :, :], sg[:, :, :], ACT.Ln, bias=1.0).then_inc(S("g_ln"), 1)
                for p in range(2):
                    bc = area(A_BC + p * T)
                    act.wait_ge(S("g_cum"), p + 1)
                    if p == 0:
                        act.wait_ge(S("g_cum"), 2)
                    act.activation(tg[:, p, :], bc, ACT.Exp, scale=1.0 / GLA_TAU).then_inc(S("g_eb"), 1)
                    act.activation(area(A_KINV + p * T), bc, ACT.Exp, scale=-1.0 / GLA_TAU).then_inc(S("g_einv"), 1)
                    act.activation(col[:, p * 8:p * 8 + 8], bc.rearrange("p (c i) -> p c i", i=64)[:, :, 63],
                                   ACT.Exp, scale=1.0 / GLA_TAU).then_inc(S("g_decay"), 1)
                for p in range(2):
                    act.wait_ge(S("g_rel"), p + 1)
                    act.activation(tu[:, p, :], tu[:, p, :], ACT.Exp, scale=-1.0 / GLA_TAU).then_inc(S("g_eend"), 1)
                act.wait_ge(S("proj_out"), 13)
                act.activation(ar[:, 9 * T:13 * T], ar[:, 9 * T:13 * T], ACT.Silu).then_inc(S("g_silu"), 1)

            def gla(fill):
                fill(3)
                act.wait_ge(S("kend_tr"), 1)
                for p in range(2):
                    act.activation(kend_t[:, :, p, :], ps[:, 6 + p, :].rearrange("p (t f) -> p t f", t=4), ACT.Copy
                                   ).then_inc(S("kend_t"), 1)
                fill(3)
                for hd in range(4):
                    act.wait_ge(S("go_mm"), hd + 1)
                    if hd >= 2:
                        act.wait_ge(S("gms_mm"), hd - 1)
                    act.activation(sq[:, hd % 2, :], ps[:, BANKS[hd % 2], :], ACT.Square).then_inc(S("gsq"), 1)
                    act.wait_ge(S("gms_mm"), hd + 1)
                    if hd >= 1:
                        act.wait_ge(S("grstd"), hd)
                    act.activation(std[:], ps[:, hd % 2, :], ACT.Sqrt, bias=epsc[:, 0:1], scale=float(KC)
                                   ).then_inc(S("gstd"), 1)
                    act.wait_ge(S("gla_o"), hd + 1)
                    hi(X[0][:, hd, 0, :], area(A_O + hd * T), 0)
                    fill(2)

            def s5_constants():
                act.wait_ge(S("th_ready"), 1)
                act.activation(tiny[:, 6, :], tiny[:, 5, :], ACT.Abs).then_inc(S("th_abs"), 1)
                act.activation(tiny[:, 8, :], tiny[:, 5, :], ACT.Sin).then_inc(S("th_trig"), 1)
                act.wait_ge(S("th_abs"), 1)
                act.activation(tiny[:, 7, :], tiny[:, 6, :], ACT.Sin, scale=-1.0, bias=epsc[:, 1:2]
                               ).then_inc(S("th_trig"), 1)

            def s5_load(j):
                t = A_S5T + (j % 3) * 2 * T
                if j == 0:
                    for s in range(2):
                        act.wait_ge(S(f"tab_out{s}"), 16 * 8)
                if j >= 3:
                    act.wait_ge(S("s5_xi"), j - 2)
                act.dma_start(area(t, 2 * T), s5_tables[j]).then_inc(S(f"s5_tab{j % 3}"), 16)

            def s5_begin():
                act.wait_ge(S("x_lo"), X_LO_HID[0] + FC)
                act.dma_start(area(A_S5B, 2 * T), s5b.rearrange("p c q s -> p (c q s)")).then_inc(S("s5b_in"), 16)
                act.dma_start(area(A_S5C, 2 * T), s5c.rearrange("p c j o -> p (c j o)")).then_inc(S("s5c_in"), 16)
                for j in range(3):
                    s5_load(j)

            def s5_gelu(q):
                act.wait_ge(S("s5_y"), q + 1)
                act.activation(Pt[q], Pt[q], ACT.Gelu_apprx_tanh).then_inc(S("gelu"), 1)

            def s5(fill):
                for j in range(S5_TILES):
                    fill(j)
                    if j >= 1 and j + 2 < S5_TILES:
                        s5_load(j + 2)
                    if j % 4 == 1 and j >= 5:
                        s5_gelu(j // 4 - 1)
                act.wait_ge(S("s5_xi"), S5_TILES)
                act.dma_start(chunk_mask, rows[1:2, :].to_broadcast([P, T])).then_inc(S("cmask_in"), 16)
                act.dma_start(wal, w_alpha).then_inc(S("wal_in"), 16)
                s5_gelu(3)
                act.wait_ge(S("gelu"), 4)
                for q in range(4):
                    hi(X[1][:, q, 0, :], Pt[q], 0)

            def glu():
                for n in range(4):
                    act.wait_ge(S("half_done") if n % 2 == 0 else S("block_done"), GLU_AT + n // 2 + 1)
                    if n >= 2:
                        act.wait_ge(S("glu_o"), n - 1)
                    act.activation(sg[:, n % 2, :], ps[:, GLU_BANKS[n], :], ACT.Sigmoid,
                                   bias=vec[:, V_BGLU + n:V_BGLU + n + 1]).then_inc(S("glu_sig"), 1)

            def glu_split():
                act.wait_ge(S("glu_o"), 4)
                act.wait_ge(S("block_done"), kv_block(0, 15) + 1)
                for n in range(4):
                    hi(X[0][:, 4 + n, 0, :], Pt[n], 0)

            def tables():
                act.dma_start(area(A_POS + T).bitcast(I32), pos.to_broadcast([P, T])).then_inc(S("pos_in"), 16)
                for i in range(2):
                    act.wait_ge(S("ang"), i + 1)
                    s, c = area(A_TAB + (2 * i + 1) * T), area(A_TAB + 2 * i * T)
                    act.activation(c, s, ACT.Abs).then_inc(S("ang_abs"), 1)
                    act.wait_ge(S("ang_abs"), i + 1)
                    act.activation(s, s, ACT.Sin).then_inc(S("tab"), 1)
                    act.activation(c, c, ACT.Sin, scale=-1.0, bias=epsc[:, 1:2]).then_inc(S("tab"), 1)

            def indexer(fill):
                for i in range(24):
                    nk = (i // 8 + 2) * P
                    if i % 8 == 5:
                        fill(1)
                    act.wait_ge(S("logit_mm"), i + 1)
                    if i >= 2:
                        act.wait_ge(S("idx_acc"), i - 1)
                    act.activation(tg[:, i % 2, 0:nk], ps[:, BANKS[i % 4], 0:nk], ACT.Relu).then_inc(S("relu"), 1)

            def attention():
                def exps(i):
                    g, qb = UNITS[i]
                    pb, c = (A_P if i % 2 == 0 else A_P1), 16 * (i % 2)
                    act.wait_ge(S("att_nm"), i + 1)
                    for j in range(4):
                        row = area(pb + j * T)[:, 0:(qb + 1) * P]
                        act.activation(row, row, ACT.Exp, bias=col[:, c + 4 + j:c + 5 + j],
                                       accum_out=col[:, c + 8 + j:c + 9 + j]).then_inc(S("att_e"), 1)

                nt = 0
                exps(0)
                for i, (g, qb) in enumerate(UNITS):
                    if i + 1 < len(UNITS):
                        exps(i + 1)
                    for kc in range(qb + 1):
                        act.wait_ge(S("att_tr"), nt + 1)
                        if i >= 1 and kc == 0:
                            act.wait_ge(S("att_o"), i)
                        act.activation(area(A_PT + kc * T), ps[:, 6 + nt % 2, :], ACT.Copy).then_inc(S("att_t"), 1)
                        nt += 1
                    act.wait_ge(S("att_o"), i + 1)
                    hi(X[0][:, 4 * g:4 * g + 4, 0, qb * P:(qb + 1) * P],
                       ps[:, i % 2, :].rearrange("p (j q) -> p j q", j=4), 0)

            def cross(l):
                def exps(hd):
                    pb, c = A_XP + (hd % 2) * 2 * T, 16 * (hd % 2)
                    act.wait_ge(S("xa_nm"), 4 * l + hd + 1)
                    for qb in range(QB):
                        e = act.activation(area(pb + qb * MEM, MEM),
                                           ps[:, XS_BANKS[hd % 2] + qb // 2, (qb % 2) * MEM:(qb % 2 + 1) * MEM],
                                           ACT.Exp, scale=XA_DIM ** -0.5, bias=col[:, c + 4 + qb:c + 5 + qb],
                                           accum_out=col[:, c + 8 + qb:c + 9 + qb])
                    e.then_inc(S("xa_p"), 1)

                def copies(hd):
                    for mc in range(2):
                        act.wait_ge(S("xa_tr"), 8 * l + 2 * hd + mc + 1)
                        if hd >= 2:
                            act.wait_ge(S("xa_o"), 8 * l + 2 * hd - 2)
                        act.activation(area(A_XPT + (hd % 2) * 2 * T + mc * T), ps[:, BANKS[2 + mc], :], ACT.Copy
                                       ).then_inc(S("xa_t"), 1)

                def upper(hd):
                    for dc in range(2):
                        act.wait_ge(S("xa_o"), 8 * l + 2 * hd + dc + 1)
                        hi(X[0][:, 2 * hd + dc, 0, :], ps[:, XO_BANKS[hd][dc], :], 0)

                exps(0)
                exps(1)
                copies(0)
                exps(2)
                upper(0)
                copies(1)
                exps(3)
                upper(1)
                for hd in (2, 3):
                    copies(hd)
                    upper(hd)

            kv_next = [0]

            def fill(l, banks, n):
                for _ in range(n):
                    if kv_next[0] < 16:
                        kv_out(l, kv_next[0], banks)
                        kv_next[0] += 1

            norm(0)
            ffn(0, lambda: memory_split(0))
            s5_begin()
            norm(1)
            s5(lambda j: fill(0, KV_BANKS, 1) if j >= 14 else None)
            gla_decay()
            glu()
            gla(lambda n: fill(0, KV_BANKS, n))
            fill(0, KV_BANKS, 16)
            glu_split()
            norm(2)
            cross(0)
            norm(3)
            ffn(1, tables)
            act.dma_start(area(A_MEM, 4 * T).rearrange("p (k m) -> p k m", m=MEM), memT).then_inc(S("mem_in1"), 16)
            norm(4)
            ffn(2, lambda: memory_split(1))
            norm(5)
            kv_next[0] = 0
            indexer(lambda n: fill(1, [6, 7], n))
            fill(1, [6, 7], 16)
            attention()
            norm(6)
            cross(1)
            norm(7)
            ffn(3)
            norm(8)
            for k in range(KC):
                act.wait_ge(S("y_ready"), k + 1)
                act.dma_start(out[:, k, :], h[:, k, :]).then_inc(S("out_done"), 16)
            act.wait_ge(S("out_done"), 16 * KC)

        @block.vector
        def _(dve):
            step = [0]

            def chain(ins):
                step[0] += 1
                ins.then_inc(S("dve_step"), 1)
                dve.wait_ge(S("dve_step"), step[0])

            def lo_of(dst, src, hi_ap, count):
                dve.wait_ge(S("x_hi"), count)
                dve.tensor_tensor(dst, src, hi_ap.bitcast(F32), ALU.subtract).then_inc(S("x_lo"), 1)

            def norm(n, factor, mm_sem, mm_base, banks):
                to = NORM_TO[n] if n < 8 else None

                def lower(k):
                    if to is None:
                        return
                    dve.wait_ge(S("x_hi"), X_LO_NORM[n] + k + 1)
                    dve.scalar_tensor_tensor(X[to][:, k, 1, :], h[:, k, :], gain(n, k),
                                             X[to][:, k, 0, :].bitcast(F32), ALU.mult, ALU.subtract
                                             ).then_inc(S("x_lo"), 1)

                if n == 0:
                    for k in range(KC):
                        lower(k)
                else:
                    for k in range(KC):
                        if mm_sem is not None and k < 7:
                            dve.wait_ge(mm_sem, mm_base[0] + k + 1)
                        elif mm_sem is not None:
                            dve.wait_ge(S("block_done"), mm_base[1])
                        else:
                            dve.wait_ge(S("block_done"), mm_base[0] + k + 1)
                        dve.scalar_tensor_tensor(h[:, k, :], ps[:, banks[k], :], factor, h[:, k, :],
                                                 ALU.mult, ALU.add).then_inc(S("h_ready"), 1)
                        if k >= 1:
                            lower(k - 1)
                    lower(KC - 1)
                dve.wait_ge(S("std_ready"), n + 1)
                dve.reciprocal(rstd[:], std[:]).then_inc(S("rstd_ready"), 1)
                dve.wait_ge(S("rstd_ready"), n + 1)

            def norm_after_ffn(n, f):
                norm(n, 0.5, S("down_out"), (7 * f, FFN_AT[f] + FFN_BLOCKS), DOWN_BANKS)

            def norm_after_out(n, o):
                norm(n, 1.0, None, (OUT_AT[o],), [BANKS[t % 4] for t in range(8)])

            def ffn(f, beside=None):
                at, xo = FFN_AT[f], 1 - NORM_TO[FFN_NORM[f]]

                def gate(i, s):
                    dve.wait_ge(S("block_done"), i * 4 + (at + 2 * s + 1))
                    dve.tensor_tensor(tg[:, s, :], ps[:, BANKS[2 * s], :], rstd[:], ALU.mult
                                      ).then_inc(S("gate_ready"), 1)
                    dve.wait_ge(S("block_done"), i * 4 + (at + 2 * s + 2))
                    dve.tensor_tensor(tu[:, s, :], ps[:, BANKS[2 * s + 1], :], rstd[:], ALU.mult
                                      ).then_inc(S("up_ready"), 1)
                    dve.wait_ge(S("up_ready"), i * 2 + (FC * f + s + 1))
                    dve.wait_ge(S("silu"), i * 2 + (FC * f + s + 1))
                    j = i * 2 + s
                    dst = hid[:, j:j + 1, :] if isinstance(i, int) else hid[:, bass.ds(j, 1), :]
                    dve.tensor_tensor(dst, sg[:, s:s + 1, :], tu[:, s:s + 1, :], ALU.mult
                                      ).then_inc(S("hid_done"), 1)

                last = FC // 2 - 1
                if f == 0:
                    parts = s5_constants()
                    for i in range(4):
                        for s in range(2):
                            gate(i, s)
                        if i == 1:
                            memory(0)
                        if i < 3:
                            next(parts)
                        else:
                            for s in range(2):
                                turns(i, s)
                    with dve.Fori(4, last) as i:
                        for s in range(2):
                            gate(i, s)
                        for s in range(2):
                            turns(i, s)
                elif f == 2:
                    for i in range(2):
                        for s in range(2):
                            gate(i, s)
                    memory(1)
                    with dve.Fori(2, last) as i:
                        for s in range(2):
                            gate(i, s)
                else:
                    with dve.Fori(0, last) as i:
                        for s in range(2):
                            gate(i, s)

                def part(d, d4, count):
                    ch = [6, 7, 4, 5][d4]
                    dve.wait_ge(S("x_hi"), count)
                    dve.tensor_tensor(X[xo][:, ch:ch + 1, 1, :], hid[:, d, :],
                                      X[xo][:, ch:ch + 1, 0, :].bitcast(F32), ALU.subtract
                                      ).then_inc(S("x_lo"), 1)

                base = X_LO_HID[f]
                dve.wait_ge(S("hid_done"), FC * f + 4)
                for d in range(4):
                    part(slice(d, d + 1), d, base + d + 1)
                for s in range(2):
                    gate(last, s)
                if f == 0:
                    for s in range(2):
                        turns(last, s)
                dve.wait_ge(S("hid_done"), FC * (f + 1))
                if beside is not None:
                    beside()
                with dve.Fori(1, 5) as i:
                    for s in range(4):
                        part(bass.ds(i * 4 + s, 1), s, i * 4 + (base + s + 1))
                for d in (20, 21):
                    part(slice(d, d + 1), d % 4, base + d + 1)

            def tile_out(at, t):
                dve.wait_ge(S("block_done"), at + t + 1)
                dve.tensor_tensor(Pt[t], ps[:, BANKS[t % 4], :], rstd[:], ALU.mult).then_inc(S("proj_out"), 1)

            def rstd_columns(l):
                dve.wait_ge(S("rcol_mm"), l + 1)
                dve.tensor_copy(col[:, 16:20], ps[:, 1, :].rearrange("p (t n) -> p t n", n=P)[:, :, 0]
                                ).then_inc(S("rcol_ready"), 1)
                dve.wait_ge(S("rcol_ready"), l + 1)

            def memory(l):
                m = area(A_MEM, 4 * T).rearrange("p (k m) -> p k m", m=MEM)
                dve.wait_ge(S("mstd"), l + 1)
                dve.reciprocal(std[:, MEM:T], std[:, 0:MEM]).then_inc(S("mrstd"), 1)
                dve.wait_ge(S("mrstd"), l + 1)
                for k in range(KC):
                    g = vec[:, V_MEMG + k:V_MEMG + k + 1]
                    dve.scalar_tensor_tensor(m[:, k, :], m[:, k, :], g, std[:, MEM:T], ALU.mult, ALU.mult
                                             ).then_inc(S("mem_n"), 1)
                dve.wait_ge(S("mem_n"), 8 * l + 8)

            def memory_split(l):
                m = area(A_MEM, 4 * T).rearrange("p (k m) -> p k m", m=MEM)
                for k in range(KC):
                    dve.wait_ge(S("mem_hi"), 8 * l + k + 1)
                    dve.tensor_tensor(memX[:, k, 1, :], m[:, k, :], memX[:, k, 0, :].bitcast(F32), ALU.subtract
                                      ).then_inc(S("mem_lo"), 1)

            def tn(i):
                return tiny[:, i, :]

            def exact_exp(dst, src):
                k, r, p = tn(9), tn(10), tn(11)
                chain(dve.tensor_scalar(k, src, 1.4426950408889634, MAGIC, ALU.mult, ALU.add))
                chain(dve.tensor_scalar(k, k, MAGIC, None, ALU.subtract))
                chain(dve.tensor_scalar(k, k, -126.0, 127.0, ALU.max, ALU.min))
                chain(dve.scalar_tensor_tensor(r, k, -0.693359375, src, ALU.mult, ALU.add))
                chain(dve.scalar_tensor_tensor(r, k, 2.12194440e-4, r, ALU.mult, ALU.add))
                chain(dve.tensor_scalar(p, r, 1.0 / 5040, 1.0 / 720, ALU.mult, ALU.add))
                for c in (1.0 / 120, 1.0 / 24, 1.0 / 6, 0.5, 1.0, 1.0):
                    chain(dve.tensor_tensor(p, p, r, ALU.mult))
                    chain(dve.tensor_scalar(p, p, c, None, ALU.add))
                chain(dve.tensor_scalar(k, k, 127.0, None, ALU.add))
                chain(dve.tensor_copy(tiny_i[:], k))
                chain(dve.tensor_scalar(tiny_i[:], tiny_i[:], 23, None, ALU.logical_shift_left))
                chain(dve.tensor_tensor(dst, p, tiny_i[:].bitcast(F32), ALU.mult))

            def s5_constants():
                lr, dt, th, ab_r, ab_i = tn(0), tn(1), tn(2), tn(3), tn(4)
                mag, ph, pl = sc5[:, C_MAG:C_MAG + 16], sc5[:, C_PH:C_PH + 16], sc5[:, C_PL:C_PL + 16]
                fr, fi = sc5[:, C_FR:C_FR + 16], sc5[:, C_FI:C_FI + 16]
                li = vec[:, V_LIM:V_LIM + 16]
                chain(dve.tensor_scalar(lr, vec[:, V_LRE:V_LRE + 16], -1e-4, None, ALU.min))
                exact_exp(dt, vec[:, V_LDT:V_LDT + 16])
                chain(dve.tensor_tensor(th, lr, dt, ALU.mult))
                exact_exp(mag, th)
                yield
                chain(dve.tensor_tensor(th, li, dt, ALU.mult))
                reduce_angle(th, tn(5))
                dve.tensor_scalar(tn(5), th, PI_BELOW, -PI_BELOW, ALU.min, ALU.max).then_inc(S("th_ready"), 1)
                chain(dve.tensor_scalar(th, th, 0.15915494309189535, None, ALU.mult))
                chain(dve.tensor_scalar(ph, th, 4096.0, MAGIC, ALU.mult, ALU.add))
                chain(dve.tensor_scalar(ph, ph, MAGIC, 1.0 / 4096, ALU.subtract, ALU.mult))
                chain(dve.tensor_tensor(pl, th, ph, ALU.subtract))
                yield
                dve.wait_ge(S("th_trig"), 2)
                chain(dve.tensor_tensor(ab_r, tn(7), mag, ALU.mult))
                chain(dve.tensor_tensor(ab_i, tn(8), mag, ALU.mult))
                chain(dve.tensor_scalar(ab_r, ab_r, 1.0, None, ALU.subtract))
                den, t1 = tn(5), tn(6)
                chain(dve.tensor_tensor(den, lr, lr, ALU.mult))
                chain(dve.tensor_tensor(t1, li, li, ALU.mult))
                chain(dve.tensor_tensor(den, den, t1, ALU.add))
                chain(dve.reciprocal(den, den))
                chain(dve.tensor_tensor(fr, ab_r, lr, ALU.mult))
                chain(dve.tensor_tensor(t1, ab_i, li, ALU.mult))
                chain(dve.tensor_tensor(fr, fr, t1, ALU.add))
                chain(dve.tensor_tensor(fr, fr, den, ALU.mult))
                chain(dve.tensor_tensor(fi, ab_i, lr, ALU.mult))
                chain(dve.tensor_tensor(t1, ab_r, li, ALU.mult))
                chain(dve.tensor_tensor(fi, fi, t1, ALU.subtract))
                chain(dve.tensor_tensor(fi, fi, den, ALU.mult))
                yield

            def reduce_angle(x, k):
                chain(dve.tensor_scalar(k, x, 0.15915494309189535, MAGIC, ALU.mult, ALU.add))
                chain(dve.tensor_scalar(k, k, MAGIC, None, ALU.subtract))
                for c in (TWO_PI_1, TWO_PI_2, TWO_PI_3):
                    chain(dve.scalar_tensor_tensor(x, k, -c, x, ALU.mult, ALU.add))

            def turns(i, s):
                time = area(A_TIME)
                if isinstance(i, int):
                    dve.wait_ge(S("time_in"), 16)
                    j = 2 * (i - 3) + s
                    ph, pl = sc5[:, C_PH + j:C_PH + j + 1], sc5[:, C_PL + j:C_PL + j + 1]
                else:
                    ph = sc5[:, bass.ds(i * 2 + (C_PH + s - 6), 1)]
                    pl = sc5[:, bass.ds(i * 2 + (C_PL + s - 6), 1)]
                a, b = kv[:, 4 * s * T:(4 * s + 1) * T], kv[:, (4 * s + 1) * T:(4 * s + 2) * T]

                def then(ins, n):
                    ins.then_inc(S("turn_step"), 1)
                    dve.wait_ge(S("turn_step"), i * 10 + (5 * s + n - 30))

                then(dve.tensor_scalar(a, time, ph, None, ALU.mult), 1)
                then(dve.tensor_scalar(b, a, MAGIC, MAGIC, ALU.add, ALU.subtract), 2)
                then(dve.tensor_tensor(a, a, b, ALU.subtract), 3)
                then(dve.scalar_tensor_tensor(a, time, pl, a, ALU.mult, ALU.add), 4)
                then(dve.tensor_scalar(b, a, MAGIC, MAGIC, ALU.add, ALU.subtract), 5)
                dve.tensor_tensor(a, a, b, ALU.subtract).then_inc(S("s5_turn"), 1)

            def gla_decay():
                dve.wait_ge(S("alpha_mm"), 1)
                for p in range(2):
                    dve.tensor_scalar(tu[:, p, :], ps[:, 6 + p, :], vec[:, V_BALPHA + p:V_BALPHA + p + 1], None,
                                      ALU.add).then_inc(S("zb_ready"), 1)
                dve.wait_ge(S("g_ln"), 1)
                dve.wait_ge(S("cmask_in"), 16)
                for p in range(2):
                    chain(dve.scalar_tensor_tensor(tu[:, p, :], tu[:, p, :], 0.0, sg[:, p, :], ALU.min, ALU.subtract))
                    dve.tensor_tensor_scan(area(A_BC + p * T), chunk_mask, tu[:, p, :], 0.0, ALU.mult, ALU.add
                                           ).then_inc(S("g_cum"), 1)
                dve.wait_ge(S("g_cum"), 2)
                for p in range(2):
                    bc = area(A_BC + p * T).rearrange("p (c i) -> p c i", i=64)
                    dve.tensor_tensor(tu[:, p, :].rearrange("p (c i) -> p c i", i=64), bc,
                                      bc[:, :, 63:64].to_broadcast([P, NCH, 64]), ALU.subtract).then_inc(S("g_rel"), 1)
                for p in range(2):
                    dve.wait_ge(S("g_eb"), p + 1)
                    dve.scalar_tensor_tensor(Pt[5 + p], Pt[5 + p], GLA_DK ** -0.5, tg[:, p, :], ALU.mult, ALU.mult
                                             ).then_inc(S("qdec"), 1)
                    dve.wait_ge(S("g_einv"), p + 1)
                    dve.tensor_tensor(area(A_KINV + p * T), area(A_KINV + p * T), Pt[7 + p], ALU.mult
                                      ).then_inc(S("kinv"), 1)
                    dve.wait_ge(S("g_eend"), p + 1)
                    dve.tensor_tensor(Pt[7 + p], Pt[7 + p], tu[:, p, :], ALU.mult).then_inc(S("kend"), 1)
                dve.wait_ge(S("qdec"), 2)
                for p in range(2):
                    chain(dve.memset(tg[:, p, :], 0.0))

            def gla():
                dve.wait_ge(S("g_decay"), 2)
                for c in range(NCH - 1):
                    dve.wait_ge(S("state_mm"), c + 1)
                    for p in range(2):
                        for e in range(2):
                            r = slice(64 * e, 64 * e + 64)
                            src = ps[r, BANKS[c % 2], p * 256 + e * P:p * 256 + (e + 1) * P]
                            if c == 0:
                                dve.tensor_copy(state[r, p, 1, :], src).then_inc(S("state"), 1)
                            else:
                                dve.scalar_tensor_tensor(state[r, p, c + 1, :], state[r, p, c, :],
                                                         col[r, p * 8 + c:p * 8 + c + 1], src, ALU.mult, ALU.add
                                                         ).then_inc(S("state"), 1)
                    dve.wait_ge(S("state"), 4 * (c + 1))

                def score(hd):
                    dve.wait_ge(S("gscore_mm"), hd + 1)
                    if hd >= 2:
                        dve.wait_ge(S("go_mm"), hd - 1)
                    dve.copy_predicated(tg[:, hd % 2, :].rearrange("p (t i) -> p t i", t=4),
                                        msk[:].unsqueeze(1).to_broadcast([P, 4, P]),
                                        ps[:, 6 + hd % 2, :].rearrange("p (t i) -> p t i", t=4)
                                        ).then_inc(S("gscore"), 1)

                dve.wait_ge(S("msk_in"), 16)
                score(0)
                for hd in range(4):
                    if hd < 3:
                        score(hd + 1)
                    dve.wait_ge(S("gstd"), hd + 1)
                    dve.reciprocal(rstd[:], std[:]).then_inc(S("grstd"), 1)
                    dve.wait_ge(S("grstd"), hd + 1)
                    o = area(A_O + hd * T)
                    chain(dve.scalar_tensor_tensor(o, ps[:, BANKS[hd % 2], :], vec[:, V_GLAN:V_GLAN + 1], rstd[:],
                                                   ALU.mult, ALU.mult))
                    if hd == 0:
                        dve.wait_ge(S("g_silu"), 1)
                    dve.tensor_tensor(o, o, Pt[9 + hd], ALU.mult).then_inc(S("gla_o"), 1)
                    dve.wait_ge(S("x_hi"), X_LO_GLA + hd + 1)
                    dve.wait_ge(S("gla_o"), hd + 1)
                    dve.tensor_tensor(X[0][:, hd, 1, :], o, X[0][:, hd, 0, :].bitcast(F32), ALU.subtract
                                      ).then_inc(S("x_lo"), 1)

            def s5_output_matrices():
                dve.wait_ge(S("s5c_in"), 16)
                cr, ci = s5ct[:, 0, :, :], s5ct[:, 1, :, :]
                fr = sc5[:, C_FR:C_FR + 16].unsqueeze(2).to_broadcast([P, 16, 32])
                fi = sc5[:, C_FI:C_FI + 16].unsqueeze(2).to_broadcast([P, 16, 32])
                tA = tu[:, 0, :].rearrange("p (j c) -> p j c", j=16)
                tB = tu[:, 1, :].rearrange("p (j c) -> p j c", j=16)
                chain(dve.tensor_tensor(tA, cr, fi, ALU.mult))
                chain(dve.tensor_tensor(tB, ci, fi, ALU.mult))
                chain(dve.tensor_tensor(cr, cr, fr, ALU.mult))
                dve.tensor_tensor(cr, cr, tB, ALU.subtract).then_inc(S("s5_c"), 1)
                chain(dve.tensor_tensor(ci, ci, fr, ALU.mult))
                chain(dve.tensor_tensor(ci, ci, tA, ALU.add))
                dve.tensor_scalar(ci, ci, -1.0, None, ALU.mult).then_inc(S("s5_c"), 1)

            def s5(fill):
                done = [0]

                def op(ins):
                    done[0] += 1
                    ins.then_inc(S("s5_step"), 1)
                    return done[0]

                def after(n):
                    if n:
                        dve.wait_ge(S("s5_step"), n)

                free = 0

                def out(q):
                    dve.wait_ge(S("s5_out_mm"), 4 * q + 4)
                    dve.scalar_tensor_tensor(Pt[q], Pt[q], vec[:, V_D + q:V_D + q + 1],
                                             ps[:, 6 + q % 2, :], ALU.mult, ALU.add).then_inc(S("s5_y"), 1)

                p1, p2, p3, p4, zr, zi = tg[:, 0, :], tg[:, 1, :], tu[:, 0, :], tu[:, 1, :], sg[:, 0, :], sg[:, 1, :]
                vr, vi = ps[:, 0, :], ps[:, 1, :]
                for j in range(S5_TILES):
                    fill(j)
                    t = A_S5T + (j % 3) * 2 * T
                    c, s = area(t), area(t + T)
                    x = A_S5X + (j % 2) * 2 * T
                    xr, xi = area(x), area(x + T)
                    mag = sc5[:, C_MAG + j:C_MAG + j + 1].to_broadcast([P, T])
                    dve.wait_ge(S(f"s5_tab{j % 3}"), 16 * (j // 3 + 1))
                    dve.wait_ge(S("s5_in_mm"), j + 1)
                    after(free)
                    op(dve.tensor_tensor(p1, vr, c, ALU.mult))
                    n2 = op(dve.tensor_tensor(p2, vi, s, ALU.mult))
                    if j >= 1:
                        dve.wait_ge(S("s5_xi"), j)
                    op(dve.tensor_tensor(p3, vi, c, ALU.mult))
                    dve.tensor_tensor(p4, vr, s, ALU.mult).then_inc(S("s5_read"), 1)
                    after(n2)
                    nr = op(dve.tensor_tensor(p1, p1, p2, ALU.add))
                    dve.wait_ge(S("s5_read"), j + 1)
                    ni = op(dve.tensor_tensor(p3, p3, p4, ALU.subtract))
                    after(nr)
                    nr = op(dve.tensor_tensor_scan(zr, mag, p1, 0.0, ALU.mult, ALU.add))
                    after(ni)
                    ni = op(dve.tensor_tensor_scan(zi, mag, p3, 0.0, ALU.mult, ALU.add))
                    after(nr)
                    op(dve.tensor_tensor(p1, zr, c, ALU.mult))
                    after(ni)
                    n2 = op(dve.tensor_tensor(p2, zi, s, ALU.mult))
                    op(dve.tensor_tensor(p3, zr, s, ALU.mult))
                    n4 = op(dve.tensor_tensor(p4, zi, c, ALU.mult))
                    if j >= 2:
                        dve.wait_ge(S("s5_out_mm"), j - 1)
                    after(n2)
                    free = op(dve.tensor_tensor(xr, p1, p2, ALU.subtract))
                    after(n4)
                    dve.tensor_tensor(xi, p3, p4, ALU.add).then_inc(S("s5_xi"), 1)
                    if j % 4 == 0 and j >= 4:
                        out(j // 4 - 1)
                dve.wait_ge(S("s5_xi"), S5_TILES)
                out(3)
                for q in range(4):
                    lo_of(X[1][:, q, 1, :], Pt[q], X[1][:, q, 0, :], X_LO_Y + q + 1)

            def glu():
                for n in range(4):
                    dve.wait_ge(S("glu_sig"), n + 1)
                    dve.tensor_tensor(Pt[n], Pt[n], sg[:, n % 2, :], ALU.mult).then_inc(S("glu_o"), 1)
                dve.wait_ge(S("glu_o"), 4)

            def glu_split():
                for n in range(4):
                    lo_of(X[0][:, 4 + n, 1, :], Pt[n], X[0][:, 4 + n, 0, :], X_LO_GLU + n + 1)

            def tables():
                dve.wait_ge(S("pos_in"), 16)
                chain(dve.tensor_copy(area(A_POS), area(A_POS + T).bitcast(I32)))
                for i in range(2):
                    x = area(A_TAB + (2 * i + 1) * T)
                    chain(dve.tensor_scalar(x, area(A_POS), vec[:, V_INVA + i:V_INVA + i + 1], None, ALU.mult))
                    reduce_angle(x, area(A_TAB + 2 * i * T))
                    dve.tensor_scalar(x, x, PI_BELOW, -PI_BELOW, ALU.min, ALU.max).then_inc(S("ang"), 1)

            def rope(t):
                c = area(A_TAB + (0 if t < 10 else 2) * T)
                s = area(A_TAB + (1 if t < 10 else 3) * T)
                if t == 0:
                    dve.wait_ge(S("tab"), 4)
                dve.wait_ge(S("rope_mm"), t + 1)
                dve.tensor_tensor(tg[:, t % 2, :], ps[:, 6 + t % 2, :], s, ALU.mult).then_inc(S("rope_s"), 1)
                chain(dve.tensor_tensor(Pt[t], Pt[t], c, ALU.mult))
                dve.wait_ge(S("rope_s"), t + 1)
                dve.tensor_tensor(Pt[t], Pt[t], tg[:, t % 2, :], ALU.add).then_inc(S("rope_done"), 1)

            def indexer_weights():
                dve.wait_ge(S("wi_mm"), 1)
                dve.tensor_scalar(col[:, 32:64].rearrange("p (t i) -> p t i", i=8),
                                  ps[:, 1, :].rearrange("p (t n) -> p t n", n=P)[:, :, 0:8],
                                  (IDX_HEADS * IDX_DIM) ** -0.5, None, ALU.mult).then_inc(S("wi_ready"), 1)
                dve.wait_ge(S("wi_ready"), 1)

            def indexer():
                dve.wait_ge(S("rope_done"), len(ROPE_TILES))
                i = 0
                for qb in range(1, QB):
                    nk = (qb + 1) * P
                    sc = area(A_SC + qb * T)[:, 0:nk]
                    for hd in range(IDX_HEADS):
                        w = col[:, 32 + 8 * qb + hd:33 + 8 * qb + hd]
                        dve.wait_ge(S("relu"), i + 1)
                        if hd == 0:
                            ins = dve.tensor_scalar(sc, tg[:, i % 2, 0:nk], w, None, ALU.mult)
                        else:
                            ins = dve.scalar_tensor_tensor(sc, tg[:, i % 2, 0:nk], w, sc, ALU.mult, ALU.add)
                        ins.then_inc(S("idx_acc"), 1)
                        i += 1
                        dve.wait_ge(S("idx_acc"), i)
                    chain(dve.tensor_tensor(sc[:, qb * P:nk], sc[:, qb * P:nk], cmask, ALU.add))
                chain(dve.tensor_copy(area(A_SC)[:, 0:P], cmask))

            def topk():
                for qb in range(1, QB):
                    nk = (qb + 1) * P
                    sc = area(A_SC + qb * T)[:, 0:nk]
                    for _ in range(TOPK // 8):
                        chain(dve.max(col[:, 20:28], sc))
                        chain(dve.match_replace(sc, col[:, 20:28], sc, TAKEN))
                    chain(dve.tensor_scalar(sc, sc, TAKEN / 2, MASKED, ALU.is_gt, ALU.mult))

            def attention():
                def unit(i):
                    g, qb = UNITS[i]
                    nk = (qb + 1) * P
                    pb, c = (A_P if i % 2 == 0 else A_P1), 16 * (i % 2)
                    return g, qb, nk, c, area(pb, 4 * T).rearrange("p (j n) -> p j n", j=4)[:, :, 0:nk]

                def front(i):
                    g, qb, nk, c, pr = unit(i)
                    bias = area(A_SC + qb * T)[:, 0:nk].unsqueeze(1).to_broadcast([P, 4, nk])
                    dve.wait_ge(S("att_mm"), i + 1)
                    if i >= 2:
                        dve.wait_ge(S("att_tr"), UNIT_TR[i - 2])
                    dve.scalar_tensor_tensor(pr, ps[:, 2:6, 0:nk], ATT_DIM ** -0.5, bias, ALU.mult, ALU.add
                                             ).then_inc(S("att_s"), 1)
                    dve.wait_ge(S("att_s"), i + 1)
                    chain(dve.tensor_reduce(col[:, c:c + 4], pr, AX.X, ALU.max))
                    dve.tensor_scalar(col[:, c + 4:c + 8], col[:, c:c + 4], -1.0, None, ALU.mult
                                      ).then_inc(S("att_nm"), 1)

                def normalise(i):
                    g, qb, nk, c, pr = unit(i)
                    dve.wait_ge(S("att_e"), 4 * i + 4)
                    chain(dve.reciprocal(col[:, c + 12:c + 16], col[:, c + 8:c + 12]))
                    dve.tensor_tensor(pr, pr, col[:, c + 12:c + 16].unsqueeze(2).to_broadcast([P, 4, nk]), ALU.mult
                                      ).then_inc(S("att_p"), 1)

                def lower(i):
                    g, qb, nk, c, pr = unit(i)
                    dve.wait_ge(S("x_hi"), X_LO_ATT + i + 1)
                    qc = slice(qb * P, (qb + 1) * P)
                    dve.tensor_tensor(X[0][:, 4 * g:4 * g + 4, 1, qc],
                                      ps[:, i % 2, :].rearrange("p (j q) -> p j q", j=4),
                                      X[0][:, 4 * g:4 * g + 4, 0, qc].bitcast(F32), ALU.subtract
                                      ).then_inc(S("x_lo"), 1)

                front(0)
                for i in range(len(UNITS)):
                    if i + 1 < len(UNITS):
                        front(i + 1)
                    normalise(i)
                    if i >= 1:
                        lower(i - 1)
                lower(len(UNITS) - 1)

            def cross(l):
                at, base = XQ_AT[l], 0

                def front(hd):
                    c = 16 * (hd % 2)
                    dve.wait_ge(S("xa_mm"), 4 * l + hd + 1)
                    b = XS_BANKS[hd % 2]
                    chain(dve.tensor_reduce(col[:, c:c + 4], ps[:, b:b + 2, :].rearrange("p a (b n) -> p (a b) n", b=2),
                                            AX.X, ALU.max))
                    dve.tensor_scalar(col[:, c + 4:c + 8], col[:, c:c + 4], -XA_DIM ** -0.5, None, ALU.mult
                                      ).then_inc(S("xa_nm"), 1)

                def normalise(hd):
                    c = 16 * (hd % 2)
                    pr = area(A_XP + (hd % 2) * 2 * T, 2 * T).rearrange("p (j n) -> p j n", j=4)
                    dve.wait_ge(S("xa_p"), 4 * l + hd + 1)
                    chain(dve.reciprocal(col[:, c + 12:c + 16], col[:, c + 8:c + 12]))
                    dve.tensor_tensor(pr, pr, col[:, c + 12:c + 16].unsqueeze(2).to_broadcast([P, 4, MEM]), ALU.mult
                                      ).then_inc(S("xa_pn"), 1)

                def lower(hd):
                    for dc in range(2):
                        lo_of(X[0][:, 2 * hd + dc, 1, :], ps[:, XO_BANKS[hd][dc], :], X[0][:, 2 * hd + dc, 0, :],
                              X_LO_XA[l] + 2 * hd + dc + 1)

                for t in range(8):
                    tile_out(at, t)
                    if t in (4, 6):
                        front((t - 4) // 2)
                normalise(0)
                front(2)
                normalise(1)
                lower(0)
                front(3)
                normalise(2)
                lower(1)
                normalise(3)
                lower(2)
                lower(3)

            dve.memset(ones[:], 1.0 / D).then_inc(S("ones_set"), 1)
            dve.memset(epsc[:, 0:1], EPS).then_inc(S("eps_set"), 1)
            dve.memset(epsc[:, 1:2], float(np.pi / 2)).then_inc(S("eps_set"), 1)
            norm(0, 1.0, None, (0,), None)
            ffn(0, lambda: memory_split(0))
            norm_after_ffn(1, 0)
            for t in range(4):
                tile_out(EV_AT, t)
            rstd_columns(0)
            s5_output_matrices()

            def ev_out(j):
                if 1 <= j <= 9:
                    tile_out(EV_AT, 3 + j)
                if j == 13:
                    dve.wait_ge(S("block_done"), EV_V_AT + 4)
                    for tt in range(4):
                        dve.tensor_scalar(val[:, tt, :], ps[:, BANKS[tt], :], col[:, 16 + tt:17 + tt], None, ALU.mult
                                          ).then_inc(S("gla_v"), 1)

            s5(ev_out)
            gla_decay()
            glu()
            gla()
            glu_split()
            norm_after_out(2, 0)
            cross(0)
            norm_after_out(3, 1)
            ffn(1, tables)
            norm_after_ffn(4, 1)
            ffn(2, lambda: memory_split(1))
            norm_after_ffn(5, 2)
            for t in range(OD_TILES):
                tile_out(OD_AT, t)
                if t >= 7:
                    for r in ([2 * (t - 7), 2 * (t - 7) + 1] if t < 13 else [t - 1]):
                        rope(r)
            rstd_columns(1)
            dve.wait_ge(S("block_done"), OD_V_AT + 2)
            for tt in range(4):
                dve.tensor_scalar(od_val[:, tt, :], ps[:, BANKS[tt], 0:2 * P], col[:, 16 + tt:17 + tt], None,
                                  ALU.mult).then_inc(S("od_v"), 1)
            indexer_weights()
            indexer()
            topk()
            attention()
            norm_after_out(6, 2)
            cross(1)
            norm_after_out(7, 3)
            ffn(3)
            norm_after_ffn(8, 3)
            for k in range(KC):
                dve.scalar_tensor_tensor(h[:, k, :], h[:, k, :], gain(8, k), rstd[:], ALU.mult, ALU.mult
                                         ).then_inc(S("y_ready"), 1)


def wide(w):
    k, n = w.shape
    return w.reshape(k // P, P, n // P, P).transpose(2, 1, 0, 3)


def rows_of(w, per):
    k, n = w.shape
    return w.reshape(k // P // per, per, P, n).transpose(0, 2, 1, 3)


def lay_out(inp):
    f = np.float32
    a = {k: np.asarray(v) for k, v in inp.items()}

    def chunks(m):
        return np.ascontiguousarray(m.T.reshape(KC, P, -1).transpose(1, 0, 2))

    def cols(v):
        return v.reshape(-1, P).T

    def pad(w):
        return np.concatenate([w, np.zeros((w.shape[0], P - w.shape[1]), f)], axis=1)

    blocks = []

    def add(b):
        blocks.append(b.reshape(b.shape[0], P, BLK))

    def ffn(name, l):
        gate, up = wide(a[f"{name}_w_gate"][l]), wide(a[f"{name}_w_up"][l])
        add(np.stack([gate, up], axis=1).reshape(2 * FC, P, KC, P))
        add(rows_of(a[f"{name}_w_down"][l], 1))

    def memory(l, glu=None):
        wk = wide(a["xa_wk"][l])
        if glu is not None:
            add(wk[:3])
            add(glu)
            wk = wk[3:]
        add(wk)
        wv = a["xa_wv"][l]
        for half in range(2):
            add(rows_of(wv[:, half * T:(half + 1) * T], 2))

    ev, od = a["ev_w_in"][0], a["od_w_in"][0]
    q, k, v, r, al, u = np.split(ev, np.cumsum([256, 256, 512, 512, 16]), axis=1)
    ffn("ffn1", 0)
    add(wide(np.concatenate([u, pad(al), q, k, r], axis=1)))
    add(rows_of(v, 2))
    memory(0, wide(a["s5_w_glu"][0]).reshape(2, 2, P, 4, P).transpose(0, 2, 1, 3, 4))
    add(wide(a["ev_w_out"][0]))
    add(wide(a["xa_wq"][0]))
    add(wide(a["xa_wo"][0]))
    ffn("ffn2", 0)
    ffn("ffn1", 1)
    q, k, v, qi, ki, wi = np.split(od, np.cumsum([1024, 256, 256, 512, 64]), axis=1)
    add(wide(np.concatenate([q, k, qi, ki, ki, pad(wi)], axis=1)))
    add(rows_of(v, 4))
    memory(1)
    add(wide(a["od_w_out"][0]))
    add(wide(a["xa_wq"][1]))
    add(wide(a["xa_wo"][1]))
    ffn("ffn2", 1)
    stream = np.concatenate(blocks, axis=0)
    assert stream.shape == (N_BLOCKS, P, BLK)

    norms = [a["ffn1_norm"][0], a["mix_norm"][0], a["xa_norm"][0], a["ffn2_norm"][0],
             a["ffn1_norm"][1], a["mix_norm"][1], a["xa_norm"][1], a["ffn2_norm"][1], a["final_norm"]]
    lane = np.arange(P)
    inv_a = (np.float32(10000.0) ** (-(2 * (lane % 64)).astype(f) / np.float32(128)))[:, None].astype(f)
    inv_i = (np.float32(10000.0) ** (-(2 * (lane % 32)).astype(f) / np.float32(64)))[:, None].astype(f)
    vecs = np.concatenate(
        [cols(n) for n in norms] + [cols(a["mem_norm"]), cols(a["gla_norm"][0]), cols(a["gla_b_alpha"][0]),
         cols(a["s5_D"][0].reshape(-1)), cols(a["s5_b_glu"][0]),
         cols(a["s5_lambda_re"][0].reshape(-1)), cols(a["s5_lambda_im"][0].reshape(-1)),
         cols(np.repeat(a["s5_log_dt"][0], 64)), inv_a, inv_i], axis=1)

    s5b = np.zeros((P, 2, 4, P), f)
    s5c = np.zeros((P, 2, S5_TILES, 32), f)
    for g in range(32):
        j, e = g // 2, g % 2
        p0 = 32 * (j % 4) + 16 * e
        for c, (b, cc) in enumerate((("s5_B_re", "s5_C_re"), ("s5_B_im", "s5_C_im"))):
            s5b[p0:p0 + 16, c, j // 4, 64 * e:64 * e + 64] = a[b][0, g].T
            s5c[64 * e:64 * e + 64, c, j, 16 * e:16 * e + 16] = a[cc][0, g].T

    mats = np.zeros((P, 4, P), f)
    mats[:, 0] = np.eye(P)
    for i, half in ((1, 64), (2, 32)):
        for m in range(P):
            low = m % (2 * half) < half
            mats[m + half if low else m - half, i, m] = -1.0 if low else 1.0
    mats[:, 3] = np.where(lane[None, :] <= lane[:, None], 0.0, MASKED)
    mask = ((lane[:, None] // 64 == lane[None, :] // 64) & (lane[:, None] <= lane[None, :])).astype(np.int32)
    rows = np.stack([np.arange(T), np.arange(T) % GLA_CHUNK != 0]).astype(f)
    return {
        "xT": chunks(a["x"][0]), "memT": chunks(a["mem"][0]), "pos": a["positions"],
        "vecs": vecs, "w_alpha": a["gla_w_alpha"][0], "s5b": s5b, "s5c": s5c, "mats": mats,
        "mask": mask, "rows": rows, "stream": stream,
    }


def kernel(**inputs):
    import concourse.bacc as bacc
    from concourse.bass_utils import run_bass_kernel_spmd as run

    nc = bacc.Bacc("TRN2", target_bir_lowering=False, num_devices=1)
    arrays, args = {}, []
    for name, a in lay_out(inputs).items():
        a = np.ascontiguousarray(a)
        arrays[f"in_{name}"] = a
        args.append(nc.dram_tensor(f"in_{name}", a.shape, mybir.dt.from_np(a.dtype), kind="ExternalInput").ap())
    args.append(nc.dram_tensor("out_0", (P, KC, T), F32, kind="ExternalOutput").ap())
    build_trunk(nc, *args)
    r = run(nc, [arrays], core_ids=[0])
    got = r.results[0]["out_0"]
    return np.ascontiguousarray(got.transpose(2, 1, 0).reshape(1, T, D))
```

```python
from contextlib import ExitStack

import numpy as np

import concourse.bass as bass
from concourse import mybir

F32 = mybir.dt.float32
F32R = mybir.dt.float32r
I32 = mybir.dt.int32
ALU = mybir.AluOpType
ACT = mybir.ActivationFunctionType
AX = mybir.AxisListType

P = 128
T = 512
D = 1024
KC = D // P
MEM = 256
FF = 2816
FC = FF // P
EPS = 1e-6
BLK = 1024
HALF = BLK // 2
MAGIC = 12582912.0
TWO_PI_BELOW = 6.2831845
PI_BELOW = 3.1415925
TWO_PI_1, TWO_PI_2, TWO_PI_3 = 6.28125, 0.0019350051879882812, 3.0199159819e-07

GLA_HEADS, GLA_DK, GLA_DV, GLA_CHUNK, GLA_TAU = 4, 64, 128, 64, 16.0
NCH = T // GLA_CHUNK
S5_TILES = 16
QB = T // P
TOPK = 128
IDX_HEADS, IDX_DIM = 8, 64
ATT_HEADS, ATT_DIM = 8, 128
XA_HEADS, XA_DIM = 4, 256
MASKED = -1.0e30
TAKEN = -3.0e38

XS_BANKS = [0, 6]
XO_BANKS = [(2, 4)] * 3 + [(6, 7)]

FFN_BLOCKS = 3 * FC
FFN_AT = [0, 125, 191, 315]
EV_AT, EV_TILES = 66, 13
EV_V_AT = 79
EARLY_KEYS = 5
GLU_AT = 83 + EARLY_KEYS


def kv_block(l, t):
    return 275 + t if l else 83 + t + (2 if t >= EARLY_KEYS else 0)


OUT_AT = [101, 117, 291, 307]
XQ_AT = [109, 299]
LONE = XQ_AT[0] - 1
OD_AT, OD_TILES = 257, 16
OD_V_AT = 273
N_BLOCKS = 381

BANKS = [2, 4, 3, 5]
DOWN_BANKS = [0, 2, 4, 3, 5, 6, 7, 1]
DOWN_FIRST = [5, 6, 7, 0, 1, 2, 3, 4]
SSQ_BANK = 0
GLU_BANKS = [0, 1, 6, 7]
KV_BANKS = [3, 5]

NORM_TO = [0, 1, 1, 1, 0, 1, 1, 1]
FFN_NORM = [0, 3, 4, 7]

OUT_NORM = [2, 3, 6, 7]
XQ_BASE, OD_BASE = [13, 37], 21

_SPLITS = [("n0", 8), ("h0", FC), ("n1", 8), ("y", 4), ("gla", 4), ("glu", 4), ("n2", 8), ("xa0", 8),
           ("n3", 8), ("h1", FC), ("n4", 8), ("h2", FC), ("n5", 8), ("att", 8), ("n6", 8), ("xa1", 8),
           ("n7", 8), ("h3", FC)]
BEFORE = {name: sum(n for _, n in _SPLITS[:i]) for i, (name, _) in enumerate(_SPLITS)}
X_LO_NORM = [BEFORE[f"n{i}"] for i in range(8)]
X_LO_HID = [BEFORE[f"h{i}"] for i in range(4)]
X_LO_GLA, X_LO_Y, X_LO_GLU, X_LO_ATT = (BEFORE[i] for i in ("gla", "y", "glu", "att"))
X_LO_XA = [BEFORE["xa0"], BEFORE["xa1"]]

ROPE_TILES = range(15)
UNITS = [(g, qb) for qb in (0, 3, 2, 1) for g in range(2)]
KEPT = [1, 3, 5]
SPLIT_ORDER = [0, 2, 4, 1, 3, 5, 6, 7]
UNIT_TR = [sum(qb + 1 for _, qb in UNITS[:i + 1]) for i in range(len(UNITS))]

V_GAIN = 0
V_MEMG = 72
V_GLAN = 80
V_BALPHA = 81
V_D = 83
V_BGLU = 87
V_LRE, V_LIM, V_LDT = 91, 107, 123
V_INVA, V_INVI = 139, 140
NV = 141
C_MAG, C_PH, C_PL, C_FR, C_FI = [16 * i for i in range(5)]

A_TIME = FC * T
A_MEM = 27 * T
ARENA = 31 * T
A_V = EV_TILES * T
A_S5X = A_V + 4 * T
A_S5T = A_TIME + T
A_BC = A_V + 4 * T
A_KINV = A_BC + 2 * T
A_KENDT = A_KINV + 2 * T
A_S = A_KENDT + 2 * T
A_O = A_S + 4 * T
A_ODV = OD_TILES * T
A_SC = A_ODV + 2 * T
A_TAB = FC * T
A_POS = A_TAB + 4 * T
A_P = A_TAB + 4 * T
A_P1 = A_TAB
A_KEPT = [14 * T, 15 * T, 30 * T]
A_PT = 10 * T
A_XP = 8 * T
A_XPT = A_XP + 4 * T


def build_trunk(nc, xT, memT, pos, vecs, w_alpha, s5b, s5c, mats, mask, rows, stream, out):
    with ExitStack() as ctx:
        def sb(name, shape, dt=F32):
            return ctx.enter_context(nc.sbuf_tensor(name, shape, dt))

        sems = {}

        def S(name):
            if name not in sems:
                sems[name] = ctx.enter_context(nc.semaphore(name))
            return sems[name]

        ps = ctx.enter_context(nc.psum_tensor("ps", [P, 8, T], F32))
        h = sb("h", [P, KC, T])
        X = [sb(f"x{i}", [P, KC, 2, T], F32R) for i in range(2)]
        W = sb("w_split", [P, 2, 2, BLK], F32R)
        raw = sb("w_raw", [P, 2, BLK])
        kv = sb("kv", [P, 8 * T])
        ar = sb("arena", [P, ARENA])
        tg = sb("tg", [P, 2, T])
        tu = sb("tu", [P, 2, T])
        sg = sb("sg", [P, 2, T])
        sq = sb("sq", [P, 2, T])
        rstd = sb("rstd", [P, T])
        std = sb("std", [P, T])
        vec = sb("vec", [P, NV])
        mat = sb("mat", [P, 4, P])
        msk = sb("msk", [P, P], I32)
        ones = sb("ones", [P, P])
        sc5 = sb("sc5", [P, 80])
        tiny = sb("tiny", [P, 12, 16])
        col = sb("col", [P, 64])
        epsc = sb("epsc", [P, 2])

        s5_tables = nc.dram_tensor("s5_tables", (S5_TILES, P, 2 * T), F32, kind="Internal").ap()
        ident = mat[:, 0, :]
        cmask = mat[:, 3, :]
        gate = sb("gate", [P, 2])
        tiny_i = sb("tiny_i", [P, 16], I32)
        Pt = [ar[:, i * T:(i + 1) * T] for i in range(16)]
        KT = kv[:, 0:4 * T].rearrange("p (n m) -> p n m", m=MEM)
        VM = kv[:, 4 * T:8 * T].rearrange("p (t d) -> p t d", t=2)
        hid = ar[:, 0:FC * T].rearrange("p (k t) -> p k t", t=T)
        memX = X[0][:, 4:8, :, :].rearrange("p a b t -> p (a b t)").rearrange(
            "p (k s m) -> p k s m", k=KC, s=2)

        def area(at, n=T):
            return ar[:, at:at + n]

        val = area(A_V, 4 * T).rearrange("p (t d) -> p t d", t=4)
        kend_t = area(A_KENDT, 2 * T).rearrange("p (t q f) -> p t q f", t=4, q=2)
        state = area(A_S, 4 * T).rearrange("p (q c e) -> p q c e", q=2, c=NCH)
        wal = kv[0:16, 2 * T:2 * T + 2 * P]
        chunk_mask = kv[:, 3 * T:4 * T]
        s5ct = kv[:, 4 * T:6 * T].rearrange("p (c j o) -> p c j o", c=2, j=16)
        s5bt = kv[:, 6 * T:8 * T].rearrange("p (c q s) -> p c q s", c=2, q=4)
        od_val = area(A_ODV, 2 * T).rearrange("p (t d) -> p t d", t=4)

        def gain(n, k):
            return vec[:, V_GAIN + 8 * n + k:V_GAIN + 8 * n + k + 1]

        split_ready = S("split_ready")

        block = ctx.enter_context(nc.Block())

        @block.sync
        def _(sp):
            def load(b, s, half):
                c = slice(half * HALF, (half + 1) * HALF)
                src = stream[b] if isinstance(b, int) else stream[bass.ds(b, 1)].rearrange("a p n -> p (a n)")
                sp.dma_start(raw[:, s, c], src[:, c]).then_inc(S(f"raw{s}{'ab'[half]}"), 16)

            def reload(b, s, half):
                sp.wait_ge(split_ready if half else S("half_split"), b - 1)
                load(b, s, half)

            load(0, 0, 0)
            sp.dma_start(h[:, 0:2, :], xT[:, 0:2, :]).then_inc(S("x_in0"), 16)
            sp.dma_start(vec[:], vecs).then_inc(S("vec_in"), 16)
            load(1, 1, 0)
            load(0, 0, 1)
            load(1, 1, 1)
            sp.dma_start(h[:, 2:8, :], xT[:, 2:8, :]).then_inc(S("x_in1"), 16)
            sp.dma_start(mat[:], mats).then_inc(S("mat_in"), 16)
            sp.dma_start(msk[:], mask).then_inc(S("msk_in"), 16)
            sp.dma_start(area(A_MEM, 4 * T).rearrange("p (k m) -> p k m", m=MEM), memT).then_inc(S("mem_in0"), 16)
            sp.dma_start(area(A_TIME), rows[0:1, :].to_broadcast([P, T])).then_inc(S("time_in"), 16)
            with sp.Fori(1, LONE // 2) as i:
                for half in range(2):
                    for e in range(2):
                        reload(i * 2 + e, e, half)
            for half in range(2):
                reload(LONE, 0, half)
            with sp.Fori(LONE // 2, N_BLOCKS // 2) as i:
                for half in range(2):
                    for e in range(2):
                        reload(i * 2 + (e + 1), 1 - e, half)

        @block.gpsimd
        def _(pool):
            def split(b, s, half, count, first=False):
                c = slice(half * HALF, (half + 1) * HALF)
                pool.wait_ge(S(f"raw{s}{'ab'[half]}"), count * 16)
                if not first:
                    pool.wait_ge(S("block_done") if half else S("half_done"), b - 1)
                    pool.tensor_tensor(gate[:, 0:1], gate[:, 1:2], gate[:, 1:2], ALU.add)
                pool.tensor_scalar(W[:, s, 0, c], raw[:, s, c], 1.0, 0.0, ALU.mult, ALU.add
                                   ).then_inc(S(f"w_hi{'ab'[half]}"), 1)
                pool.wait_ge(S(f"w_hi{'ab'[half]}"), b + 1)
                pool.tensor_tensor(W[:, s, 1, c], raw[:, s, c], W[:, s, 0, c].bitcast(F32), ALU.subtract
                                   ).then_inc(split_ready if half else S("half_split"), 1)

            pool.memset(gate[:], 0.0).then_inc(S("gate_set"), 1)
            pool.wait_ge(S("gate_set"), 1)
            for half in range(2):
                for e in range(2):
                    split(e, e, half, 1, first=True)
            with pool.Fori(1, LONE // 2) as i:
                for half in range(2):
                    for e in range(2):
                        split(i * 2 + e, e, half, i + 1)
            for half in range(2):
                split(LONE, 0, half, LONE // 2 + 1)
            with pool.Fori(LONE // 2, N_BLOCKS // 2) as i:
                for half in range(2):
                    for e in range(2):
                        split(i * 2 + (e + 1), 1 - e, half, i + (e + 1))

        @block.tensor
        def _(pe):
            def mm3(dst, wh, wl, xh, xl, start, stop):
                pe.matmul(dst, wh, xh, start=start, stop=False)
                pe.matmul(dst, wh, xl, start=False, stop=False)
                return pe.matmul(dst, wl, xh, start=False, stop=stop)

            def tile_k(bank, slot, x, k, start, stop):
                c = slice(k * P, (k + 1) * P)
                return mm3(ps[:, bank, :], W[:, slot, 0, c], W[:, slot, 1, c],
                           X[x][:, k, 0, :], X[x][:, k, 1, :], start, stop)

            def mean_square(n):
                pe.wait_ge(S("sq_added"), 8 * n + 8)
                pe.wait_ge(*((S("ones_set"), 1) if n == 0 else (S("std_ready"), n)))
                pe.matmul(ps[:, SSQ_BANK, :], ones[:], tg[:, 0, :], start=True, stop=True
                          ).then_inc(S("ssq_done"), 1)

            def tile(b, t, x, free=None):
                slot, bank = t
                pe.wait_ge(S("half_split"), b + 1)
                if free is not None:
                    pe.wait_ge(*free)
                for k in range(KC):
                    if k == KC // 2:
                        m.then_inc(S("half_done"), 1)
                        pe.wait_ge(split_ready, b + 1)
                    m = tile_k(bank, slot, x, k, k == 0, k == KC - 1)
                m.then_inc(S("block_done"), 1)

            def project(n, at, nt, x, free_sem, free_base, per, waits0, waits1, between=None):
                pe.wait_ge(S("half_split"), at + 2)
                for s, v in waits0:
                    pe.wait_ge(s, v)
                for k in range(KC):
                    if k == KC // 2:
                        pe.wait_ge(split_ready, at + 2)
                    pe.wait_ge(S("x_lo"), X_LO_NORM[n] + k + 1)
                    for t in range(min(2, nt)):
                        m = tile_k(BANKS[t], (at + t) % 2, x, k, k == 0, k == KC - 1)
                        if k == KC // 2 - 1:
                            m.then_inc(S("half_done"), 1)
                        if k == KC - 1:
                            m.then_inc(S("block_done"), 1)
                mean_square(n)
                for s, v in waits1:
                    pe.wait_ge(s, v)
                for t in (2, 3):
                    tile(at + t, ((at + t) % 2, BANKS[t]), x)
                full, first = (nt - 4) // 4, 1
                if between is not None:
                    for t in range(4, 8):
                        tile(at + t, ((at + t) % 2, BANKS[t % 4]), x, (free_sem, free_base + t // 2 - 1))
                    between()
                    first = 2
                if full >= 1:
                    with pe.Fori(first, 1 + full) as i:
                        for t in range(4):
                            need = (i * 2 + (t // 2 - 1) if per == 2 else i * 4 + (t - 3)) + free_base
                            tile(i * 4 + (at + t), ((at + t) % 2, BANKS[t]), x, (free_sem, need))
                for t in range(4 + 4 * full, nt):
                    tile(at + t, ((at + t) % 2, BANKS[t % 4]), x, (free_sem, free_base + t - 3))

            def ffn(f):
                n, at = FFN_NORM[f], FFN_AT[f]
                x, xo = NORM_TO[n], 1 - NORM_TO[n]
                w0 = [(S("h_ready"), 8 * (n - 1) + (3 if f == 2 else 6))] if n else []
                w1 = [(S("h_ready"), 8 * n)] if n else []
                project(n, at, 2 * FC, x, S("hid_done"), FC * f, 2, w0, w1,
                        (lambda: memory_norm(f // 2)) if f % 2 == 0 else None)
                dn = at + 2 * FC

                def down_k(slot, d4, b, nn, start, stop):
                    at = DOWN_FIRST.index(nn) if start else nn
                    c = slice(at * P, (at + 1) * P)
                    ch = [6, 7, 4, 5][d4]
                    return mm3(ps[:, DOWN_BANKS[nn], :], W[:, slot, 0, c], W[:, slot, 1, c],
                               X[xo][:, ch, 0, :], X[xo][:, ch, 1, :], start, stop)

                def down(b, slot, d4, lo, first):
                    pe.wait_ge(S("half_split"), b + 1)
                    pe.wait_ge(S("x_lo"), lo)
                    for i, nn in enumerate(DOWN_FIRST if first else range(8)):
                        if i == 4:
                            m.then_inc(S("half_done"), 1)
                            pe.wait_ge(split_ready, b + 1)
                        if first and nn == 0:
                            pe.wait_ge(S("std_ready"), n + 1)
                        if first and nn == 1:
                            pe.wait_ge(S("hid_done"), FC * (f + 1))
                        m = down_k(slot, d4, b, nn, first, False)
                    m.then_inc(S("block_done"), 1)

                lo0 = X_LO_HID[f]
                for d in range(4):
                    down(dn + d, (dn + d) % 2, d, lo0 + d + 1, d == 0)
                with pe.Fori(1, 5) as i:
                    for s in range(4):
                        down(i * 4 + (dn + s), (dn + s) % 2, s, i * 4 + (lo0 + s + 1), False)
                pe.wait_ge(S("half_split"), dn + FC)
                pe.wait_ge(S("x_lo"), lo0 + FC)
                for nn in range(8):
                    if nn == 4:
                        pe.wait_ge(split_ready, dn + FC)
                    m = down_k((dn + 20) % 2, 0, 0, nn, False, False)
                    if nn in (3, 4):
                        m.then_inc(S("half_done"), 1)
                    if nn == 7:
                        m.then_inc(S("block_done"), 1)
                    m = down_k((dn + 21) % 2, 1, 0, nn, False, True)
                    m.then_inc(S("down_out") if nn < 7 else S("block_done"), 1)

            def out_proj(o, lo, n_prev_free):
                at, n = OUT_AT[o], OUT_NORM[o]
                for s, v in n_prev_free:
                    pe.wait_ge(s, v)
                for t in range(8):
                    pe.wait_ge(S("half_split"), at + t + 1)
                    if t >= 4:
                        pe.wait_ge(S("h_ready"), 8 * (n - 1) + t - 3)
                    for k in range(KC):
                        if k == KC // 2:
                            m.then_inc(S("half_done"), 1)
                            pe.wait_ge(split_ready, at + t + 1)
                        if t == 0:
                            pe.wait_ge(S("x_lo"), lo[k])
                        m = tile_k(BANKS[t % 4], (at + t) % 2, 0, k, k == 0, k == KC - 1)
                    m.then_inc(S("block_done"), 1)

            def memory_norm(l):
                for k in range(KC):
                    pe.wait_ge(S("msq_ready"), 8 * l + k + 1)
                    pe.matmul(ps[:, 1, 0:MEM], ones[:], sq[:, k % 2, 0:MEM], start=(k == 0), stop=(k == 7)
                              ).then_inc(S("mssq_done"), 1)

            def kv_tile(l, t, banks):
                b = kv_block(l, t)
                if t == 0:
                    pe.wait_ge(S("mem_lo"), 8 * l + 8)
                pe.wait_ge(S("half_split"), b + 1)
                if t < 8:
                    if t >= len(banks):
                        pe.wait_ge(S("kv_out"), 12 * l + t + 1 - len(banks))
                    for k in range(KC):
                        if k == KC // 2:
                            m.then_inc(S("half_done"), 1)
                            pe.wait_ge(split_ready, b + 1)
                        c = slice(k * P, (k + 1) * P)
                        m = mm3(ps[:, banks[t % len(banks)], 0:MEM], W[:, b % 2, 0, c], W[:, b % 2, 1, c],
                                memX[:, k, 0, :], memX[:, k, 1, :], k == 0, k == 7)
                else:
                    quarter, q = (t - 8) // 2, t % 2
                    if q == 0:
                        pe.wait_ge(S("kv_out"), 12 * l + 9 + quarter - len(banks))
                    for kk in range(4):
                        if kk == 2:
                            m.then_inc(S("half_done"), 1)
                            pe.wait_ge(split_ready, b + 1)
                        k = 4 * q + kk
                        wc = slice(kk * MEM, (kk + 1) * MEM)
                        for mt in range(2):
                            mc = slice(mt * P, (mt + 1) * P)
                            m = mm3(ps[:, banks[quarter % len(banks)], mt * MEM:(mt + 1) * MEM],
                                    memX[:, k, 0, mc], memX[:, k, 1, mc],
                                    W[:, b % 2, 0, wc], W[:, b % 2, 1, wc], k == 0 and mt == 0, k == 7 and mt == 1)
                m.then_inc(S("block_done"), 1)

            def values(at, q, width):
                per = BLK // width
                b = at + q
                pe.wait_ge(S("half_split"), b + 1)
                for kk in range(per):
                    if kk == per // 2:
                        m.then_inc(S("half_done"), 1)
                        pe.wait_ge(split_ready, b + 1)
                    k = q * per + kk
                    for tt in range(4):
                        tc = slice(tt * P, (tt + 1) * P)
                        wc = slice(kk * width, (kk + 1) * width)
                        m = mm3(ps[:, BANKS[tt], 0:width], X[1][:, k, 0, tc], X[1][:, k, 1, tc],
                                W[:, b % 2, 0, wc], W[:, b % 2, 1, wc], k == 0, k == 7)
                m.then_inc(S("block_done"), 1)

            def rstd_columns(l):
                pe.wait_ge(S("rstd_ready"), [2, 6][l])
                if l == 0:
                    pe.wait_ge(S("mat_in"), 16)
                for tt in range(4):
                    m = pe.transpose(ps[:, 1, tt * P:(tt + 1) * P], rstd[:, tt * P:(tt + 1) * P], ident)
                m.then_inc(S("rcol_mm"), 1)

            def gla_alpha():
                pe.wait_ge(S("proj_out"), 5)
                pe.wait_ge(S("wal_in"), 16)
                pe.wait_ge(S("gla_v"), 4)
                for p in range(2):
                    m = pe.matmul(ps[:, BANKS[p], :], wal[:, p * P:(p + 1) * P], Pt[4][0:16, :],
                                  start=True, stop=True)
                m.then_inc(S("alpha_mm"), 1)

            def gla(fill):
                fill(3)
                pe.wait_ge(S("kend"), 2)
                pe.wait_ge(S("glu_sig"), 4)
                for p in range(2):
                    for tt in range(4):
                        m = pe.transpose(ps[:, 6 + p, tt * P:(tt + 1) * P],
                                         Pt[7 + p][:, tt * P:(tt + 1) * P], ident)
                m.then_inc(S("kend_tr"), 1)
                pe.wait_ge(S("kend_t"), 2)
                pe.wait_ge(S("gla_v"), 4)
                for c in range(NCH - 1):
                    if c >= 2:
                        pe.wait_ge(S("state"), 4 * (c - 1))
                    r = slice(64 * (c % 2), 64 * (c % 2) + 64)
                    for p in range(2):
                        m = pe.matmul(ps[:, BANKS[c % 2], p * 256:(p + 1) * 256],
                                      kend_t[r, c // 2, p, :], val[r, c // 2, p * 256:(p + 1) * 256],
                                      start=True, stop=True)
                    m.then_inc(S("state_mm"), 1)
                    if c in (2, 5):
                        fill(1)
                pe.wait_ge(S("qdec"), 2)
                pe.wait_ge(S("kinv"), 2)

                def scores(hd):
                    p, r = hd // 2, slice(64 * (hd % 2), 64 * (hd % 2) + 64)
                    if hd >= 2:
                        pe.wait_ge(S("gscore"), hd - 1)
                    for tt in range(4):
                        tc = slice(tt * P, (tt + 1) * P)
                        m = pe.matmul(ps[:, 6 + hd % 2, tc], area(A_KINV + p * T)[r, tc], Pt[5 + p][r, tc],
                                      start=True, stop=True)
                    m.then_inc(S("gscore_mm"), 1)

                scores(0)
                fill(1)
                pe.wait_ge(S("state"), 4 * (NCH - 1))
                for hd in range(4):
                    if hd < 3:
                        scores(hd + 1)
                    if hd >= 2:
                        pe.wait_ge(S("gla_o"), hd - 1)
                    p, r = hd // 2, slice(64 * (hd % 2), 64 * (hd % 2) + 64)
                    pe.wait_ge(S("gscore"), hd + 1)
                    for tt in range(4):
                        dst = ps[:, BANKS[hd % 2], tt * P:(tt + 1) * P]
                        pe.matmul(dst, val[:, tt, hd * P:(hd + 1) * P], tg[:, hd % 2, tt * P:(tt + 1) * P],
                                  start=True, stop=False)
                        for c in (2 * tt, 2 * tt + 1):
                            if c == 0:
                                continue
                            cc = slice(c * 64, (c + 1) * 64)
                            m = pe.matmul(ps[:, BANKS[hd % 2], cc], state[r, p, c, :], Pt[5 + p][r, cc],
                                          start=False, stop=(c % 2 == 1))
                    m.then_inc(S("go_mm"), 1)
                    pe.wait_ge(S("gsq"), hd + 1)
                    if hd >= 2:
                        pe.wait_ge(S("gstd"), hd - 1)
                    pe.matmul(ps[:, hd % 2, :], ones[:], sq[:, hd % 2, :], start=True, stop=True
                              ).then_inc(S("gms_mm"), 1)
                    fill(2)

            def s5(fill):
                def inputs(j):
                    q, r = j // 4, slice(32 * (j % 4), 32 * (j % 4) + 32)
                    if j == 0:
                        pe.wait_ge(S("s5b_in"), 16)
                        pe.wait_ge(S("rcol_ready"), 1)
                    if j % 4 == 0:
                        pe.wait_ge(S("proj_out"), q + 1)
                    if j >= 1:
                        pe.wait_ge(S("s5_read"), j)
                    for c in range(2):
                        m = pe.matmul(ps[:, c, :], s5bt[r, c, q, :], Pt[q][r, :], start=True, stop=True)
                    m.then_inc(S("s5_in_mm"), 1)

                def outputs(j):
                    q, r = j // 4, slice(32 * (j % 4), 32 * (j % 4) + 32)
                    if j == 0:
                        pe.wait_ge(S("s5_c"), 2)
                    if j % 4 == 0 and q >= 2:
                        pe.wait_ge(S("s5_y"), q - 1)
                    pe.wait_ge(S("s5_xi"), j + 1)
                    x = A_S5X + (j % 2) * 2 * T
                    pe.matmul(ps[r, 6 + q % 2, :], s5ct[:, 0, j, :], area(x), start=True, stop=False)
                    pe.matmul(ps[r, 6 + q % 2, :], s5ct[:, 1, j, :], area(x + T), start=False, stop=True
                              ).then_inc(S("s5_out_mm"), 1)

                inputs(0)
                for j in range(S5_TILES):
                    fill(j)
                    if j + 1 < S5_TILES:
                        inputs(j + 1)
                    outputs(j)

            def glu():
                for n in range(4):
                    pe.wait_ge(S("half_split") if n % 2 == 0 else split_ready, GLU_AT + n // 2 + 1)
                    for k in range(4):
                        if n == 0:
                            pe.wait_ge(S("x_lo"), X_LO_Y + k + 1)
                        b = GLU_AT + n // 2
                        c = slice(((n % 2) * 4 + k) * P, ((n % 2) * 4 + k + 1) * P)
                        m = mm3(ps[:, GLU_BANKS[n], :], W[:, b % 2, 0, c], W[:, b % 2, 1, c],
                                X[1][:, k, 0, :], X[1][:, k, 1, :], k == 0, k == 3)
                    m.then_inc(S("half_done") if n % 2 == 0 else S("block_done"), 1)

            def rope(t):
                pe.wait_ge(S("proj_out"), OD_BASE + t + 1)
                if t == 0:
                    pe.wait_ge(S("kv_out"), 12)
                if t >= 2:
                    pe.wait_ge(S("rope_s"), t - 1)
                pe.matmul(ps[:, 6 + t % 2, :], mat[:, 1 if t < 10 else 2, :], Pt[t], start=True, stop=True
                          ).then_inc(S("rope_mm"), 1)

            def indexer_weights():
                pe.wait_ge(S("rcol_ready"), 2)
                pe.wait_ge(S("proj_out"), OD_BASE + 16)
                for tt in range(4):
                    m = pe.transpose(ps[:, 1, tt * P:(tt + 1) * P], Pt[15][:, tt * P:(tt + 1) * P], ident)
                m.then_inc(S("wi_mm"), 1)

            def indexer(fill):
                pe.wait_ge(S("rope_done"), len(ROPE_TILES))
                pe.wait_ge(S("od_v"), 4)
                i = 0
                for qb in range(1, QB):
                    nk = (qb + 1) * P
                    for hd in range(IDX_HEADS):
                        r = slice(64 * (hd % 2), 64 * (hd % 2) + 64)
                        if i >= 4:
                            pe.wait_ge(S("relu"), i - 3)
                        pe.matmul(ps[:, BANKS[i % 4], 0:nk], Pt[10 + hd // 2][r, qb * P:(qb + 1) * P],
                                  Pt[14][r, 0:nk], start=True, stop=True).then_inc(S("logit_mm"), 1)
                        i += 1
                        if hd == 3:
                            fill(1)

            def attention(fill):
                def scores(i):
                    g, qb = UNITS[i]
                    nk = (qb + 1) * P
                    if i == 0:
                        pe.wait_ge(S("relu"), 24)
                    else:
                        pe.wait_ge(S("att_s"), i)
                    for j in range(4):
                        m = pe.matmul(ps[:, 2 + j, 0:nk], Pt[4 * g + j][:, qb * P:(qb + 1) * P],
                                      Pt[8 + g][:, 0:nk], start=True, stop=True)
                    m.then_inc(S("att_mm"), 1)

                nt = 0
                scores(0)
                fill(2)
                for i, (g, qb) in enumerate(UNITS):
                    if i + 1 < len(UNITS):
                        scores(i + 1)
                    fill(1)
                    pe.wait_ge(S("att_p"), i + 1)
                    pb = A_P if i % 2 == 0 else A_P1
                    for kc in range(qb + 1):
                        if nt >= 2:
                            pe.wait_ge(S("att_t"), nt - 1)
                        for j in range(4):
                            m = pe.transpose(ps[:, 6 + nt % 2, j * P:(j + 1) * P],
                                             area(pb + j * T)[:, kc * P:(kc + 1) * P], ident)
                        m.then_inc(S("att_tr"), 1)
                        nt += 1
                    if i < 6:
                        fill(1)
                    if i - 1 in KEPT:
                        pe.wait_ge(S("att_kept"), KEPT.index(i - 1) + 1)
                    elif i >= 1:
                        pe.wait_ge(S("x_lo"), X_LO_ATT + SPLIT_ORDER.index(i - 1) + 1)
                    pe.wait_ge(S("att_t"), nt)
                    for kc in range(qb + 1):
                        m = pe.matmul(ps[:, 0, :], od_val[:, kc, g * P:(g + 1) * P],
                                      area(A_PT + kc * T), start=(kc == 0), stop=(kc == qb))
                    m.then_inc(S("att_o"), 1)

            def cross(l, n, waits0, waits1):
                base, at = XQ_BASE[l], XQ_AT[l]

                def scores(hd):
                    pe.wait_ge(S("proj_out"), base + 2 * hd + 2)
                    if hd == 0:
                        pe.wait_ge(S("kv_out"), 12 * (l + 1))
                        pe.wait_ge(S("std_ready"), n + 1)
                    if hd >= 2:
                        pe.wait_ge(S("xa_p"), 4 * l + hd - 1)
                    for qb in range(QB):
                        for c in range(2):
                            m = pe.matmul(ps[:, XS_BANKS[hd % 2] + qb // 2, (qb % 2) * MEM:(qb % 2 + 1) * MEM],
                                          Pt[2 * hd + c][:, qb * P:(qb + 1) * P], KT[:, 2 * hd + c, :],
                                          start=(c == 0), stop=(c == 1))
                    m.then_inc(S("xa_mm"), 1)

                def turn(hd):
                    pe.wait_ge(S("xa_pn"), 4 * l + hd + 1)
                    if hd >= 1:
                        pe.wait_ge(S("xa_t"), 8 * l + 2 * hd)
                    pb = A_XP + (hd % 2) * 2 * T
                    for mc in range(2):
                        for qb in range(QB):
                            m = pe.transpose(ps[:, BANKS[2 + mc], qb * P:(qb + 1) * P],
                                             area(pb + qb * MEM)[:, mc * P:(mc + 1) * P], ident)
                        m.then_inc(S("xa_tr"), 1)

                def outputs(hd):
                    pe.wait_ge(S("xa_t"), 8 * l + 2 * hd + 2)
                    for dc in range(2):
                        if 1 <= hd <= 2:
                            pe.wait_ge(S("x_lo"), X_LO_XA[l] + 2 * (hd - 1) + dc + 1)
                        ch = 2 * hd + dc
                        for mc in range(2):
                            m = pe.matmul(ps[:, XO_BANKS[hd][dc], :], VM[:, mc, ch * P:(ch + 1) * P],
                                          area(A_XPT + (hd % 2) * 2 * T + mc * T), start=(mc == 0), stop=(mc == 1))
                        m.then_inc(S("xa_o"), 1)

                project(n, at, 4, 1, S("proj_out"), base, 1, waits0, waits1)
                for t in range(4, 8):
                    if t in (4, 6):
                        scores((t - 4) // 2)
                    tile(at + t, ((at + t) % 2, BANKS[t % 4]), 1, (S("proj_out"), base + t - 3))
                pe.wait_ge(S("proj_out"), base + 8)
                turn(0)
                scores(2)
                outputs(0)
                turn(1)
                scores(3)
                outputs(1)
                for hd in (2, 3):
                    turn(hd)
                    outputs(hd)

            def ev_fill(j):
                if j < 9:
                    t = 4 + j
                    tile(EV_AT + t, ((EV_AT + t) % 2, BANKS[t % 4]), 1, (S("proj_out"), t - 3))
                elif j < 13:
                    if j == 9:
                        pe.wait_ge(S("proj_out"), 13)
                    values(EV_V_AT, j - 9, T)
                else:
                    if j == 13:
                        gla_alpha()
                    for t in ([0], [1, 2], [3, 4])[j - 13]:
                        kv_tile(0, t, KV_BANKS)

            kv_at = [EARLY_KEYS]

            def gla_fill(n):
                for _ in range(n):
                    if kv_at[0] < 16:
                        kv_tile(0, kv_at[0], KV_BANKS)
                        kv_at[0] += 1

            ffn(0)
            project(1, EV_AT, 4, 1, S("proj_out"), 0, 1,
                    [(S("h_ready"), 3)], [(S("h_ready"), 8)])
            rstd_columns(0)
            s5(ev_fill)
            glu()
            gla(gla_fill)
            gla_fill(16)
            out_proj(0, [X_LO_GLA + k + 1 for k in range(4)] + [X_LO_GLU + k + 1 for k in range(4)], [])
            cross(0, 2, [(S("h_ready"), 14)], [(S("h_ready"), 16)])
            out_proj(1, [X_LO_XA[0] + max(k + 1, 6) for k in range(8)], [])
            ffn(1)
            ffn(2)
            project(5, OD_AT, 4, 1, S("proj_out"), OD_BASE, 1,
                    [(S("h_ready"), 35)], [(S("h_ready"), 40)])
            for t in range(4, OD_TILES):
                tile(OD_AT + t, ((OD_AT + t) % 2, BANKS[t % 4]), 1, (S("proj_out"), OD_BASE + t - 3))
                if t >= 7:
                    for r in ([2 * (t - 7), 2 * (t - 7) + 1] if t < 13 else [t - 1]):
                        rope(r)
            rstd_columns(1)
            pe.wait_ge(S("proj_out"), OD_BASE + 16)
            for q in range(2):
                values(OD_V_AT, q, 2 * P)
            indexer_weights()
            kv_at[0] = 0

            def od_fill(n):
                if kv_at[0] == 0:
                    pe.wait_ge(S("wi_ready"), 1)
                for _ in range(n):
                    if kv_at[0] < 16:
                        kv_tile(1, kv_at[0], [1])
                        kv_at[0] += 1

            indexer(od_fill)
            attention(od_fill)
            out_proj(2, [X_LO_ATT + 8] * 8, [(S("att_s"), 8)])
            cross(1, 6, [(S("h_ready"), 46), (S("x_lo"), X_LO_ATT + 8)], [(S("h_ready"), 48)])
            out_proj(3, [X_LO_XA[1] + max(k + 1, 6) for k in range(8)], [])
            ffn(3)
            pe.wait_ge(S("h_ready"), 8 * 7 + 1)
            mean_square(8)

        @block.scalar
        def _(act):
            def hi(dst, src, count, **kw):
                act.activation(dst, src, ACT.Copy, **kw).then_inc(S("x_hi"), 1)

            def norm(n):
                to = NORM_TO[n] if n < 8 else None
                for k in range(KC):
                    if n == 0:
                        if k == 0:
                            act.wait_ge(S("vec_in"), 16)
                            act.wait_ge(S("x_in0"), 16)
                        if k == 2:
                            act.wait_ge(S("x_in1"), 16)
                    else:
                        act.wait_ge(S("h_ready"), 8 * (n - 1) + k + 1)
                    if to is not None:
                        if n in (1, 4, 5) and k >= 4:
                            f = {1: 0, 4: 1, 5: 2}[n]
                            act.wait_ge(S("block_done"), FFN_AT[f] + FFN_BLOCKS - (2 if k < 6 else 0))
                        hi(X[to][:, k, 0, :], h[:, k, :], 0, scale=gain(n, k))
                    if 8 * n + k >= 2:
                        act.wait_ge(S("sq_added"), 8 * n + k - 1)
                    act.activation(sq[:, k % 2, :], h[:, k, :], ACT.Square).then_inc(S("sq_ready"), 1)
                if n == 0:
                    act.wait_ge(S("eps_set"), 2)
                act.wait_ge(S("ssq_done"), n + 1)
                if n >= 1:
                    act.wait_ge(S("rstd_ready"), n)
                act.activation(std[:], ps[:, SSQ_BANK, :], ACT.Sqrt, bias=epsc[:, 0:1]
                               ).then_inc(S("std_ready"), 1)

            def ffn(f, beside=None, behind=None):
                at, xo = FFN_AT[f], 1 - NORM_TO[FFN_NORM[f]]

                def silu(i, s):
                    act.wait_ge(S("gate_ready"), i * 2 + (FC * f + s + 1))
                    act.activation(sg[:, s, :], tg[:, s, :], ACT.Silu).then_inc(S("silu"), 1)

                def table(i, s):
                    act.wait_ge(S("s5_turn"), i * 2 + (s - 5))
                    m, c, sn = kv[:, 4 * s * T:(4 * s + 1) * T], kv[:, (4 * s + 2) * T:(4 * s + 3) * T], \
                        kv[:, (4 * s + 3) * T:(4 * s + 4) * T]
                    if not (isinstance(i, int) and i == 3):
                        act.wait_ge(S(f"tab_out{s}"), i * 16 - 48)
                    act.activation(sn, m, ACT.Sin, scale=TWO_PI_BELOW).then_inc(S("s5_sin"), 1)
                    act.wait_ge(S("s5_sin"), i * 2 + (s - 5))
                    act.activation(m, m, ACT.Abs).then_inc(S("s5_abs"), 1)
                    act.wait_ge(S("s5_abs"), i * 2 + (s - 5))
                    act.activation(c, m, ACT.Sin, scale=-TWO_PI_BELOW, bias=epsc[:, 1:2]).then_inc(S("s5_cos"), 1)
                    act.wait_ge(S("s5_cos"), i * 2 + (s - 5))
                    j = i * 2 + (s - 6)
                    dst = s5_tables[j] if isinstance(i, int) else \
                        s5_tables[bass.ds(j, 1)].rearrange("a p n -> p (a n)")
                    act.dma_start(dst, kv[:, (4 * s + 2) * T:(4 * s + 4) * T]).then_inc(S(f"tab_out{s}"), 16)

                last = FC // 2 - 1
                if f == 0:
                    for i in range(4):
                        for s in range(2):
                            silu(i, s)
                        if i == 1:
                            memory(0)
                            s5_constants()
                        if i == 3:
                            for s in range(2):
                                table(i, s)
                    with act.Fori(4, last) as i:
                        for s in range(2):
                            silu(i, s)
                        for s in range(2):
                            table(i, s)
                elif f == 2:
                    for i in range(2):
                        for s in range(2):
                            silu(i, s)
                    memory(1)
                    with act.Fori(2, last) as i:
                        for s in range(2):
                            silu(i, s)
                else:
                    with act.Fori(0, last) as i:
                        for s in range(2):
                            silu(i, s)
                dn = at + 2 * FC

                def part(d, d4, used):
                    if used is not None:
                        act.wait_ge(S("block_done"), used)
                    ch = [6, 7, 4, 5][d4]
                    act.activation(X[xo][:, ch:ch + 1, 0, :], hid[:, d, :], ACT.Copy).then_inc(S("x_hi"), 1)

                for d in range(4):
                    act.wait_ge(S("hid_done"), FC * f + d + 1)
                    part(slice(d, d + 1), d, None)
                for s in range(2):
                    silu(last, s)
                if f == 0:
                    for s in range(2):
                        table(last, s)
                act.wait_ge(S("hid_done"), FC * (f + 1))
                if beside is not None:
                    beside()
                with act.Fori(1, 5) as i:
                    for s in range(4):
                        part(bass.ds(i * 4 + s, 1), s, i * 4 + (dn + s - 3))
                for d in (20, 21):
                    part(slice(d, d + 1), d % 4, dn + d - 3)
                if behind is not None:
                    behind()

            def memory(l):
                m = area(A_MEM, 4 * T).rearrange("p (k m) -> p k m", m=MEM)
                act.wait_ge(S(f"mem_in{l}"), 16)
                for k in range(KC):
                    if k >= 2:
                        act.wait_ge(S("mssq_done"), 8 * l + k - 1)
                    act.activation(sq[:, k % 2, 0:MEM], m[:, k, :], ACT.Square).then_inc(S("msq_ready"), 1)
                act.wait_ge(S("mssq_done"), 8 * l + 8)
                act.wait_ge(S("rstd_ready"), [1, 5][l])
                act.activation(std[:, 0:MEM], ps[:, 1, 0:MEM], ACT.Sqrt, bias=epsc[:, 0:1]
                               ).then_inc(S("mstd"), 1)

            def memory_split(l):
                m = area(A_MEM, 4 * T).rearrange("p (k m) -> p k m", m=MEM)
                act.wait_ge(S("mem_n"), 8 * l + 8)
                act.wait_ge(S("block_done"), FFN_AT[2 * l] + 2 * FC)
                for k in range(KC):
                    act.activation(memX[:, k, 0, :], m[:, k, :], ACT.Copy).then_inc(S("mem_hi"), 1)

            def kv_out(l, t, banks):
                act.wait_ge(S("block_done"), kv_block(l, t) + 1)
                if t < 8:
                    act.activation(KT[:, t, :], ps[:, banks[t % len(banks)], 0:MEM], ACT.Copy
                                   ).then_inc(S("kv_out"), 1)
                elif t % 2 == 1:
                    quarter = (t - 8) // 2
                    act.activation(VM[:, :, quarter * MEM:(quarter + 1) * MEM],
                                   ps[:, banks[quarter % len(banks)], :].rearrange("p (m d) -> p m d", m=2), ACT.Copy
                                   ).then_inc(S("kv_out"), 1)

            def gla_log():
                act.wait_ge(S("alpha_mm"), 1)
                for p in range(2):
                    act.activation(sq[:, p, :], ps[:, BANKS[p], :], ACT.Abs,
                                   bias=vec[:, V_BALPHA + p:V_BALPHA + p + 1]).then_inc(S("g_abs"), 1)
                act.wait_ge(S("g_abs"), 2)
                act.activation(sq[:, :, :], sq[:, :, :], ACT.Exp, scale=-1.0).then_inc(S("g_exp"), 1)
                act.wait_ge(S("g_exp"), 1)
                act.activation(sq[:, :, :], sq[:, :, :], ACT.Ln, bias=1.0).then_inc(S("g_ln"), 1)

            def gla_decay():
                for p in range(2):
                    bc = area(A_BC + p * T)
                    act.wait_ge(S("g_cum"), p + 1)
                    if p == 0:
                        act.wait_ge(S("g_cum"), 2)
                    act.activation(tg[:, p, :], bc, ACT.Exp, scale=1.0 / GLA_TAU).then_inc(S("g_eb"), 1)
                    act.activation(area(A_KINV + p * T), bc, ACT.Exp, scale=-1.0 / GLA_TAU).then_inc(S("g_einv"), 1)
                    act.activation(col[:, p * 8:p * 8 + 8], bc.rearrange("p (c i) -> p c i", i=64)[:, :, 63],
                                   ACT.Exp, scale=1.0 / GLA_TAU).then_inc(S("g_decay"), 1)
                for p in range(2):
                    act.wait_ge(S("g_rel"), p + 1)
                    act.activation(tu[:, p, :], tu[:, p, :], ACT.Exp, scale=-1.0 / GLA_TAU).then_inc(S("g_eend"), 1)
                act.wait_ge(S("proj_out"), 13)
                act.activation(ar[:, 9 * T:13 * T], ar[:, 9 * T:13 * T], ACT.Silu).then_inc(S("g_silu"), 1)

            def gla(fill):
                fill(3)
                act.wait_ge(S("kend_tr"), 1)
                for p in range(2):
                    act.activation(kend_t[:, :, p, :], ps[:, 6 + p, :].rearrange("p (t f) -> p t f", t=4), ACT.Copy
                                   ).then_inc(S("kend_t"), 1)
                fill(3)
                for hd in range(4):
                    act.wait_ge(S("go_mm"), hd + 1)
                    if hd >= 2:
                        act.wait_ge(S("gms_mm"), hd - 1)
                    act.activation(sq[:, hd % 2, :], ps[:, BANKS[hd % 2], :], ACT.Square).then_inc(S("gsq"), 1)
                    act.wait_ge(S("gms_mm"), hd + 1)
                    if hd >= 1:
                        act.wait_ge(S("grstd"), hd)
                    act.activation(std[:], ps[:, hd % 2, :], ACT.Sqrt, bias=epsc[:, 0:1], scale=float(KC)
                                   ).then_inc(S("gstd"), 1)
                    act.wait_ge(S("gla_o"), hd + 1)
                    hi(X[0][:, hd, 0, :], area(A_O + hd * T), 0)
                    fill(2)

            def s5_constants():
                act.wait_ge(S("th_ready"), 1)
                act.activation(tiny[:, 6, :], tiny[:, 5, :], ACT.Abs).then_inc(S("th_abs"), 1)
                act.activation(tiny[:, 8, :], tiny[:, 5, :], ACT.Sin).then_inc(S("th_trig"), 1)
                act.wait_ge(S("th_abs"), 1)
                act.activation(tiny[:, 7, :], tiny[:, 6, :], ACT.Sin, scale=-1.0, bias=epsc[:, 1:2]
                               ).then_inc(S("th_trig"), 1)

            def s5_load(j):
                t = A_S5T + (j % 3) * 2 * T
                if j == 2:
                    act.wait_ge(S("mem_lo"), 8)
                if j >= 3:
                    act.wait_ge(S("s5_xi"), j - 2)
                act.dma_start(area(t, 2 * T), s5_tables[j]).then_inc(S(f"s5_tab{j % 3}"), 16)

            def s5_begin():
                for s in range(2):
                    act.wait_ge(S(f"tab_out{s}"), 16 * 8)
                act.dma_start(kv[:, 4 * T:6 * T], s5c.rearrange("p c j o -> p (c j o)")).then_inc(S("s5c_in"), 16)
                act.dma_start(kv[:, 6 * T:8 * T], s5b.rearrange("p c q s -> p (c q s)")).then_inc(S("s5b_in"), 16)
                act.dma_start(chunk_mask, rows[1:2, :].to_broadcast([P, T])).then_inc(S("cmask_in"), 16)
                act.dma_start(wal, w_alpha).then_inc(S("wal_in"), 16)
                for j in range(3):
                    s5_load(j)

            def s5_gelu(q):
                act.wait_ge(S("s5_y"), q + 1)
                act.activation(Pt[q], Pt[q], ACT.Gelu_apprx_tanh).then_inc(S("gelu"), 1)

            def s5(fill):
                for j in range(S5_TILES):
                    fill(j)
                    if j >= 1 and j + 2 < S5_TILES:
                        s5_load(j + 2)
                    if j % 4 == 1 and j >= 5:
                        s5_gelu(j // 4 - 1)
                    if j == 13:
                        act.wait_ge(S("block_done"), EV_V_AT + 4)
                        act.wait_ge(S("rcol_ready"), 1)
                        for tt in range(4):
                            act.activation(val[:, tt, :], ps[:, BANKS[tt], :], ACT.Copy,
                                           scale=col[:, 16 + tt:17 + tt]).then_inc(S("gla_v"), 1)
                    if j == 14:
                        gla_log()
                    if j == 15:
                        act.wait_ge(S("gelu"), 3)
                        for q in range(3):
                            hi(X[1][:, q, 0, :], Pt[q], 0)
                s5_gelu(3)
                act.wait_ge(S("gelu"), 4)
                hi(X[1][:, 3, 0, :], Pt[3], 0)

            def glu():
                for n in range(4):
                    act.wait_ge(S("half_done") if n % 2 == 0 else S("block_done"), GLU_AT + n // 2 + 1)
                    if n >= 2:
                        act.wait_ge(S("glu_o"), n - 1)
                    act.activation(sg[:, n % 2, :], ps[:, GLU_BANKS[n], :], ACT.Sigmoid,
                                   bias=vec[:, V_BGLU + n:V_BGLU + n + 1]).then_inc(S("glu_sig"), 1)

            def glu_split():
                act.wait_ge(S("glu_o"), 4)
                act.wait_ge(S("block_done"), kv_block(0, 15) + 1)
                for n in range(4):
                    hi(X[0][:, 4 + n, 0, :], Pt[n], 0)

            def tables():
                act.dma_start(area(A_POS + T).bitcast(I32), pos.to_broadcast([P, T])).then_inc(S("pos_in"), 16)
                for i in range(2):
                    act.wait_ge(S("ang"), i + 1)
                    s, c = area(A_TAB + (2 * i + 1) * T), area(A_TAB + 2 * i * T)
                    act.activation(c, s, ACT.Abs).then_inc(S("ang_abs"), 1)
                    act.wait_ge(S("ang_abs"), i + 1)
                    act.activation(s, s, ACT.Sin).then_inc(S("tab"), 1)
                    act.activation(c, c, ACT.Sin, scale=-1.0, bias=epsc[:, 1:2]).then_inc(S("tab"), 1)

            def indexer(fill):
                for i in range(24):
                    nk = (i // 8 + 2) * P
                    if i % 8 == 5:
                        fill(1)
                    act.wait_ge(S("logit_mm"), i + 1)
                    if i >= 2:
                        act.wait_ge(S("idx_acc"), i - 1)
                    act.activation(tg[:, i % 2, 0:nk], ps[:, BANKS[i % 4], 0:nk], ACT.Relu).then_inc(S("relu"), 1)

            def attention(fill):
                def exps(i):
                    g, qb = UNITS[i]
                    pb, c = (A_P if i % 2 == 0 else A_P1), 16 * (i % 2)
                    act.wait_ge(S("att_nm"), i + 1)
                    for j in range(4):
                        row = area(pb + j * T)[:, 0:(qb + 1) * P]
                        act.activation(row, row, ACT.Exp, bias=col[:, c + 4 + j:c + 5 + j],
                                       accum_out=col[:, c + 8 + j:c + 9 + j]).then_inc(S("att_e"), 1)

                nt = 0
                exps(0)
                fill(2)
                for i, (g, qb) in enumerate(UNITS):
                    fill(1)
                    if i == 6:
                        exps(7)
                        act.wait_ge(S("block_done"), kv_block(1, 15) + 1)
                        act.wait_ge(S("att_kept"), len(KEPT))
                        for n, u in enumerate(KEPT):
                            qc = slice(UNITS[u][1] * P, (UNITS[u][1] + 1) * P)
                            hi(X[0][:, 4:8, 0, qc], area(A_KEPT[n]).rearrange("p (j q) -> p j q", j=4), 0)
                    for kc in range(qb + 1):
                        act.wait_ge(S("att_tr"), nt + 1)
                        if i >= 1 and kc == 0:
                            act.wait_ge(S("att_o"), i)
                        act.activation(area(A_PT + kc * T), ps[:, 6 + nt % 2, :], ACT.Copy).then_inc(S("att_t"), 1)
                        nt += 1
                    if i < 6:
                        fill(1)
                    act.wait_ge(S("att_o"), i + 1)
                    if i in KEPT:
                        act.activation(area(A_KEPT[KEPT.index(i)]), ps[:, 0, :], ACT.Copy).then_inc(S("att_kept"), 1)
                    else:
                        hi(X[0][:, 4 * g:4 * g + 4, 0, qb * P:(qb + 1) * P],
                           ps[:, 0, :].rearrange("p (j q) -> p j q", j=4), 0)
                    if i < 6:
                        exps(i + 1)

            def cross(l):
                def exps(hd):
                    pb, c = A_XP + (hd % 2) * 2 * T, 16 * (hd % 2)
                    act.wait_ge(S("xa_nm"), 4 * l + hd + 1)
                    for qb in range(QB):
                        e = act.activation(area(pb + qb * MEM, MEM),
                                           ps[:, XS_BANKS[hd % 2] + qb // 2, (qb % 2) * MEM:(qb % 2 + 1) * MEM],
                                           ACT.Exp, scale=XA_DIM ** -0.5, bias=col[:, c + 4 + qb:c + 5 + qb],
                                           accum_out=col[:, c + 8 + qb:c + 9 + qb])
                    e.then_inc(S("xa_p"), 1)

                def copies(hd):
                    for mc in range(2):
                        act.wait_ge(S("xa_tr"), 8 * l + 2 * hd + mc + 1)
                        if hd >= 2:
                            act.wait_ge(S("xa_o"), 8 * l + 2 * hd - 2)
                        act.activation(area(A_XPT + (hd % 2) * 2 * T + mc * T), ps[:, BANKS[2 + mc], :], ACT.Copy
                                       ).then_inc(S("xa_t"), 1)

                def upper(hd):
                    for dc in range(2):
                        act.wait_ge(S("xa_o"), 8 * l + 2 * hd + dc + 1)
                        hi(X[0][:, 2 * hd + dc, 0, :], ps[:, XO_BANKS[hd][dc], :], 0)

                exps(0)
                exps(1)
                copies(0)
                exps(2)
                upper(0)
                copies(1)
                exps(3)
                upper(1)
                for hd in (2, 3):
                    copies(hd)
                    upper(hd)

            kv_next = [0]

            def fill(l, banks, n):
                for _ in range(n):
                    if kv_next[0] < 16:
                        kv_out(l, kv_next[0], banks)
                        kv_next[0] += 1

            norm(0)
            ffn(0, lambda: memory_split(0), s5_begin)
            norm(1)
            s5(lambda j: fill(0, KV_BANKS, j - 13) if j >= 14 else None)
            fill(0, KV_BANKS, 2)
            gla_decay()
            glu()
            gla(lambda n: fill(0, KV_BANKS, n))
            fill(0, KV_BANKS, 16)
            glu_split()
            norm(2)
            cross(0)
            norm(3)
            ffn(1, tables)
            act.dma_start(area(A_MEM, 4 * T).rearrange("p (k m) -> p k m", m=MEM), memT).then_inc(S("mem_in1"), 16)
            norm(4)
            ffn(2, lambda: memory_split(1))
            norm(5)
            kv_next[0] = 0
            indexer(lambda n: fill(1, [1], n))
            attention(lambda n: fill(1, [1], n))
            norm(6)
            cross(1)
            norm(7)
            ffn(3)
            norm(8)
            for k in range(KC):
                act.wait_ge(S("y_ready"), k + 1)
                act.dma_start(out[:, k, :], h[:, k, :]).then_inc(S("out_done"), 16)
            act.wait_ge(S("out_done"), 16 * KC)

        @block.vector
        def _(dve):
            step = [0]

            def chain(ins):
                step[0] += 1
                ins.then_inc(S("dve_step"), 1)
                dve.wait_ge(S("dve_step"), step[0])

            def lo_of(dst, src, hi_ap, count):
                dve.wait_ge(S("x_hi"), count)
                dve.tensor_tensor(dst, src, hi_ap.bitcast(F32), ALU.subtract).then_inc(S("x_lo"), 1)

            def norm(n, factor, mm_sem, mm_base, banks):
                to = NORM_TO[n] if n < 8 else None

                def lower(k):
                    if to is None:
                        return
                    dve.wait_ge(S("x_hi"), X_LO_NORM[n] + k + 1)
                    dve.scalar_tensor_tensor(X[to][:, k, 1, :], h[:, k, :], gain(n, k),
                                             X[to][:, k, 0, :].bitcast(F32), ALU.mult, ALU.subtract
                                             ).then_inc(S("x_lo"), 1)

                def add_square(k):
                    dve.wait_ge(S("sq_ready"), 8 * n + k + 1)
                    if k == 0:
                        ins = dve.tensor_copy(tg[:, 0, :], sq[:, 0, :])
                    else:
                        dve.wait_ge(S("sq_added"), 8 * n + k)
                        ins = dve.tensor_tensor(tg[:, 0, :], tg[:, 0, :], sq[:, k % 2, :], ALU.add)
                    ins.then_inc(S("sq_added"), 1)

                if n == 0:
                    for k in range(KC):
                        lower(k)
                        add_square(k)
                else:
                    for k in range(KC):
                        if mm_sem is not None and k < 7:
                            dve.wait_ge(mm_sem, mm_base[0] + k + 1)
                        elif mm_sem is not None:
                            dve.wait_ge(S("block_done"), mm_base[1])
                        else:
                            dve.wait_ge(S("block_done"), mm_base[0] + k + 1)
                        dve.scalar_tensor_tensor(h[:, k, :], ps[:, banks[k], :], factor, h[:, k, :],
                                                 ALU.mult, ALU.add).then_inc(S("h_ready"), 1)
                        if k >= 1:
                            lower(k - 1)
                            add_square(k - 1)
                    lower(KC - 1)
                    add_square(KC - 1)
                dve.wait_ge(S("std_ready"), n + 1)
                dve.reciprocal(rstd[:], std[:]).then_inc(S("rstd_ready"), 1)
                dve.wait_ge(S("rstd_ready"), n + 1)

            def norm_after_ffn(n, f):
                norm(n, 0.5, S("down_out"), (7 * f, FFN_AT[f] + FFN_BLOCKS), DOWN_BANKS)

            def norm_after_out(n, o):
                norm(n, 1.0, None, (OUT_AT[o],), [BANKS[t % 4] for t in range(8)])

            def ffn(f, beside=None, behind=None):
                at, xo = FFN_AT[f], 1 - NORM_TO[FFN_NORM[f]]

                def gate(i, s):
                    dve.wait_ge(S("block_done"), i * 4 + (at + 2 * s + 1))
                    dve.tensor_tensor(tg[:, s, :], ps[:, BANKS[2 * s], :], rstd[:], ALU.mult
                                      ).then_inc(S("gate_ready"), 1)
                    dve.wait_ge(S("block_done"), i * 4 + (at + 2 * s + 2))
                    dve.tensor_tensor(tu[:, s, :], ps[:, BANKS[2 * s + 1], :], rstd[:], ALU.mult
                                      ).then_inc(S("up_ready"), 1)
                    dve.wait_ge(S("up_ready"), i * 2 + (FC * f + s + 1))
                    dve.wait_ge(S("silu"), i * 2 + (FC * f + s + 1))
                    j = i * 2 + s
                    dst = hid[:, j:j + 1, :] if isinstance(i, int) else hid[:, bass.ds(j, 1), :]
                    dve.tensor_tensor(dst, sg[:, s:s + 1, :], tu[:, s:s + 1, :], ALU.mult
                                      ).then_inc(S("hid_done"), 1)

                last = FC // 2 - 1
                if f == 0:
                    parts = s5_constants()
                    for i in range(4):
                        for s in range(2):
                            gate(i, s)
                        if i == 1:
                            memory(0)
                        if i < 3:
                            next(parts)
                        else:
                            for s in range(2):
                                turns(i, s)
                    with dve.Fori(4, last) as i:
                        for s in range(2):
                            gate(i, s)
                        for s in range(2):
                            turns(i, s)
                elif f == 2:
                    for i in range(2):
                        for s in range(2):
                            gate(i, s)
                    memory(1)
                    with dve.Fori(2, last) as i:
                        for s in range(2):
                            gate(i, s)
                else:
                    with dve.Fori(0, last) as i:
                        for s in range(2):
                            gate(i, s)

                def part(d, d4, count):
                    ch = [6, 7, 4, 5][d4]
                    dve.wait_ge(S("x_hi"), count)
                    dve.tensor_tensor(X[xo][:, ch:ch + 1, 1, :], hid[:, d, :],
                                      X[xo][:, ch:ch + 1, 0, :].bitcast(F32), ALU.subtract
                                      ).then_inc(S("x_lo"), 1)

                base = X_LO_HID[f]
                dve.wait_ge(S("hid_done"), FC * f + 4)
                for d in range(4):
                    part(slice(d, d + 1), d, base + d + 1)
                for s in range(2):
                    gate(last, s)
                if f == 0:
                    for s in range(2):
                        turns(last, s)
                dve.wait_ge(S("hid_done"), FC * (f + 1))
                if beside is not None:
                    beside()
                with dve.Fori(1, 5) as i:
                    for s in range(4):
                        part(bass.ds(i * 4 + s, 1), s, i * 4 + (base + s + 1))
                for d in (20, 21):
                    part(slice(d, d + 1), d % 4, base + d + 1)
                if behind is not None:
                    behind()

            def tile_out(at, t):
                dve.wait_ge(S("block_done"), at + t + 1)
                dve.tensor_tensor(Pt[t], ps[:, BANKS[t % 4], :], rstd[:], ALU.mult).then_inc(S("proj_out"), 1)

            def rstd_columns(l):
                dve.wait_ge(S("rcol_mm"), l + 1)
                dve.tensor_copy(col[:, 16:20], ps[:, 1, :].rearrange("p (t n) -> p t n", n=P)[:, :, 0]
                                ).then_inc(S("rcol_ready"), 1)
                dve.wait_ge(S("rcol_ready"), l + 1)

            def memory(l):
                m = area(A_MEM, 4 * T).rearrange("p (k m) -> p k m", m=MEM)
                dve.wait_ge(S("mstd"), l + 1)
                dve.reciprocal(std[:, MEM:T], std[:, 0:MEM]).then_inc(S("mrstd"), 1)
                dve.wait_ge(S("mrstd"), l + 1)
                for k in range(KC):
                    g = vec[:, V_MEMG + k:V_MEMG + k + 1]
                    dve.scalar_tensor_tensor(m[:, k, :], m[:, k, :], g, std[:, MEM:T], ALU.mult, ALU.mult
                                             ).then_inc(S("mem_n"), 1)
                dve.wait_ge(S("mem_n"), 8 * l + 8)

            def memory_split(l):
                m = area(A_MEM, 4 * T).rearrange("p (k m) -> p k m", m=MEM)
                for k in range(KC):
                    dve.wait_ge(S("mem_hi"), 8 * l + k + 1)
                    dve.tensor_tensor(memX[:, k, 1, :], m[:, k, :], memX[:, k, 0, :].bitcast(F32), ALU.subtract
                                      ).then_inc(S("mem_lo"), 1)

            def tn(i):
                return tiny[:, i, :]

            def exact_exp(dst, src):
                k, r, p = tn(9), tn(10), tn(11)
                chain(dve.tensor_scalar(k, src, 1.4426950408889634, MAGIC, ALU.mult, ALU.add))
                chain(dve.tensor_scalar(k, k, MAGIC, None, ALU.subtract))
                chain(dve.tensor_scalar(k, k, -126.0, 127.0, ALU.max, ALU.min))
                chain(dve.scalar_tensor_tensor(r, k, -0.693359375, src, ALU.mult, ALU.add))
                chain(dve.scalar_tensor_tensor(r, k, 2.12194440e-4, r, ALU.mult, ALU.add))
                chain(dve.tensor_scalar(p, r, 1.0 / 5040, 1.0 / 720, ALU.mult, ALU.add))
                for c in (1.0 / 120, 1.0 / 24, 1.0 / 6, 0.5, 1.0, 1.0):
                    chain(dve.tensor_tensor(p, p, r, ALU.mult))
                    chain(dve.tensor_scalar(p, p, c, None, ALU.add))
                chain(dve.tensor_scalar(k, k, 127.0, None, ALU.add))
                chain(dve.tensor_copy(tiny_i[:], k))
                chain(dve.tensor_scalar(tiny_i[:], tiny_i[:], 23, None, ALU.logical_shift_left))
                chain(dve.tensor_tensor(dst, p, tiny_i[:].bitcast(F32), ALU.mult))

            def s5_constants():
                lr, dt, th, ab_r, ab_i = tn(0), tn(1), tn(2), tn(3), tn(4)
                mag, ph, pl = sc5[:, C_MAG:C_MAG + 16], sc5[:, C_PH:C_PH + 16], sc5[:, C_PL:C_PL + 16]
                fr, fi = sc5[:, C_FR:C_FR + 16], sc5[:, C_FI:C_FI + 16]
                li = vec[:, V_LIM:V_LIM + 16]
                chain(dve.tensor_scalar(lr, vec[:, V_LRE:V_LRE + 16], -1e-4, None, ALU.min))
                exact_exp(dt, vec[:, V_LDT:V_LDT + 16])
                chain(dve.tensor_tensor(th, lr, dt, ALU.mult))
                exact_exp(mag, th)
                yield
                chain(dve.tensor_tensor(th, li, dt, ALU.mult))
                reduce_angle(th, tn(5))
                dve.tensor_scalar(tn(5), th, PI_BELOW, -PI_BELOW, ALU.min, ALU.max).then_inc(S("th_ready"), 1)
                chain(dve.tensor_scalar(th, th, 0.15915494309189535, None, ALU.mult))
                chain(dve.tensor_scalar(ph, th, 4096.0, MAGIC, ALU.mult, ALU.add))
                chain(dve.tensor_scalar(ph, ph, MAGIC, 1.0 / 4096, ALU.subtract, ALU.mult))
                chain(dve.tensor_tensor(pl, th, ph, ALU.subtract))
                yield
                dve.wait_ge(S("th_trig"), 2)
                chain(dve.tensor_tensor(ab_r, tn(7), mag, ALU.mult))
                chain(dve.tensor_tensor(ab_i, tn(8), mag, ALU.mult))
                chain(dve.tensor_scalar(ab_r, ab_r, 1.0, None, ALU.subtract))
                den, t1 = tn(5), tn(6)
                chain(dve.tensor_tensor(den, lr, lr, ALU.mult))
                chain(dve.tensor_tensor(t1, li, li, ALU.mult))
                chain(dve.tensor_tensor(den, den, t1, ALU.add))
                chain(dve.reciprocal(den, den))
                chain(dve.tensor_tensor(fr, ab_r, lr, ALU.mult))
                chain(dve.tensor_tensor(t1, ab_i, li, ALU.mult))
                chain(dve.tensor_tensor(fr, fr, t1, ALU.add))
                chain(dve.tensor_tensor(fr, fr, den, ALU.mult))
                chain(dve.tensor_tensor(fi, ab_i, lr, ALU.mult))
                chain(dve.tensor_tensor(t1, ab_r, li, ALU.mult))
                chain(dve.tensor_tensor(fi, fi, t1, ALU.subtract))
                chain(dve.tensor_tensor(fi, fi, den, ALU.mult))
                yield

            def reduce_angle(x, k):
                chain(dve.tensor_scalar(k, x, 0.15915494309189535, MAGIC, ALU.mult, ALU.add))
                chain(dve.tensor_scalar(k, k, MAGIC, None, ALU.subtract))
                for c in (TWO_PI_1, TWO_PI_2, TWO_PI_3):
                    chain(dve.scalar_tensor_tensor(x, k, -c, x, ALU.mult, ALU.add))

            def turns(i, s):
                time = area(A_TIME)
                if isinstance(i, int):
                    dve.wait_ge(S("time_in"), 16)
                    j = 2 * (i - 3) + s
                    ph, pl = sc5[:, C_PH + j:C_PH + j + 1], sc5[:, C_PL + j:C_PL + j + 1]
                else:
                    ph = sc5[:, bass.ds(i * 2 + (C_PH + s - 6), 1)]
                    pl = sc5[:, bass.ds(i * 2 + (C_PL + s - 6), 1)]
                a, b = kv[:, 4 * s * T:(4 * s + 1) * T], kv[:, (4 * s + 1) * T:(4 * s + 2) * T]

                def then(ins, n):
                    ins.then_inc(S("turn_step"), 1)
                    dve.wait_ge(S("turn_step"), i * 10 + (5 * s + n - 30))

                then(dve.tensor_scalar(a, time, ph, None, ALU.mult), 1)
                then(dve.tensor_scalar(b, a, MAGIC, MAGIC, ALU.add, ALU.subtract), 2)
                then(dve.tensor_tensor(a, a, b, ALU.subtract), 3)
                then(dve.scalar_tensor_tensor(a, time, pl, a, ALU.mult, ALU.add), 4)
                then(dve.tensor_scalar(b, a, MAGIC, MAGIC, ALU.add, ALU.subtract), 5)
                dve.tensor_tensor(a, a, b, ALU.subtract).then_inc(S("s5_turn"), 1)

            def gla_decay():
                dve.wait_ge(S("g_ln"), 1)
                dve.wait_ge(S("cmask_in"), 16)
                for p in range(2):
                    chain(dve.tensor_scalar(tu[:, p, :], ps[:, BANKS[p], :], vec[:, V_BALPHA + p:V_BALPHA + p + 1],
                                            0.0, ALU.add, ALU.min))
                    chain(dve.tensor_tensor(tu[:, p, :], tu[:, p, :], sq[:, p, :], ALU.subtract))
                    dve.tensor_tensor_scan(area(A_BC + p * T), chunk_mask, tu[:, p, :], 0.0, ALU.mult, ALU.add
                                           ).then_inc(S("g_cum"), 1)
                dve.wait_ge(S("g_cum"), 2)
                for p in range(2):
                    bc = area(A_BC + p * T).rearrange("p (c i) -> p c i", i=64)
                    dve.tensor_tensor(tu[:, p, :].rearrange("p (c i) -> p c i", i=64), bc,
                                      bc[:, :, 63:64].to_broadcast([P, NCH, 64]), ALU.subtract).then_inc(S("g_rel"), 1)
                for p in range(2):
                    dve.wait_ge(S("g_eb"), p + 1)
                    dve.scalar_tensor_tensor(Pt[5 + p], Pt[5 + p], GLA_DK ** -0.5, tg[:, p, :], ALU.mult, ALU.mult
                                             ).then_inc(S("qdec"), 1)
                    dve.wait_ge(S("g_einv"), p + 1)
                    dve.tensor_tensor(area(A_KINV + p * T), area(A_KINV + p * T), Pt[7 + p], ALU.mult
                                      ).then_inc(S("kinv"), 1)
                    dve.wait_ge(S("g_eend"), p + 1)
                    dve.tensor_tensor(Pt[7 + p], Pt[7 + p], tu[:, p, :], ALU.mult).then_inc(S("kend"), 1)
                dve.wait_ge(S("qdec"), 2)
                for p in range(2):
                    chain(dve.memset(tg[:, p, :], 0.0))

            def gla():
                dve.wait_ge(S("g_decay"), 2)
                for c in range(NCH - 1):
                    dve.wait_ge(S("state_mm"), c + 1)
                    for p in range(2):
                        for e in range(2):
                            r = slice(64 * e, 64 * e + 64)
                            src = ps[r, BANKS[c % 2], p * 256 + e * P:p * 256 + (e + 1) * P]
                            if c == 0:
                                dve.tensor_copy(state[r, p, 1, :], src).then_inc(S("state"), 1)
                            else:
                                dve.scalar_tensor_tensor(state[r, p, c + 1, :], state[r, p, c, :],
                                                         col[r, p * 8 + c:p * 8 + c + 1], src, ALU.mult, ALU.add
                                                         ).then_inc(S("state"), 1)
                    dve.wait_ge(S("state"), 4 * (c + 1))

                def score(hd):
                    dve.wait_ge(S("gscore_mm"), hd + 1)
                    if hd >= 2:
                        dve.wait_ge(S("go_mm"), hd - 1)
                    dve.copy_predicated(tg[:, hd % 2, :].rearrange("p (t i) -> p t i", t=4),
                                        msk[:].unsqueeze(1).to_broadcast([P, 4, P]),
                                        ps[:, 6 + hd % 2, :].rearrange("p (t i) -> p t i", t=4)
                                        ).then_inc(S("gscore"), 1)

                dve.wait_ge(S("msk_in"), 16)
                score(0)
                for hd in range(4):
                    if hd < 3:
                        score(hd + 1)
                    dve.wait_ge(S("gstd"), hd + 1)
                    dve.reciprocal(rstd[:], std[:]).then_inc(S("grstd"), 1)
                    dve.wait_ge(S("grstd"), hd + 1)
                    o = area(A_O + hd * T)
                    chain(dve.scalar_tensor_tensor(o, ps[:, BANKS[hd % 2], :], vec[:, V_GLAN:V_GLAN + 1], rstd[:],
                                                   ALU.mult, ALU.mult))
                    if hd == 0:
                        dve.wait_ge(S("g_silu"), 1)
                    dve.tensor_tensor(o, o, Pt[9 + hd], ALU.mult).then_inc(S("gla_o"), 1)
                    dve.wait_ge(S("x_hi"), X_LO_GLA + hd + 1)
                    dve.wait_ge(S("gla_o"), hd + 1)
                    dve.tensor_tensor(X[0][:, hd, 1, :], o, X[0][:, hd, 0, :].bitcast(F32), ALU.subtract
                                      ).then_inc(S("x_lo"), 1)

            def s5_output_matrices():
                dve.wait_ge(S("s5c_in"), 16)
                cr, ci = s5ct[:, 0, :, :], s5ct[:, 1, :, :]
                fr = sc5[:, C_FR:C_FR + 16].unsqueeze(2).to_broadcast([P, 16, 32])
                fi = sc5[:, C_FI:C_FI + 16].unsqueeze(2).to_broadcast([P, 16, 32])
                tA = tu[:, 0, :].rearrange("p (j c) -> p j c", j=16)
                tB = tu[:, 1, :].rearrange("p (j c) -> p j c", j=16)
                chain(dve.tensor_tensor(tA, cr, fi, ALU.mult))
                chain(dve.tensor_tensor(tB, ci, fi, ALU.mult))
                chain(dve.tensor_tensor(cr, cr, fr, ALU.mult))
                dve.tensor_tensor(cr, cr, tB, ALU.subtract).then_inc(S("s5_c"), 1)
                chain(dve.tensor_tensor(ci, ci, fr, ALU.mult))
                chain(dve.tensor_tensor(ci, ci, tA, ALU.add))
                dve.tensor_scalar(ci, ci, -1.0, None, ALU.mult).then_inc(S("s5_c"), 1)

            def s5(fill):
                done = [0]

                def op(ins):
                    done[0] += 1
                    ins.then_inc(S("s5_step"), 1)
                    return done[0]

                def after(n):
                    if n:
                        dve.wait_ge(S("s5_step"), n)

                free = 0

                def out(q):
                    dve.wait_ge(S("s5_out_mm"), 4 * q + 4)
                    dve.scalar_tensor_tensor(Pt[q], Pt[q], vec[:, V_D + q:V_D + q + 1],
                                             ps[:, 6 + q % 2, :], ALU.mult, ALU.add).then_inc(S("s5_y"), 1)

                p1, p2, p3, p4, zr, zi = tg[:, 0, :], tg[:, 1, :], tu[:, 0, :], tu[:, 1, :], sg[:, 0, :], sg[:, 1, :]
                vr, vi = ps[:, 0, :], ps[:, 1, :]
                for j in range(S5_TILES):
                    fill(j)
                    t = A_S5T + (j % 3) * 2 * T
                    c, s = area(t), area(t + T)
                    x = A_S5X + (j % 2) * 2 * T
                    xr, xi = area(x), area(x + T)
                    mag = sc5[:, C_MAG + j:C_MAG + j + 1].to_broadcast([P, T])
                    dve.wait_ge(S(f"s5_tab{j % 3}"), 16 * (j // 3 + 1))
                    dve.wait_ge(S("s5_in_mm"), j + 1)
                    after(free)
                    op(dve.tensor_tensor(p1, vr, c, ALU.mult))
                    n2 = op(dve.tensor_tensor(p2, vi, s, ALU.mult))
                    if j >= 1:
                        dve.wait_ge(S("s5_xi"), j)
                    op(dve.tensor_tensor(p3, vi, c, ALU.mult))
                    dve.tensor_tensor(p4, vr, s, ALU.mult).then_inc(S("s5_read"), 1)
                    after(n2)
                    nr = op(dve.tensor_tensor(p1, p1, p2, ALU.add))
                    dve.wait_ge(S("s5_read"), j + 1)
                    ni = op(dve.tensor_tensor(p3, p3, p4, ALU.subtract))
                    after(nr)
                    nr = op(dve.tensor_tensor_scan(zr, mag, p1, 0.0, ALU.mult, ALU.add))
                    after(ni)
                    ni = op(dve.tensor_tensor_scan(zi, mag, p3, 0.0, ALU.mult, ALU.add))
                    after(nr)
                    op(dve.tensor_tensor(p1, zr, c, ALU.mult))
                    after(ni)
                    n2 = op(dve.tensor_tensor(p2, zi, s, ALU.mult))
                    op(dve.tensor_tensor(p3, zr, s, ALU.mult))
                    n4 = op(dve.tensor_tensor(p4, zi, c, ALU.mult))
                    if j >= 2:
                        dve.wait_ge(S("s5_out_mm"), j - 1)
                    after(n2)
                    free = op(dve.tensor_tensor(xr, p1, p2, ALU.subtract))
                    after(n4)
                    dve.tensor_tensor(xi, p3, p4, ALU.add).then_inc(S("s5_xi"), 1)
                    if j % 4 == 0 and j >= 4:
                        out(j // 4 - 1)
                dve.wait_ge(S("s5_xi"), S5_TILES)
                for q in range(4):
                    if q == 3:
                        out(3)
                    lo_of(X[1][:, q, 1, :], Pt[q], X[1][:, q, 0, :], X_LO_Y + q + 1)

            def glu():
                for n in range(4):
                    dve.wait_ge(S("glu_sig"), n + 1)
                    dve.tensor_tensor(Pt[n], Pt[n], sg[:, n % 2, :], ALU.mult).then_inc(S("glu_o"), 1)
                dve.wait_ge(S("glu_o"), 4)

            def glu_split():
                for n in range(4):
                    lo_of(X[0][:, 4 + n, 1, :], Pt[n], X[0][:, 4 + n, 0, :], X_LO_GLU + n + 1)

            def tables():
                dve.wait_ge(S("pos_in"), 16)
                chain(dve.tensor_copy(area(A_POS), area(A_POS + T).bitcast(I32)))
                for i in range(2):
                    x = area(A_TAB + (2 * i + 1) * T)
                    chain(dve.tensor_scalar(x, area(A_POS), vec[:, V_INVA + i:V_INVA + i + 1], None, ALU.mult))
                    reduce_angle(x, area(A_TAB + 2 * i * T))
                    dve.tensor_scalar(x, x, PI_BELOW, -PI_BELOW, ALU.min, ALU.max).then_inc(S("ang"), 1)

            def rope(t):
                c = area(A_TAB + (0 if t < 10 else 2) * T)
                s = area(A_TAB + (1 if t < 10 else 3) * T)
                if t == 0:
                    dve.wait_ge(S("tab"), 4)
                dve.wait_ge(S("rope_mm"), t + 1)
                dve.tensor_tensor(tg[:, t % 2, :], ps[:, 6 + t % 2, :], s, ALU.mult).then_inc(S("rope_s"), 1)
                chain(dve.tensor_tensor(Pt[t], Pt[t], c, ALU.mult))
                dve.wait_ge(S("rope_s"), t + 1)
                dve.tensor_tensor(Pt[t], Pt[t], tg[:, t % 2, :], ALU.add).then_inc(S("rope_done"), 1)

            def indexer_weights():
                dve.wait_ge(S("wi_mm"), 1)
                dve.tensor_scalar(col[:, 32:64].rearrange("p (t i) -> p t i", i=8),
                                  ps[:, 1, :].rearrange("p (t n) -> p t n", n=P)[:, :, 0:8],
                                  (IDX_HEADS * IDX_DIM) ** -0.5, None, ALU.mult).then_inc(S("wi_ready"), 1)
                dve.wait_ge(S("wi_ready"), 1)

            def indexer():
                dve.wait_ge(S("rope_done"), len(ROPE_TILES))
                i = 0
                for qb in range(1, QB):
                    nk = (qb + 1) * P
                    sc = area(A_SC + qb * T)[:, 0:nk]
                    for hd in range(IDX_HEADS):
                        w = col[:, 32 + 8 * qb + hd:33 + 8 * qb + hd]
                        dve.wait_ge(S("relu"), i + 1)
                        if hd == 0:
                            ins = dve.tensor_scalar(sc, tg[:, i % 2, 0:nk], w, None, ALU.mult)
                        else:
                            ins = dve.scalar_tensor_tensor(sc, tg[:, i % 2, 0:nk], w, sc, ALU.mult, ALU.add)
                        ins.then_inc(S("idx_acc"), 1)
                        i += 1
                        dve.wait_ge(S("idx_acc"), i)
                    chain(dve.tensor_tensor(sc[:, qb * P:nk], sc[:, qb * P:nk], cmask, ALU.add))
                chain(dve.tensor_copy(area(A_SC)[:, 0:P], cmask))

            def topk(qb, first, last):
                nk = (qb + 1) * P
                sc = area(A_SC + qb * T)[:, 0:nk]
                for _ in range(first, last):
                    chain(dve.max(col[:, 32:40], sc))
                    chain(dve.match_replace(sc, col[:, 32:40], sc, TAKEN))
                if last == TOPK // 8:
                    chain(dve.tensor_scalar(sc, sc, TAKEN / 2, MASKED, ALU.is_gt, ALU.mult))

            def attention():
                def unit(i):
                    g, qb = UNITS[i]
                    nk = (qb + 1) * P
                    pb, c = (A_P if i % 2 == 0 else A_P1), 16 * (i % 2)
                    return g, qb, nk, c, area(pb, 4 * T).rearrange("p (j n) -> p j n", j=4)[:, :, 0:nk]

                def front(i):
                    g, qb, nk, c, pr = unit(i)
                    bias = area(A_SC + qb * T)[:, 0:nk].unsqueeze(1).to_broadcast([P, 4, nk])
                    dve.wait_ge(S("att_mm"), i + 1)
                    if i >= 2:
                        dve.wait_ge(S("att_tr"), UNIT_TR[i - 2])
                    dve.scalar_tensor_tensor(pr, ps[:, 2:6, 0:nk], ATT_DIM ** -0.5, bias, ALU.mult, ALU.add
                                             ).then_inc(S("att_s"), 1)
                    dve.wait_ge(S("att_s"), i + 1)
                    chain(dve.tensor_reduce(col[:, c:c + 4], pr, AX.X, ALU.max))
                    dve.tensor_scalar(col[:, c + 4:c + 8], col[:, c:c + 4], -1.0, None, ALU.mult
                                      ).then_inc(S("att_nm"), 1)

                def normalise(i):
                    g, qb, nk, c, pr = unit(i)
                    dve.wait_ge(S("att_e"), 4 * i + 4)
                    chain(dve.reciprocal(col[:, c + 12:c + 16], col[:, c + 8:c + 12]))
                    dve.tensor_tensor(pr, pr, col[:, c + 12:c + 16].unsqueeze(2).to_broadcast([P, 4, nk]), ALU.mult
                                      ).then_inc(S("att_p"), 1)

                def lower(i):
                    g, qb, nk, c, pr = unit(i)
                    dve.wait_ge(S("x_hi"), X_LO_ATT + SPLIT_ORDER.index(i) + 1)
                    qc = slice(qb * P, (qb + 1) * P)
                    dve.tensor_tensor(X[0][:, 4 * g:4 * g + 4, 1, qc],
                                      (area(A_KEPT[KEPT.index(i)]) if i in KEPT else ps[:, 0, :]
                                       ).rearrange("p (j q) -> p j q", j=4),
                                      X[0][:, 4 * g:4 * g + 4, 0, qc].bitcast(F32), ALU.subtract
                                      ).then_inc(S("x_lo"), 1)

                front(0)
                for pair, qb in enumerate((3, 2, 1)):
                    i = 2 * pair
                    topk(qb, 0, 4)
                    normalise(i)
                    front(i + 1)
                    topk(qb, 4, 11)
                    normalise(i + 1)
                    lower(i)
                    topk(qb, 11, 16)
                    front(i + 2)
                front(7)
                normalise(6)
                for u in KEPT:
                    lower(u)
                normalise(7)
                lower(6)
                lower(7)

            def cross(l):
                at, base = XQ_AT[l], 0

                def front(hd):
                    c = 16 * (hd % 2)
                    dve.wait_ge(S("xa_mm"), 4 * l + hd + 1)
                    b = XS_BANKS[hd % 2]
                    chain(dve.tensor_reduce(col[:, c:c + 4], ps[:, b:b + 2, :].rearrange("p a (b n) -> p (a b) n", b=2),
                                            AX.X, ALU.max))
                    dve.tensor_scalar(col[:, c + 4:c + 8], col[:, c:c + 4], -XA_DIM ** -0.5, None, ALU.mult
                                      ).then_inc(S("xa_nm"), 1)

                def normalise(hd):
                    c = 16 * (hd % 2)
                    pr = area(A_XP + (hd % 2) * 2 * T, 2 * T).rearrange("p (j n) -> p j n", j=4)
                    dve.wait_ge(S("xa_p"), 4 * l + hd + 1)
                    chain(dve.reciprocal(col[:, c + 12:c + 16], col[:, c + 8:c + 12]))
                    dve.tensor_tensor(pr, pr, col[:, c + 12:c + 16].unsqueeze(2).to_broadcast([P, 4, MEM]), ALU.mult
                                      ).then_inc(S("xa_pn"), 1)

                def lower(hd):
                    for dc in range(2):
                        lo_of(X[0][:, 2 * hd + dc, 1, :], ps[:, XO_BANKS[hd][dc], :], X[0][:, 2 * hd + dc, 0, :],
                              X_LO_XA[l] + 2 * hd + dc + 1)

                for t in range(8):
                    tile_out(at, t)
                    if t in (4, 6):
                        front((t - 4) // 2)
                normalise(0)
                front(2)
                normalise(1)
                lower(0)
                front(3)
                normalise(2)
                lower(1)
                normalise(3)
                lower(2)
                lower(3)

            dve.memset(ones[:], 1.0 / D).then_inc(S("ones_set"), 1)
            dve.memset(epsc[:, 0:1], EPS).then_inc(S("eps_set"), 1)
            dve.memset(epsc[:, 1:2], float(np.pi / 2)).then_inc(S("eps_set"), 1)
            norm(0, 1.0, None, (0,), None)
            ffn(0, lambda: memory_split(0), s5_output_matrices)
            norm_after_ffn(1, 0)
            for t in range(4):
                tile_out(EV_AT, t)
            rstd_columns(0)

            def ev_out(j):
                if 1 <= j <= 9:
                    tile_out(EV_AT, 3 + j)

            s5(ev_out)
            gla_decay()
            glu()
            gla()
            glu_split()
            norm_after_out(2, 0)
            cross(0)
            norm_after_out(3, 1)
            ffn(1, tables)
            norm_after_ffn(4, 1)
            ffn(2, lambda: memory_split(1))
            norm_after_ffn(5, 2)
            for t in range(OD_TILES):
                tile_out(OD_AT, t)
                if t >= 7:
                    for r in ([2 * (t - 7), 2 * (t - 7) + 1] if t < 13 else [t - 1]):
                        rope(r)
            rstd_columns(1)
            dve.wait_ge(S("block_done"), OD_V_AT + 2)
            for tt in range(4):
                dve.tensor_scalar(od_val[:, tt, :], ps[:, BANKS[tt], 0:2 * P], col[:, 16 + tt:17 + tt], None,
                                  ALU.mult).then_inc(S("od_v"), 1)
            indexer_weights()
            indexer()
            attention()
            norm_after_out(6, 2)
            cross(1)
            norm_after_out(7, 3)
            ffn(3)
            norm_after_ffn(8, 3)
            for k in range(KC):
                dve.scalar_tensor_tensor(h[:, k, :], h[:, k, :], gain(8, k), rstd[:], ALU.mult, ALU.mult
                                         ).then_inc(S("y_ready"), 1)


def wide(w):
    k, n = w.shape
    return w.reshape(k // P, P, n // P, P).transpose(2, 1, 0, 3)


def rows_of(w, per):
    k, n = w.shape
    return w.reshape(k // P // per, per, P, n).transpose(0, 2, 1, 3)


def lay_out(inp):
    f = np.float32
    a = {k: np.asarray(v) for k, v in inp.items()}

    def chunks(m):
        return np.ascontiguousarray(m.T.reshape(KC, P, -1).transpose(1, 0, 2))

    def cols(v):
        return v.reshape(-1, P).T

    def pad(w):
        return np.concatenate([w, np.zeros((w.shape[0], P - w.shape[1]), f)], axis=1)

    blocks = []

    def add(b):
        blocks.append(b.reshape(b.shape[0], P, BLK))

    def ffn(name, l):
        gate, up = wide(a[f"{name}_w_gate"][l]), wide(a[f"{name}_w_up"][l])
        add(np.stack([gate, up], axis=1).reshape(2 * FC, P, KC, P))
        down = rows_of(a[f"{name}_w_down"][l], 1).reshape(FC, P, 8, P)
        down[0] = down[0][:, DOWN_FIRST]
        add(down)

    def memory(l, glu=None):
        wk = wide(a["xa_wk"][l])
        if glu is not None:
            add(wk[:EARLY_KEYS])
            add(glu)
            wk = wk[EARLY_KEYS:]
        add(wk)
        wv = a["xa_wv"][l]
        for quarter in range(4):
            add(rows_of(wv[:, quarter * MEM:(quarter + 1) * MEM], 4))

    ev, od = a["ev_w_in"][0], a["od_w_in"][0]
    q, k, v, r, al, u = np.split(ev, np.cumsum([256, 256, 512, 512, 16]), axis=1)
    ffn("ffn1", 0)
    add(wide(np.concatenate([u, pad(al), q, k, r], axis=1)))
    add(rows_of(v, 2))
    memory(0, wide(a["s5_w_glu"][0]).reshape(2, 2, P, 4, P).transpose(0, 2, 1, 3, 4))
    add(wide(a["ev_w_out"][0]))
    add(wide(a["xa_wq"][0]))
    add(wide(a["xa_wo"][0]))
    ffn("ffn2", 0)
    ffn("ffn1", 1)
    q, k, v, qi, ki, wi = np.split(od, np.cumsum([1024, 256, 256, 512, 64]), axis=1)
    add(wide(np.concatenate([q, k, qi, ki, ki, pad(wi)], axis=1)))
    add(rows_of(v, 4))
    memory(1)
    add(wide(a["od_w_out"][0]))
    add(wide(a["xa_wq"][1]))
    add(wide(a["xa_wo"][1]))
    ffn("ffn2", 1)
    stream = np.concatenate(blocks, axis=0)
    assert stream.shape == (N_BLOCKS, P, BLK)

    norms = [a["ffn1_norm"][0], a["mix_norm"][0], a["xa_norm"][0], a["ffn2_norm"][0],
             a["ffn1_norm"][1], a["mix_norm"][1], a["xa_norm"][1], a["ffn2_norm"][1], a["final_norm"]]
    lane = np.arange(P)
    inv_a = (np.float32(10000.0) ** (-(2 * (lane % 64)).astype(f) / np.float32(128)))[:, None].astype(f)
    inv_i = (np.float32(10000.0) ** (-(2 * (lane % 32)).astype(f) / np.float32(64)))[:, None].astype(f)
    vecs = np.concatenate(
        [cols(n) for n in norms] + [cols(a["mem_norm"]), cols(a["gla_norm"][0]), cols(a["gla_b_alpha"][0]),
         cols(a["s5_D"][0].reshape(-1)), cols(a["s5_b_glu"][0]),
         cols(a["s5_lambda_re"][0].reshape(-1)), cols(a["s5_lambda_im"][0].reshape(-1)),
         cols(np.repeat(a["s5_log_dt"][0], 64)), inv_a, inv_i], axis=1)

    s5b = np.zeros((P, 2, 4, P), f)
    s5c = np.zeros((P, 2, S5_TILES, 32), f)
    for g in range(32):
        j, e = g // 2, g % 2
        p0 = 32 * (j % 4) + 16 * e
        for c, (b, cc) in enumerate((("s5_B_re", "s5_C_re"), ("s5_B_im", "s5_C_im"))):
            s5b[p0:p0 + 16, c, j // 4, 64 * e:64 * e + 64] = a[b][0, g].T
            s5c[64 * e:64 * e + 64, c, j, 16 * e:16 * e + 16] = a[cc][0, g].T

    mats = np.zeros((P, 4, P), f)
    mats[:, 0] = np.eye(P)
    for i, half in ((1, 64), (2, 32)):
        for m in range(P):
            low = m % (2 * half) < half
            mats[m + half if low else m - half, i, m] = -1.0 if low else 1.0
    mats[:, 3] = np.where(lane[None, :] <= lane[:, None], 0.0, MASKED)
    mask = ((lane[:, None] // 64 == lane[None, :] // 64) & (lane[:, None] <= lane[None, :])).astype(np.int32)
    rows = np.stack([np.arange(T), np.arange(T) % GLA_CHUNK != 0]).astype(f)
    return {
        "xT": chunks(a["x"][0]), "memT": chunks(a["mem"][0]), "pos": a["positions"],
        "vecs": vecs, "w_alpha": a["gla_w_alpha"][0], "s5b": s5b, "s5c": s5c, "mats": mats,
        "mask": mask, "rows": rows, "stream": stream,
    }


def kernel(**inputs):
    import concourse.bacc as bacc
    from concourse.bass_utils import run_bass_kernel_spmd as run

    nc = bacc.Bacc("TRN2", target_bir_lowering=False, num_devices=1)
    arrays, args = {}, []
    for name, a in lay_out(inputs).items():
        a = np.ascontiguousarray(a)
        arrays[f"in_{name}"] = a
        args.append(nc.dram_tensor(f"in_{name}", a.shape, mybir.dt.from_np(a.dtype), kind="ExternalInput").ap())
    args.append(nc.dram_tensor("out_0", (P, KC, T), F32, kind="ExternalOutput").ap())
    build_trunk(nc, *args)
    r = run(nc, [arrays], core_ids=[0])
    got = r.results[0]["out_0"]
    return np.ascontiguousarray(got.transpose(2, 1, 0).reshape(1, T, D))
```
